# Optimizing a Trainium2 kernel written in Bass

```python
import jax
import jax.numpy as jnp
from jax import lax
import numpy as np
import math
import jax, jax.numpy as jnp

D_MODEL = 1024
BATCH = 1
SEQ = 512
DEPTH = 2

N_MIXERS = 2
GRID_W = 64
N_MEM = 256
MEM_HEADS = 4
MEM_DH = 64
MEM_W = MEM_HEADS * MEM_DH
NA_HEADS = 12
NA_DH = 64
NA_W = NA_HEADS * NA_DH
WIN_H_MAX = 8
WIN_W = 16
ML_HEADS = 4
ML_DH = 192
ML_W = ML_HEADS * ML_DH
CONV_K = 5
CHUNK = 128
MIX_W = NA_W + MEM_W
N_EXPERTS = 16
N_GROUPS = 4
EXPERTS_PER_GROUP = N_EXPERTS // N_GROUPS
TOP_K = 2
D_EXPERT = 512
MOE_BLOCK = 128
ALPHA = (2 * DEPTH) ** 0.25
BETA = (8 * DEPTH) ** -0.25
LN_EPS = 1e-5


def layer_norm(x, g, b):
    xf = x.astype(jnp.float32)
    mu = jnp.mean(xf, axis=-1, keepdims=True)
    var = jnp.mean(jnp.square(xf - mu), axis=-1, keepdims=True)
    return ((xf - mu) * lax.rsqrt(var + LN_EPS) * g + b).astype(x.dtype)

def memory_attention(q, mem_k, mem_v):
    B, S, _ = q.shape
    q = q.reshape(B, S, MEM_HEADS, MEM_DH) * (MEM_DH ** -0.5)
    s = jnp.einsum('bshd,bmhd->bhsm', q, mem_k, preferred_element_type=jnp.float32)
    p = jax.nn.softmax(s, axis=-1).astype(mem_v.dtype)
    return jnp.einsum('bhsm,bmhd->bshd', p, mem_v).reshape(B, S, MEM_W)

def neighbourhood_attention(q, k, v, rpb):
    B, R, W, H, Dh = q.shape
    win_h = min(WIN_H_MAX, R)
    n_cb = W // WIN_W
    span = 2 * WIN_W
    q_cols = np.arange(W).reshape(n_cb, WIN_W)
    cb_start = np.clip(np.arange(n_cb) * WIN_W - WIN_W // 2, 0, W - span)
    key_cols = cb_start[:, None] + np.arange(span)[None, :]
    col_start = np.clip(q_cols - WIN_W // 2, 0, W - WIN_W)
    kc = key_cols[:, None, :]
    col_in = (kc >= col_start[..., None]) & (kc < col_start[..., None] + WIN_W)
    dc_idx = np.clip(kc - q_cols[..., None] + WIN_W - 1, 0, 2 * WIN_W - 2)
    rpb_c = jnp.transpose(rpb[:, :, dc_idx], (0, 2, 3, 1, 4))

    def row_block(r):
        rs = jnp.clip(r - win_h // 2, 0, R - win_h)
        k_rows = lax.dynamic_slice_in_dim(k, rs, win_h, axis=1)
        v_rows = lax.dynamic_slice_in_dim(v, rs, win_h, axis=1)
        k_blk = k_rows[:, :, key_cols]
        v_blk = v_rows[:, :, key_cols]
        q_blk = lax.dynamic_index_in_dim(q, r, axis=1, keepdims=False).reshape(B, n_cb, WIN_W, H, Dh)
        s = jnp.einsum('bjqhd,brjkhd->bhjqrk', q_blk, k_blk, preferred_element_type=jnp.float32)
        dr = rs + jnp.arange(win_h) - r + WIN_H_MAX - 1
        s = s + jnp.take(rpb_c, dr, axis=3)[None].astype(jnp.float32)
        s = jnp.where(col_in[:, :, None, :], s, -jnp.inf)
        p = jax.nn.softmax(s.reshape(B, H, n_cb, WIN_W, win_h * span), axis=-1)
        p = p.reshape(s.shape).astype(v.dtype)
        o = jnp.einsum('bhjqrk,brjkhd->bjqhd', p, v_blk)
        return o.reshape(B, W, H, Dh)

    out = lax.map(row_block, jnp.arange(R))
    return jnp.moveaxis(out, 0, 1)

def na_mixer(x, w_in, rpb, mem_k, mem_v):
    B, S, _ = x.shape
    rows = S // GRID_W
    h = x @ w_in
    q, k, v, q_mem = jnp.split(h, [NA_W, 2 * NA_W, 3 * NA_W], axis=-1)
    grid = (B, rows, GRID_W, NA_HEADS, NA_DH)
    y = neighbourhood_attention(q.reshape(grid) * (NA_DH ** -0.5), k.reshape(grid), v.reshape(grid), rpb)
    return jnp.concatenate([y.reshape(B, S, NA_W), memory_attention(q_mem, mem_k, mem_v)], axis=-1)

def mlstm_chunkwise(q, k, v, i_pre, f_pre):
    q, k, v = q.astype(jnp.float32), k.astype(jnp.float32), v.astype(jnp.float32)
    B, H, S, Dk = q.shape
    Dv = v.shape[-1]
    nc = S // CHUNK
    log_f = jax.nn.log_sigmoid(f_pre.astype(jnp.float32))
    i_pre = i_pre.astype(jnp.float32)

    def to_chunks(a):
        return jnp.moveaxis(a.reshape(a.shape[:2] + (nc, CHUNK) + a.shape[3:]), 2, 0)

    causal = np.tril(np.ones((CHUNK, CHUNK), dtype=bool))

    def step(carry, inp):
        C, n, m = carry
        qb, kb, vb, ib, fb = inp
        b = jnp.cumsum(fb, axis=-1)
        d = jnp.where(causal, b[..., :, None] - b[..., None, :] + ib[..., None, :], -jnp.inf)
        inter = b + m[..., None]
        m_t = jnp.maximum(jnp.max(d, axis=-1), inter)
        dexp = jnp.exp(d - m_t[..., None])
        iexp = jnp.exp(inter - m_t)
        s = jnp.einsum('bhtd,bhsd->bhts', qb, kb) * dexp
        num = jnp.einsum('bhts,bhse->bhte', s, vb) + iexp[..., None] * jnp.einsum('bhtd,bhde->bhte', qb, C)
        den = jnp.sum(s, axis=-1) + iexp * jnp.einsum('bhtd,bhd->bht', qb, n)
        h = num / jnp.maximum(jnp.abs(den), jnp.exp(-m_t))[..., None]
        b_last = b[..., -1]
        w_s = b_last[..., None] - b + ib
        m_new = jnp.maximum(b_last + m, jnp.max(w_s, axis=-1))
        wexp = jnp.exp(w_s - m_new[..., None])
        cexp = jnp.exp(b_last + m - m_new)
        C_new = cexp[..., None, None] * C + jnp.einsum('bhs,bhsd,bhse->bhde', wexp, kb, vb)
        n_new = cexp[..., None] * n + jnp.einsum('bhs,bhsd->bhd', wexp, kb)
        return (C_new, n_new, m_new), h

    init = (jnp.zeros((B, H, Dk, Dv), jnp.float32), jnp.zeros((B, H, Dk), jnp.float32),
            jnp.zeros((B, H), jnp.float32))
    _, hs = lax.scan(step, init, (to_chunks(q), to_chunks(k), to_chunks(v), to_chunks(i_pre), to_chunks(log_f)))
    return jnp.moveaxis(hs, 0, 2).reshape(B, H, S, Dv)

def mlstm_mixer(x, w_in, conv_w, conv_b, w_qkv, gate_b, norm_g, skip, mem_k, mem_v):
    B, S, _ = x.shape
    h = x @ w_in
    xm, z, gates, q_mem = jnp.split(h, [ML_W, 2 * ML_W, 2 * ML_W + 4 * ML_HEADS], axis=-1)
    xc = lax.conv_general_dilated(xm, conv_w[:, None, :], window_strides=(1,), padding='SAME',
                                  dimension_numbers=('NWC', 'WIO', 'NWC'), feature_group_count=ML_W)
    xc = jax.nn.silu(xc + conv_b)
    xc_h = xc.reshape(B, S, ML_HEADS, ML_DH)
    xm_h = xm.reshape(B, S, ML_HEADS, ML_DH)
    q = jnp.einsum('bshd,hde->bhse', xc_h, w_qkv[0])
    k = jnp.einsum('bshd,hde->bhse', xc_h, w_qkv[1]) * (ML_DH ** -0.5)
    v = jnp.einsum('bshd,hde->bhse', xm_h, w_qkv[2])
    g = (gates.reshape(B, S, 4, ML_HEADS) + gate_b).astype(jnp.float32)
    g = jnp.transpose(g, (2, 0, 3, 1))
    h_f = mlstm_chunkwise(q, k, v, g[0], g[1])
    h_b = jnp.flip(mlstm_chunkwise(jnp.flip(q, 2), jnp.flip(k, 2), jnp.flip(v, 2),
                                   jnp.flip(g[2], -1), jnp.flip(g[3], -1)), 2)
    hs = h_f + h_b
    mu = jnp.mean(hs, axis=-1, keepdims=True)
    var = jnp.mean(jnp.square(hs - mu), axis=-1, keepdims=True)
    hs = (hs - mu) * lax.rsqrt(var + LN_EPS)
    hs = jnp.transpose(hs, (0, 2, 1, 3)).reshape(B, S, ML_W) * norm_g
    y = ((hs + skip * xc) * jax.nn.silu(z)).astype(x.dtype)
    return jnp.concatenate([y, memory_attention(q_mem, mem_k, mem_v)], axis=-1)

def moe(x, router_w, router_b, w_gate, w_up, w_down):
    B, S, D = x.shape
    N = B * S
    xf = x.reshape(N, D)
    scores = jax.nn.sigmoid(jnp.matmul(xf, router_w, preferred_element_type=jnp.float32))
    biased = scores + router_b.astype(jnp.float32)
    grp_score = jnp.sum(lax.top_k(biased.reshape(N, N_GROUPS, EXPERTS_PER_GROUP), 2)[0], axis=-1)
    g_sel = jnp.argmax(grp_score, axis=-1)
    in_group = (jnp.arange(N_EXPERTS) // EXPERTS_PER_GROUP)[None, :] == g_sel[:, None]
    _, idx = lax.top_k(jnp.where(in_group, biased, -jnp.inf), TOP_K)
    w = jnp.take_along_axis(scores, idx, axis=1)
    w = w / jnp.sum(w, axis=-1, keepdims=True)
    NK = N * TOP_K
    flat_e = idx.reshape(NK)
    order = jnp.argsort(flat_e)
    e_sorted = flat_e[order]
    tok_sorted = order // TOP_K
    counts = jnp.bincount(flat_e, length=N_EXPERTS)
    padded = (counts + MOE_BLOCK - 1) // MOE_BLOCK * MOE_BLOCK
    pad_end = jnp.cumsum(padded)
    pad_start = pad_end - padded
    start = jnp.cumsum(counts) - counts
    dest = pad_start[e_sorted] + jnp.arange(NK) - start[e_sorted]
    n_blocks = -(-NK // MOE_BLOCK) + N_EXPERTS
    buf = jnp.zeros((n_blocks * MOE_BLOCK, D), x.dtype).at[dest].set(xf[tok_sorted])
    block_e = jnp.minimum(jnp.searchsorted(pad_end, jnp.arange(n_blocks) * MOE_BLOCK, side='right'),
                          N_EXPERTS - 1)

    def expert_block(args):
        xb, e = args
        hb = jax.nn.silu(xb @ w_gate[e]) * (xb @ w_up[e])
        return hb @ w_down[e]

    y = lax.map(expert_block, (buf.reshape(n_blocks, MOE_BLOCK, D), block_e)).reshape(n_blocks * MOE_BLOCK, D)
    w_sorted = w.reshape(NK)[order].astype(x.dtype)
    out = jnp.zeros((N, D), x.dtype).at[tok_sorted].add(y[dest] * w_sorted[:, None])
    return out.reshape(B, S, D)

def first_inputs(seed: int = 0) -> dict:
    key = jax.random.key(seed)
    ks = jax.random.split(key, 26)
    n_a = (DEPTH + 1) // 2
    n_b = DEPTH // 2

    def nrm(k, shape, scale):
        return jax.random.normal(k, shape, jnp.float32) * scale

    x = nrm(ks[0], (BATCH, SEQ, D_MODEL), 1.0)
    mem = nrm(ks[1], (BATCH, N_MEM, D_MODEL), 1.0)
    mem_ln_g = 1.0 + nrm(ks[2], (D_MODEL,), 0.05)
    mem_ln_b = nrm(ks[3], (D_MODEL,), 0.02)
    w_mem_kv = nrm(ks[4], (D_MODEL, 2 * MEM_W), D_MODEL ** -0.5).at[:, MEM_W:].multiply(BETA)
    router_w = nrm(ks[5], (D_MODEL, N_EXPERTS), D_MODEL ** -0.5)
    router_b = nrm(ks[6], (N_EXPERTS,), 0.01)
    na_w_in = nrm(ks[7], (n_a, D_MODEL, 3 * NA_W + MEM_W), D_MODEL ** -0.5)
    na_w_in = na_w_in.at[:, :, 2 * NA_W:3 * NA_W].multiply(BETA)
    na_rpb = nrm(ks[8], (n_a, NA_HEADS, 2 * WIN_H_MAX - 1, 2 * WIN_W - 1), 0.1)
    ml_w_in = nrm(ks[9], (n_b, D_MODEL, 2 * ML_W + 4 * ML_HEADS + MEM_W), D_MODEL ** -0.5)
    ml_conv_w = nrm(ks[10], (n_b, CONV_K, ML_W), CONV_K ** -0.5)
    ml_conv_b = nrm(ks[11], (n_b, ML_W), 0.02)
    ml_w_qkv = nrm(ks[12], (n_b, 3, ML_HEADS, ML_DH, ML_DH), ML_DH ** -0.5).at[:, 2].multiply(BETA)
    i_bias = nrm(ks[13], (n_b, 2, ML_HEADS), 0.1)
    f_bias = jnp.linspace(3.0, 6.0, ML_HEADS)[None, None, :] + nrm(ks[14], (n_b, 2, ML_HEADS), 0.1)
    ml_gate_b = jnp.stack([i_bias[:, 0], f_bias[:, 0], i_bias[:, 1], f_bias[:, 1]], axis=1)
    ml_norm_g = 1.0 + nrm(ks[15], (n_b, ML_W), 0.05)
    ml_skip = 1.0 + nrm(ks[16], (n_b, ML_W), 0.05)
    w_out = nrm(ks[17], (DEPTH, MIX_W, D_MODEL), MIX_W ** -0.5 * BETA)
    ln_g = 1.0 + nrm(ks[18], (DEPTH, 2, D_MODEL), 0.05)
    ln_b = nrm(ks[19], (DEPTH, 2, D_MODEL), 0.02)
    exp_w_gate = nrm(ks[20], (DEPTH, N_EXPERTS, D_MODEL, D_EXPERT), D_MODEL ** -0.5)
    exp_w_up = nrm(ks[21], (DEPTH, N_EXPERTS, D_MODEL, D_EXPERT), D_MODEL ** -0.5)
    exp_w_down = nrm(ks[22], (DEPTH, N_EXPERTS, D_EXPERT, D_MODEL), D_EXPERT ** -0.5 * BETA)
    return {'x': x, 'mem': mem, 'mem_ln_g': mem_ln_g, 'mem_ln_b': mem_ln_b, 'w_mem_kv': w_mem_kv,
            'router_w': router_w, 'router_b': router_b, 'na_w_in': na_w_in, 'na_rpb': na_rpb,
            'ml_w_in': ml_w_in, 'ml_conv_w': ml_conv_w, 'ml_conv_b': ml_conv_b, 'ml_w_qkv': ml_w_qkv,
            'ml_gate_b': ml_gate_b, 'ml_norm_g': ml_norm_g, 'ml_skip': ml_skip, 'w_out': w_out,
            'ln_g': ln_g, 'ln_b': ln_b, 'exp_w_gate': exp_w_gate, 'exp_w_up': exp_w_up,
            'exp_w_down': exp_w_down}

def first_block(x, mem, mem_ln_g, mem_ln_b, w_mem_kv, router_w, router_b, na_w_in, na_rpb,
              ml_w_in, ml_conv_w, ml_conv_b, ml_w_qkv, ml_gate_b, ml_norm_g, ml_skip, w_out,
              ln_g, ln_b, exp_w_gate, exp_w_up, exp_w_down):
    B, M, _ = mem.shape
    mem_k, mem_v = jnp.split(layer_norm(mem, mem_ln_g, mem_ln_b) @ w_mem_kv, 2, axis=-1)
    mem_k = mem_k.reshape(B, M, MEM_HEADS, MEM_DH)
    mem_v = mem_v.reshape(B, M, MEM_HEADS, MEM_DH)
    for i in range(DEPTH):
        j = i // N_MIXERS
        if i % N_MIXERS == 0:
            mixed = na_mixer(x, na_w_in[j], na_rpb[j], mem_k, mem_v)
        else:
            mixed = mlstm_mixer(x, ml_w_in[j], ml_conv_w[j], ml_conv_b[j], ml_w_qkv[j], ml_gate_b[j],
                                ml_norm_g[j], ml_skip[j], mem_k, mem_v)
        x = layer_norm(ALPHA * x + mixed @ w_out[i], ln_g[i, 0], ln_b[i, 0])
        x = layer_norm(ALPHA * x + moe(x, router_w, router_b, exp_w_gate[i], exp_w_up[i], exp_w_down[i]),
                       ln_g[i, 1], ln_b[i, 1])
    return x


DEPTH_2 = 1

MLA_HEADS = 8
MLA_Q_RANK = 384
MLA_KV_RANK = 256
MLA_NOPE_DIM = 128
MLA_ROPE_DIM = 64
MLA_V_DIM = D_MODEL // MLA_HEADS
ROPE_THETA = 10000.0
Q_BLOCK = 128
DIL_GROUPS = ((128, 1), (512, 4), (2048, 16))
DIL_HEADS = 8
DIL_HEAD_DIM = D_MODEL // DIL_HEADS
N_DIL_HEADS = len(DIL_GROUPS) * DIL_HEADS
REL_BUCKETS = 32
REL_MAX_DIST = 1024
EC_CAPACITY_FACTOR = 2
D_FF_EXPERT = 2 * D_MODEL
N_BRANCHES = 2
NORM_EPS = 1e-6
NEG_INF = -1e30
COLS_DIL = len(DIL_GROUPS) * 3 * DIL_HEADS * DIL_HEAD_DIM
SPLIT_SIZES = (MLA_Q_RANK, MLA_KV_RANK, MLA_ROPE_DIM, COLS_DIL, N_BRANCHES * D_MODEL)
D_IN = sum(SPLIT_SIZES)


def rmsnorm(t, g):
    tf = t.astype(jnp.float32)
    y = tf * lax.rsqrt(jnp.mean(tf * tf, axis=-1, keepdims=True) + NORM_EPS)
    return (y * g.astype(jnp.float32)).astype(t.dtype)

def rope(t, cos, sin):
    t1, t2 = jnp.split(t, 2, axis=-1)
    return jnp.concatenate([t1 * cos - t2 * sin, t1 * sin + t2 * cos], axis=-1).astype(t.dtype)

def t5_bucket(rel):
    nb = REL_BUCKETS // 2
    ret = jnp.where(rel > 0, nb, 0)
    n = jnp.abs(rel)
    max_exact = nb // 2
    nf = jnp.maximum(n, 1).astype(jnp.float32)
    large = max_exact + (jnp.log(nf / max_exact) / math.log(REL_MAX_DIST / max_exact)
                         * (nb - max_exact)).astype(jnp.int32)
    large = jnp.minimum(large, nb - 1)
    return ret + jnp.where(n < max_exact, n, large)

def mla_attention(c_q, c_kv, k_pe, g_q_lat, g_kv_lat, w_uq, w_ukv, cos, sin):
    B, S, _ = c_q.shape
    q = (rmsnorm(c_q, g_q_lat) @ w_uq).reshape(B, S, MLA_HEADS, MLA_NOPE_DIM + MLA_ROPE_DIM)
    q_nope = q[..., :MLA_NOPE_DIM]
    q_pe = rope(q[..., MLA_NOPE_DIM:], cos[:, :, None], sin[:, :, None])
    kv = (rmsnorm(c_kv, g_kv_lat) @ w_ukv).reshape(B, S, MLA_HEADS, MLA_NOPE_DIM + MLA_V_DIM)
    k_nope, v = kv[..., :MLA_NOPE_DIM], kv[..., MLA_NOPE_DIM:]
    k_pe = rope(k_pe, cos, sin)
    scale = (MLA_NOPE_DIM + MLA_ROPE_DIM) ** -0.5
    nqb = S // Q_BLOCK

    def to_blocks(t):
        return jnp.moveaxis(t.reshape((B, nqb, Q_BLOCK) + t.shape[2:]), 1, 0)

    def attend(blk):
        qn, qp = blk
        s = (jnp.einsum('bqhc,bkhc->bhqk', qn, k_nope)
             + jnp.einsum('bqhr,bkr->bhqk', qp, k_pe))
        p = jax.nn.softmax(s.astype(jnp.float32) * scale, axis=-1).astype(v.dtype)
        return jnp.einsum('bhqk,bkhc->bqhc', p, v)

    o = lax.map(attend, (to_blocks(q_nope), to_blocks(q_pe)))
    return jnp.moveaxis(o, 0, 1).reshape(B, S, MLA_HEADS * MLA_V_DIM)

def dilated_band_attention(q, k, v, pos, bias_table, window, dilation):
    B, S, H, Dh = q.shape
    d = dilation
    r = window // (2 * d)
    L = S // d
    nb = -(-L // r)
    Lp = nb * r

    def to_classes(t):
        t = jnp.moveaxis(t.reshape((B, L, d) + t.shape[2:]), 2, 1)
        return jnp.pad(t, [(0, 0), (0, 0), (0, Lp - L)] + [(0, 0)] * (t.ndim - 3))

    def band(t):
        t = jnp.pad(t, [(0, 0), (0, 0), (r, r)] + [(0, 0)] * (t.ndim - 3))
        t = t.reshape((B, d, nb + 2, r) + t.shape[3:])
        return jnp.concatenate([t[:, :, :-2], t[:, :, 1:-1], t[:, :, 2:]], axis=3)

    qc, kc, vc, pc = to_classes(q), to_classes(k), to_classes(v), to_classes(pos)
    kb, vb, pkb = band(kc), band(vc), band(pc)
    qb = qc.reshape(B, d, nb, r, H, Dh)
    pqb = pc.reshape(B, d, nb, r)
    s = jnp.einsum('bgnqhc,bgnkhc->bgnhqk', qb, kb).astype(jnp.float32) * (Dh ** -0.5)
    rel = pkb[:, :, :, None, :] - pqb[..., None]
    bias = bias_table[t5_bucket(rel)]
    s = s + jnp.moveaxis(bias, -1, 3).astype(jnp.float32)
    qi = jnp.arange(nb)[:, None, None] * r + jnp.arange(r)[None, :, None]
    kj = (jnp.arange(nb)[:, None, None] - 1) * r + jnp.arange(3 * r)[None, None, :]
    valid = (jnp.abs(kj - qi) <= r) & (kj >= 0) & (kj < L)
    s = jnp.where(valid[:, None], s, NEG_INF)
    m = jnp.max(s, axis=-1, keepdims=True)
    p = jnp.exp(s - m)
    den = jnp.sum(p, axis=-1, keepdims=True)
    o = jnp.einsum('bgnhqk,bgnkhc->bgnqhc', (p / den).astype(v.dtype), vb)
    lse = (m + jnp.log(den))[..., 0]
    o = o.reshape(B, d, Lp, H, Dh)[:, :, :L]
    o = jnp.moveaxis(o, 1, 2).reshape(B, S, H, Dh)
    lse = jnp.moveaxis(lse, 3, 4).reshape(B, d, Lp, H)[:, :, :L]
    lse = jnp.moveaxis(lse, 1, 2).reshape(B, S, H)
    return o, lse

def expert_choice_ffn(h, w_router, w_gate, w_up, w_down):
    B, S, D = h.shape
    cap = EC_CAPACITY_FACTOR * S // N_EXPERTS
    aff = jax.nn.softmax((h @ w_router).astype(jnp.float32), axis=-1)
    gate, idx = lax.top_k(jnp.swapaxes(aff, 1, 2), cap)
    bidx = jnp.arange(B)[:, None, None]
    xe = h[bidx, idx]
    hid = (jax.nn.silu(jnp.einsum('becd,edf->becf', xe, w_gate))
           * jnp.einsum('becd,edf->becf', xe, w_up))
    ye = jnp.einsum('becf,efd->becd', hid, w_down) * gate[..., None].astype(h.dtype)
    return jnp.zeros_like(h).at[bidx, idx].add(ye)

def second_inputs(seed: int = 0) -> dict:
    key = jax.random.key(seed)
    ks = jax.random.split(key, 20)
    f32 = jnp.float32

    def nrm(k, shape, s):
        return jax.random.normal(k, shape, f32) * s

    def gain(k, shape):
        return 1.0 + 0.02 * jax.random.normal(k, shape, f32)

    x = nrm(ks[0], (BATCH, SEQ, D_MODEL), 1.0)
    c = nrm(ks[1], (BATCH, D_MODEL), 1.0)
    offs = jax.random.randint(ks[2], (BATCH, 1), 0, 4096, dtype=jnp.int32)
    positions = offs + jnp.arange(SEQ, dtype=jnp.int32)[None, :]
    w_ada = nrm(ks[3], (DEPTH_2, D_MODEL, 6 * D_MODEL), 0.02)
    b_ada = nrm(ks[4], (DEPTH_2, 6 * D_MODEL), 0.02)
    g_norm_mix = gain(ks[5], (DEPTH_2, D_MODEL))
    w_in = nrm(ks[6], (DEPTH_2, D_MODEL, D_IN), D_MODEL ** -0.5)
    g_q_lat = gain(ks[7], (DEPTH_2, MLA_Q_RANK))
    g_kv_lat = gain(ks[8], (DEPTH_2, MLA_KV_RANK))
    w_uq = nrm(ks[9], (DEPTH_2, MLA_Q_RANK, MLA_HEADS * (MLA_NOPE_DIM + MLA_ROPE_DIM)), MLA_Q_RANK ** -0.5)
    w_ukv = nrm(ks[10], (DEPTH_2, MLA_KV_RANK, MLA_HEADS * (MLA_NOPE_DIM + MLA_V_DIM)), MLA_KV_RANK ** -0.5)
    rel_bias = nrm(ks[11], (REL_BUCKETS, N_DIL_HEADS), 0.5)
    w_out = nrm(ks[12], (DEPTH_2, D_MODEL, D_MODEL), D_MODEL ** -0.5)
    g_norm_ffn = gain(ks[13], (DEPTH_2, D_MODEL))
    w_router = nrm(ks[14], (DEPTH_2, D_MODEL, N_EXPERTS), D_MODEL ** -0.5)
    w_gate = nrm(ks[15], (DEPTH_2, N_EXPERTS, D_MODEL, D_FF_EXPERT), D_MODEL ** -0.5)
    w_up = nrm(ks[16], (DEPTH_2, N_EXPERTS, D_MODEL, D_FF_EXPERT), D_MODEL ** -0.5)
    w_down = nrm(ks[17], (DEPTH_2, N_EXPERTS, D_FF_EXPERT, D_MODEL), D_FF_EXPERT ** -0.5)
    g_final = gain(ks[18], (D_MODEL,))
    return {'x': x, 'c': c, 'positions': positions, 'w_ada': w_ada, 'b_ada': b_ada,
            'g_norm_mix': g_norm_mix, 'w_in': w_in, 'g_q_lat': g_q_lat, 'g_kv_lat': g_kv_lat,
            'w_uq': w_uq, 'w_ukv': w_ukv, 'rel_bias': rel_bias, 'w_out': w_out,
            'g_norm_ffn': g_norm_ffn, 'w_router': w_router, 'w_gate': w_gate, 'w_up': w_up,
            'w_down': w_down, 'g_final': g_final}

def second_block(x, c, positions, w_ada, b_ada, g_norm_mix, w_in, g_q_lat, g_kv_lat, w_uq, w_ukv,
              rel_bias, w_out, g_norm_ffn, w_router, w_gate, w_up, w_down, g_final):
    B, S, D = x.shape
    inv_freq = ROPE_THETA ** (-jnp.arange(0, MLA_ROPE_DIM, 2, dtype=jnp.float32) / MLA_ROPE_DIM)
    ang = positions.astype(jnp.float32)[..., None] * inv_freq
    cos, sin = jnp.cos(ang), jnp.sin(ang)
    cond = jax.nn.silu(c)
    split_at = [int(v) for v in np.cumsum(SPLIT_SIZES)[:-1]]
    for l in range(DEPTH_2):
        mod = (cond @ w_ada[l] + b_ada[l])[:, None, :]
        sh1, sc1, gt1, sh2, sc2, gt2 = jnp.split(mod, 6, axis=-1)
        h = rmsnorm(x, g_norm_mix[l]) * (1.0 + sc1) + sh1
        c_q, c_kv, k_pe, dil, gates = jnp.split(h @ w_in[l], split_at, axis=-1)
        o_a = mla_attention(c_q, c_kv, k_pe, g_q_lat[l], g_kv_lat[l], w_uq[l], w_ukv[l], cos, sin)
        dil = dil.reshape(B, S, len(DIL_GROUPS), 3, DIL_HEADS, DIL_HEAD_DIM)
        outs, lses = [], []
        for gi, (win, dd) in enumerate(DIL_GROUPS):
            o_g, lse_g = dilated_band_attention(
                dil[:, :, gi, 0], dil[:, :, gi, 1], dil[:, :, gi, 2], positions,
                rel_bias[:, gi * DIL_HEADS:(gi + 1) * DIL_HEADS], win, dd)
            outs.append(o_g)
            lses.append(lse_g)
        wts = jax.nn.softmax(jnp.stack(lses), axis=0)
        o_b = jnp.einsum('gbsh,gbshc->bshc', wts.astype(x.dtype), jnp.stack(outs)).reshape(B, S, D)
        g_a, g_b = jnp.split(jax.nn.sigmoid(gates), 2, axis=-1)
        x = x + gt1 * ((g_a * o_a + g_b * o_b) @ w_out[l])
        h2 = rmsnorm(x, g_norm_ffn[l]) * (1.0 + sc2) + sh2
        x = x + gt2 * expert_choice_ffn(h2, w_router[l], w_gate[l], w_up[l], w_down[l])
    return rmsnorm(x, g_final)


def setup_inputs(seed=0):
    out = dict(first_inputs(seed))
    for name, value in second_inputs(seed + 1).items():
        if name != "x":
            out[name + "_2"] = value
    return out


def reference(
    x, mem, mem_ln_g, mem_ln_b, w_mem_kv, router_w, router_b, na_w_in, na_rpb, ml_w_in,
    ml_conv_w, ml_conv_b, ml_w_qkv, ml_gate_b, ml_norm_g, ml_skip, w_out, ln_g, ln_b,
    exp_w_gate, exp_w_up, exp_w_down, c_2, positions_2, w_ada_2, b_ada_2, g_norm_mix_2, w_in_2,
    g_q_lat_2, g_kv_lat_2, w_uq_2, w_ukv_2, rel_bias_2, w_out_2, g_norm_ffn_2, w_router_2,
    w_gate_2, w_up_2, w_down_2, g_final_2,
):
    x = first_block(
        x, mem, mem_ln_g, mem_ln_b, w_mem_kv, router_w, router_b, na_w_in, na_rpb, ml_w_in,
        ml_conv_w, ml_conv_b, ml_w_qkv, ml_gate_b, ml_norm_g, ml_skip, w_out, ln_g, ln_b,
        exp_w_gate, exp_w_up, exp_w_down,
    )
    return second_block(
        x, c_2, positions_2, w_ada_2, b_ada_2, g_norm_mix_2, w_in_2, g_q_lat_2, g_kv_lat_2,
        w_uq_2, w_ukv_2, rel_bias_2, w_out_2, g_norm_ffn_2, w_router_2, w_gate_2, w_up_2,
        w_down_2, g_final_2,
    )


_drawn_inputs = setup_inputs


def setup_inputs(seed=0):
    import zlib

    import numpy as np

    out = dict(_drawn_inputs(seed))
    spreads = {}
    factors = {'mem_ln_g': 5.458,
     'mem_ln_b': 3.253,
     'na_rpb': 5.494,
     'ml_norm_g': 2.85,
     'ml_skip': 4.491,
     'b_ada_2': 4.335,
     'g_norm_mix_2': 8.0,
     'g_q_lat_2': 8.0,
     'g_kv_lat_2': 8.0,
     'w_uq_2': 3.076,
     'rel_bias_2': 3.039,
     'g_norm_ffn_2': 7.894,
     'g_final_2': 2.785}
    for name, (base, spread) in spreads.items():
        noise = np.random.default_rng([zlib.crc32(name.encode()), seed]).standard_normal(out[name].shape)
        drawn = base * np.exp(spread * noise) if base else spread * noise
        out[name] = jnp.asarray(drawn.astype(out[name].dtype))
    for name, factor in factors.items():
        out[name] = (out[name] * factor).astype(out[name].dtype)
    return out
```

```python
import math
from contextlib import ExitStack, contextmanager

import numpy as np
import concourse.bass as bass
from concourse import mybir

F32 = mybir.dt.float32
I32 = mybir.dt.int32
U32 = mybir.dt.uint32
ALU = mybir.AluOpType
ACT = mybir.ActivationFunctionType
AX = mybir.AxisListType
ds = bass.ds

P = 128
S = 512
NT = S // P
D = 1024
KD = D // P
NEG = -1e30

DEPTH = 2
ALPHA = (2 * DEPTH) ** 0.25
LN_EPS = 1e-5
GRID_W = 64
N_MEM = 256
MEM_HEADS, MEM_DH = 4, 64
MEM_W = MEM_HEADS * MEM_DH
NA_HEADS, NA_DH = 12, 64
NA_W = NA_HEADS * NA_DH
WIN_W = 16
SPAN = 2 * WIN_W
ROWS = S // GRID_W
N_CB = GRID_W // WIN_W
ML_HEADS, ML_DH = 4, 192
ML_W = ML_HEADS * ML_DH
CONV_K = 5
N_EXP, N_GRP, EPG = 16, 4, 4
D_EXP = 512
MOE_BLOCKS = 24

MLA_H, Q_RANK, KV_RANK, NOPE, ROPE = 8, 384, 256, 128, 64
DIL_H = 8
DIL = ((128, 1), (512, 4), (2048, 16))
N_REL = 32
EPS2 = 1e-6
CAP = 2 * S // N_EXP
D_FF = 2048


class Stage:

    def __init__(self, nc, name):
        self.nc, self.name, self.sems, self.ctx = nc, name, [], ExitStack()

    def sb(self, name, shape, dt=F32):
        return self.ctx.enter_context(self.nc.sbuf_tensor(f"{self.name}_{name}", list(shape), dt))

    def ps(self, name, shape=(P, 512)):
        return self.ctx.enter_context(self.nc.psum_tensor(f"{self.name}_{name}", list(shape), F32))

    def sem(self, name):
        s = self.nc.alloc_semaphore(f"{self.name}_{name}")
        self.sems.append(s)
        return s


@contextmanager
def stage(nc, name):
    st = Stage(nc, name)
    with st.ctx:
        yield st
    nc.clear_and_free_semaphores(st.sems)
    nc.all_engine_barrier()


def ring_loop(eng, n, body, unroll=2):
    whole = n // unroll
    if whole == 1:
        for r in range(unroll):
            body(r, r, 0)
    elif whole > 1:
        with eng.Fori(0, whole) as i:
            for r in range(unroll):
                body(i * unroll + r, r, i)
    for r in range(n - whole * unroll):
        body(whole * unroll + r, r, whole)


def bcast_rows(vec):
    return vec.partition_broadcast(P)


def gemm(nc, name, W, col0, n_chunks, cw, xT, kp, n_tok, dest, mode, M=P, tok=None,
         clear=None):
    nk = xT.shape[1]
    tp = min(P, n_tok)
    G = cw // M if mode == "T" else n_tok // tp
    ow = n_tok if mode == "T" else cw
    op = M if mode == "T" else tp
    w_view = W.rearrange("(k p) n -> p k n", p=kp)
    if mode == "T":
        d_view = dest.rearrange("(g p) t -> p g t", p=M)
    else:
        d_view = dest.rearrange("(g p) f -> p g f", p=tp)
    with stage(nc, name) as st:
        w = [st.sb(f"w{r}", [kp, nk, cw]) for r in range(2)]
        ob = [st.sb(f"o{r}", [op, G, ow]) for r in range(2)]
        ps = [st.ps(f"ps{b}") for b in range(2 * G)]
        w_ready = [st.sem(f"w_ready{r}") for r in range(2)]
        bank_ready, bank_free = st.sem("bank_ready"), st.sem("bank_free")
        stored, ob_free = st.sem("stored"), st.sem("ob_free")
        if clear is not None:
            z = st.sb("z", [P, D])
            z_ready, cleared = st.sem("z_ready"), st.sem("cleared")
        with nc.Block() as block:

            @block.vector
            def _(dve):
                if clear is not None:
                    nc.vector.memset(z[:], 0.0).then_inc(z_ready, 1)

            @block.sync
            def _(sp):
                def load(j, r, i):
                    sp.wait_ge(bank_free, j * G + 1 + (G - 1))
                    sp.dma_start(w[r][:], w_view[:, :, ds(col0 + j * cw, cw)]).then_inc(w_ready[r], 16)
                ring_loop(sp, n_chunks, load)
                if clear is not None:
                    sp.wait_ge(z_ready, 1)
                    with sp.Fori(0, clear.shape[0] // P) as b:
                        sp.dma_start(clear[ds(b * P, P), :], z[:]).then_inc(cleared, 16)
                    sp.wait_ge(cleared, 16 * (clear.shape[0] // P))

            @block.tensor
            def _(pe):
                def chunk(j, r, i):
                    pe.wait_ge(w_ready[r], (i + 1) * 16)
                    for g in range(G):
                        pe.wait_ge(bank_free, j * G + g + 1)
                        for k in range(nk):
                            if mode == "T":
                                rhs = xT[:, k, 0:n_tok]
                                lhs, rhs = w[r][:, k, g * M:(g + 1) * M], tok(rhs) if tok else rhs
                            else:
                                lhs, rhs = xT[:, k, g * tp:(g + 1) * tp], w[r][:, k, :]
                            mm = nc.tensor.matmul(ps[r * G + g][0:op, 0:ow], lhs, rhs,
                                                  start=(k == 0), stop=(k == nk - 1))
                        mm.then_inc(bank_ready, 1)
                ring_loop(pe, n_chunks, chunk)

            @block.scalar
            def _(act):
                act.sem_inc(bank_free, 2 * G)
                act.sem_inc(ob_free, 2)

                def evict(j, r, i):
                    act.wait_ge(ob_free, j + 1)
                    for g in range(G):
                        act.wait_ge(bank_ready, j * G + g + 1)
                        nc.scalar.activation(ob[r][:, g, :], ps[r * G + g][0:op, 0:ow],
                                             ACT.Copy).then_inc(bank_free, 1)
                ring_loop(act, n_chunks, evict)

            @block.gpsimd
            def _(pool):
                def store(j, r, i):
                    pool.wait_ge(bank_free, j * G + 3 * G)
                    if mode == "T":
                        out = d_view[:, ds(j * G, G), :]
                    else:
                        out = d_view[:, :, ds(j * cw, cw)]
                    pool.dma_start(out, ob[r][:]).then_inc(stored, 16)
                    pool.wait_ge(stored, j * 16 + 16)
                    pool.sem_inc(ob_free, 1)
                ring_loop(pool, n_chunks, store)


def norm(nc, name, x_src, dst, dstT, ident, eps, rms, gain, shift=None, resid=None, alpha=1.0,
         gate=None, one_plus=None, n_tiles=NT, out_dram=None):
    from_dram = x_src.shape[0] != P or len(x_src.shape) == 2
    with stage(nc, name) as st:
        g_bc = st.sb("g", [P, D])
        vecs = [(gain, g_bc)]
        if shift is not None:
            b_bc = st.sb("b", [P, D])
            vecs.append((shift, b_bc))
        if one_plus is not None:
            s_bc = st.sb("s", [P, D])
            vecs.append((one_plus, s_bc))
        if gate is not None:
            t_bc = st.sb("t", [P, D])
            vecs.append((gate, t_bc))
        xin = st.sb("xin", [P, n_tiles, D]) if from_dram else x_src
        res = st.sb("res", [P, n_tiles, D]) if resid is not None else None
        stats = st.sb("stats", [P, n_tiles, 2, 6])
        mv = st.sb("mv", [P, n_tiles, 2])
        sq = st.sb("sq", [P, n_tiles])
        rstd = st.sb("rstd", [P, n_tiles])
        vec_in, x_in = st.sem("vec_in"), [st.sem(f"x_in{t}") for t in range(n_tiles)]
        var_ready, sqrt_ready, y_ready = st.sem("var_ready"), st.sem("sqrt_ready"), st.sem("y_ready")
        t_ready, t_free, out_done = st.sem("t_ready"), st.sem("t_free"), st.sem("out_done")
        ps = [st.ps(f"ps{b}") for b in range(4)]
        per_tile = 16 * ((1 if from_dram else 0) + (1 if resid is not None else 0))
        with nc.Block() as block:

            @block.sync
            def _(sp):
                for t in range(n_tiles):
                    if from_dram:
                        sp.dma_start(xin[:, t, :], x_src[t * P:(t + 1) * P, :]).then_inc(x_in[t], 16)
                    if resid is not None:
                        sp.dma_start(res[:, t, :], resid[t * P:(t + 1) * P, :]).then_inc(x_in[t], 16)
                for v, t in vecs:
                    sp.dma_start(t[:], bcast_rows(v)).then_inc(vec_in, 16)
                if out_dram is not None:
                    for t in range(n_tiles):
                        sp.wait_ge(y_ready, t + 1)
                        sp.dma_start(out_dram[t * P:(t + 1) * P, :], dst[:, t, :]).then_inc(out_done, 16)
                    sp.wait_ge(out_done, 16 * n_tiles)

            @block.vector
            def _(dve):
                if gate is not None:
                    dve.wait_ge(vec_in, 16 * len(vecs))
                for t in range(n_tiles):
                    if per_tile:
                        dve.wait_ge(x_in[t], per_tile)
                    if resid is not None:
                        if gate is not None:
                            nc.vector.tensor_mul(res[:, t, :], res[:, t, :], t_bc[:])
                            nc.vector.drain()
                        nc.vector.scalar_tensor_tensor(xin[:, t, :], xin[:, t, :], alpha, res[:, t, :],
                                                       ALU.mult, ALU.add)
                        nc.vector.drain()
                    for h in range(2):
                        nc.vector.bn_stats(stats[:, t, h, :], xin[:, t, h * 512:(h + 1) * 512])
                    nc.vector.drain()
                    nc.vector.bn_aggr(mv[:, t, :], stats[:, t, :, :].rearrange("p a b -> p (a b)"))
                nc.vector.drain()
                if rms:
                    nc.vector.tensor_mul(sq[:], mv[:, :, 0], mv[:, :, 0])
                    nc.vector.drain()
                    nc.vector.scalar_tensor_tensor(sq[:], mv[:, :, 1], eps, sq[:],
                                                   ALU.add, ALU.add).then_inc(var_ready, 1)
                else:
                    nc.vector.tensor_scalar(sq[:], mv[:, :, 1], eps, None, ALU.add).then_inc(var_ready, 1)
                dve.wait_ge(sqrt_ready, 1)
                nc.vector.reciprocal(rstd[:], sq[:])
                dve.wait_ge(vec_in, 16 * len(vecs))
                if one_plus is not None:
                    nc.vector.scalar_tensor_tensor(g_bc[:], s_bc[:], 1.0, g_bc[:], ALU.add, ALU.mult)
                nc.vector.drain()
                for t in range(n_tiles):
                    if rms:
                        nc.vector.tensor_scalar(dst[:, t, :], xin[:, t, :], rstd[:, t:t + 1], None, ALU.mult)
                    else:
                        nc.vector.tensor_scalar(dst[:, t, :], xin[:, t, :], mv[:, t, 0:1], rstd[:, t:t + 1],
                                                ALU.subtract, ALU.mult)
                    nc.vector.drain()
                    last = nc.vector.tensor_mul(dst[:, t, :], dst[:, t, :], g_bc[:])
                    if shift is not None:
                        nc.vector.drain()
                        last = nc.vector.tensor_add(dst[:, t, :], dst[:, t, :], b_bc[:])
                    last.then_inc(y_ready, 1)

            @block.tensor
            def _(pe):
                if dstT is None:
                    return
                pe.wait_ge(y_ready, n_tiles)
                for c in range(KD):
                    pe.wait_ge(t_free, c + 1)
                    for t in range(n_tiles):
                        mm = nc.tensor.transpose(ps[c % 4][:, t * P:(t + 1) * P],
                                                 dst[:, t, c * P:(c + 1) * P], ident[:])
                    mm.then_inc(t_ready, 1)

            @block.scalar
            def _(act):
                act.sem_inc(t_free, 4)
                act.wait_ge(var_ready, 1)
                nc.scalar.activation(sq[:], sq[:], ACT.Sqrt).then_inc(sqrt_ready, 1)
                if dstT is None:
                    return
                for c in range(KD):
                    act.wait_ge(t_ready, c + 1)
                    nc.scalar.activation(dstT[:, c, 0:n_tiles * P], ps[c % 4][:, 0:n_tiles * P],
                                         ACT.Copy).then_inc(t_free, 1)


def load_transposed(nc, name, src, dstT, ident, kp_list=None):
    with stage(nc, name) as st:
        x = st.sb("x", [P, NT, D])
        x_in, t_ready, t_free = st.sem("x_in"), st.sem("t_ready"), st.sem("t_free")
        ps = [st.ps(f"ps{b}") for b in range(4)]
        with nc.Block() as block:

            @block.sync
            def _(sp):
                sp.dma_start(x[:], src.rearrange("(t p) d -> p t d", p=P)).then_inc(x_in, 16)

            @block.tensor
            def _(pe):
                pe.wait_ge(x_in, 16)
                for c in range(KD):
                    pe.wait_ge(t_free, c + 1)
                    for t in range(NT):
                        mm = nc.tensor.transpose(ps[c % 4][:, t * P:(t + 1) * P],
                                                 x[:, t, c * P:(c + 1) * P], ident[:])
                    mm.then_inc(t_ready, 1)

            @block.scalar
            def _(act):
                act.sem_inc(t_free, 4)
                for c in range(KD):
                    act.wait_ge(t_ready, c + 1)
                    nc.scalar.activation(dstT[:, c, :], ps[c % 4][:], ACT.Copy).then_inc(t_free, 1)


def attention(nc, name, ident, n_heads, dh, dv, nk, q_src, k_src, v_src, q_at, k_at, v_at, out, scale,
              bias_src=None, pe_dims=0, n_keys=S, stats_out=None, v_chunks=None):
    U = 4
    nc_k = nk // P
    with stage(nc, name) as st:
        n_parts = 2 if pe_dims else 1
        dims = [dh] + ([pe_dims] if pe_dims else [])
        q = [[st.sb(f"q{r}{a}", [dims[a], S]) for a in range(n_parts)] for r in range(2)]
        k = [[st.sb(f"k{r}{a}", [dims[a], n_keys]) for a in range(n_parts)] for r in range(2)]
        v = [st.sb(f"v{r}", [P, v_chunks, dv]) for r in range(2)]
        bias = [st.sb(f"bias{r}", [P, U * nk]) for r in range(2)] if bias_src else None
        ssb = [st.sb(f"s{r}", [P, nk]) for r in range(2)]
        pr = [st.sb(f"p{r}", [P, nk]) for r in range(2)]
        pT = [st.sb(f"pT{r}", [P, nk]) for r in range(2)]
        ob = [st.sb(f"o{r}", [P, U, dv]) for r in range(2)]
        nmx = st.sb("nmx", [P, 8])
        den = st.sb("den", [P, 8])
        rden = st.sb("rden", [P, 8])
        stat = st.sb("stat", [P, U, n_heads, 2]) if stats_out is not None else None
        s_ps = [st.ps(f"s_ps{b}") for b in range(2)]
        t_ps = [st.ps(f"t_ps{b}") for b in range(2)]
        o_ps = [st.ps(f"o_ps{b}") for b in range(2)]
        head_in = [st.sem(f"head_in{r}") for r in range(2)]
        s_ready, s_free = st.sem("s_ready"), st.sem("s_free")
        max_ready = st.sem("max_ready")
        exp_done = st.sem("exp_done")
        pT_ready = st.sem("pT_ready")
        pT_copied = st.sem("pT_copied")
        pv_done = st.sem("pv_done")
        out_done = st.sem("out_done")
        stored, ob_free = st.sem("stored"), st.sem("ob_free")
        stat_done = st.sem("stat_done")
        probe = [len(q_src(0)), len(k_src(0)), len(v_src(0))]
        n_loads = sum(probe) + (1 if bias_src else 0)
        with nc.Block() as block:

            @block.sync
            def _(sp):
                def load(j, r, i):
                    sp.wait_ge(out_done, j * U + 4)
                    for a, ap in enumerate(q_src(j)):
                        sp.dma_start(q[r][a][:], ap).then_inc(head_in[r], 16)
                    for a, ap in enumerate(k_src(j)):
                        sp.dma_start(k[r][a][:], ap).then_inc(head_in[r], 16)
                    for sl, ap in v_src(j):
                        sp.dma_start(v[r][sl], ap).then_inc(head_in[r], 16)
                    if bias_src:
                        sp.dma_start(bias[r][:], bias_src(j)).then_inc(head_in[r], 16)
                ring_loop(sp, n_heads, load)

            @block.tensor
            def _(pe):
                def scores(j, r, i, u):
                    n = j * U + u
                    if u == 0:
                        pe.wait_ge(head_in[r], (i + 1) * (16 * n_loads))
                    pe.wait_ge(s_free if bias_src else exp_done, n + 1)
                    for a in range(n_parts):
                        mm = nc.tensor.matmul(s_ps[u % 2][:, 0:nk], q_at(q[r][a], u), k_at(k[r][a], u),
                                              start=(a == 0), stop=(a == n_parts - 1))
                    mm.then_inc(s_ready, 1)

                def turn(j, r, i, u):
                    n = j * U + u
                    pe.wait_ge(exp_done, n + 3)
                    pe.wait_ge(pT_copied, n + 1)
                    for c in range(nc_k):
                        mm = nc.tensor.transpose(t_ps[u % 2][:, c * P:(c + 1) * P],
                                                 pr[u % 2][:, c * P:(c + 1) * P], ident[:])
                    mm.then_inc(pT_ready, 1)

                def values(j, r, i, u):
                    n = j * U + u
                    pe.wait_ge(pT_copied, n + 3)
                    pe.wait_ge(out_done, n + 7)
                    for c in range(nc_k):
                        mm = nc.tensor.matmul(o_ps[u % 2][:, 0:dv], pT[u % 2][:, c * P:(c + 1) * P],
                                              v[r][:, v_at(u)[c], :], start=(c == 0), stop=(c == nc_k - 1))
                    mm.then_inc(pv_done, 1)

                def pair(i, rs):
                    todo = [(i * 2 + r, r, i, u) for r in rs for u in range(U)]
                    scores(*todo[0])
                    for n, item in enumerate(todo):
                        if n + 1 < len(todo):
                            scores(*todo[n + 1])
                        turn(*item)
                        values(*item)
                if n_heads > 2:
                    with pe.Fori(0, n_heads // 2) as i:
                        pair(i, (0, 1))
                else:
                    pair(0, (0, 1))

            @block.vector
            def _(dve):
                dve.sem_inc(out_done, 8)

                def maxes(j, r, i, u):
                    n = j * U + u
                    c = r * U + u
                    dve.wait_ge(s_ready, n + 1)
                    if bias_src:
                        dve.wait_ge(exp_done, n + 1)
                        nc.vector.scalar_tensor_tensor(ssb[u % 2][:], s_ps[u % 2][:, 0:nk], scale,
                                                       bias[r][:, u * nk:(u + 1) * nk], ALU.mult,
                                                       ALU.add).then_inc(s_free, 1)
                        nc.vector.drain()
                        nc.vector.tensor_reduce(nmx[:, c:c + 1], ssb[u % 2][:], AX.X, ALU.max, negate=True) \
                            .then_inc(max_ready, 1)
                    else:
                        nc.vector.tensor_reduce(nmx[:, c:c + 1], s_ps[u % 2][:, 0:nk], AX.X, ALU.max)
                        nc.vector.drain()
                        nc.vector.tensor_scalar(nmx[:, c:c + 1], nmx[:, c:c + 1], -scale, None, ALU.mult) \
                            .then_inc(max_ready, 1)

                def outs(j, r, i, u):
                    n = j * U + u
                    c = r * U + u
                    dve.wait_ge(pv_done, n + 3)
                    dve.wait_ge(exp_done, n + 3)
                    if u == 0:
                        dve.wait_ge(ob_free, j + 1)
                    nc.vector.reciprocal(rden[:, c:c + 1], den[:, c:c + 1])
                    if stat is not None:
                        nc.vector.tensor_copy(stat[:, u, ds(j, 1), 0:1].rearrange("p a b -> p (a b)"), nmx[:, c:c + 1])
                        nc.vector.tensor_copy(stat[:, u, ds(j, 1), 1:2].rearrange("p a b -> p (a b)"), den[:, c:c + 1])
                    nc.vector.drain()
                    nc.vector.tensor_scalar(ob[r][:, u, :], o_ps[u % 2][:, 0:dv], rden[:, c:c + 1], None,
                                            ALU.mult).then_inc(out_done, 1)

                def pair(i, rs):
                    todo = [(i * 2 + r, r, i, u) for r in rs for u in range(U)]
                    maxes(*todo[0])
                    for n, item in enumerate(todo):
                        if n + 1 < len(todo):
                            maxes(*todo[n + 1])
                        outs(*item)
                if n_heads > 2:
                    with dve.Fori(0, n_heads // 2) as i:
                        pair(i, (0, 1))
                else:
                    pair(0, (0, 1))

            @block.scalar
            def _(act):
                act.sem_inc(exp_done, 2)
                act.sem_inc(pT_copied, 2)

                def exps(j, r, i, u):
                    n = j * U + u
                    c = r * U + u
                    act.wait_ge(max_ready, n + 1)
                    act.wait_ge(pT_ready, n + 1)
                    src = ssb[u % 2][:] if bias_src else s_ps[u % 2][:, 0:nk]
                    e = nc.scalar.activation(pr[u % 2][:], src, ACT.Exp, bias=nmx[:, c:c + 1],
                                             scale=1.0 if bias_src else scale, accum_out=den[:, c:c + 1])
                    e.then_inc(exp_done, 1)

                def copies(j, r, i, u):
                    n = j * U + u
                    act.wait_ge(pT_ready, n + 3)
                    act.wait_ge(pv_done, n + 1)
                    nc.scalar.activation(pT[u % 2][:], t_ps[u % 2][:, 0:nk], ACT.Copy).then_inc(pT_copied, 1)

                def pair(i, rs):
                    todo = [(i * 2 + r, r, i, u) for r in rs for u in range(U)]
                    exps(*todo[0])
                    for n, item in enumerate(todo):
                        if n + 1 < len(todo):
                            exps(*todo[n + 1])
                        copies(*item)
                if n_heads > 2:
                    with act.Fori(0, n_heads // 2) as i:
                        pair(i, (0, 1))
                else:
                    pair(0, (0, 1))

            @block.gpsimd
            def _(pool):
                if bias_src:
                    pool.sem_inc(s_free, 2)
                pool.sem_inc(pT_ready, 2)
                pool.sem_inc(pv_done, 2)
                pool.sem_inc(ob_free, 2)

                def store(j, r, i):
                    for u in range(U):
                        pool.wait_ge(out_done, j * U + u + 9)
                        pool.dma_start(out(j, u), ob[r][:, u, :]).then_inc(stored, 16)
                    pool.wait_ge(stored, (j + 1) * (16 * U))
                    pool.sem_inc(ob_free, 1)
                ring_loop(pool, n_heads, store)
                if stats_out is not None:
                    for u in range(U):
                        pool.dma_start(stats_out(u), stat[:, u, :, :].rearrange("p h s -> p (h s)")) \
                            .then_inc(stat_done, 16)
                    pool.wait_ge(stat_done, 16 * U)

USED = ("x", "mem", "mem_ln_g", "mem_ln_b", "w_mem_kv", "router_w", "router_b", "na_w_in", "na_bias", "w_out",
        "ln_g", "ln_b", "exp_w_gate", "exp_w_up", "exp_w_down", "ml_w_in", "ml_conv_wT", "ml_conv_bP", "ml_w_qkv",
        "ml_gate_bT", "ml_norm_gP", "ml_skipP", "c_P", "w_ada_2", "b_ada_2", "g_norm_mix_2", "w_in_2", "g_q_lat_P",
        "g_kv_lat_P", "w_uq_L", "w_ukv_L", "positions_2", "inv_freq", "rel_tab", "pos_q", "band_mask", "w_out_2",
        "g_norm_ffn_2", "w_router_2", "w_gate_2", "w_up_2", "w_down_2", "g_final_2")


def consts(nc, ident, strict, ones, iota, pidx):
    with stage(nc, "consts") as st:
        it = st.sb("it", [P, P], I32)
        pi = st.sb("pi", [P, 1], I32)
        c_ready = st.sem("c_ready")
        with nc.Block() as block:

            @block.gpsimd
            def _(pool):
                nc.gpsimd.iota(it[:], [[1, P]], base=0, channel_multiplier=0)
                nc.gpsimd.iota(pi[:], [[0, 1]], base=0, channel_multiplier=1)
                nc.gpsimd.memset(ones[:], 1.0)
                nc.gpsimd.drain().then_inc(c_ready, 1)

            @block.vector
            def _(dve):
                dve.wait_ge(c_ready, 1)
                nc.vector.tensor_copy(iota[:], it[:])
                nc.vector.tensor_copy(pidx[:], pi[:])
                nc.vector.drain()
                nc.vector.tensor_scalar(ident[:], iota[:], pidx[:, 0:1], None, ALU.is_equal)
                nc.vector.tensor_scalar(strict[:], iota[:], pidx[:, 0:1], None, ALU.is_gt)


def route(nc, name, xT, x, router_w, router_b, sbr, strict, ones, iota, spill=None):
    posA, posB, wA, wB, blk_e = sbr
    with stage(nc, name) as st:
        E = N_EXP
        rw = st.sb("rw", [P, KD, E])
        rb = st.sb("rb", [P, E])
        loaded = st.sem("loaded")
        logit_ready, e_ready = st.sem("logit_ready"), st.sem("e_ready")
        m_ready, cum_ready = st.sem("m_ready"), st.sem("cum_ready")
        lg = st.ps("lg")
        cm = st.ps("cm")
        sc = st.sb("sc", [P, NT, E])
        bi = st.sb("bi", [P, NT, E])
        tmp = st.sb("tmp", [P, NT, E])
        pairs = st.sb("pairs", [P, NT * N_GRP])
        gs = st.sb("gs", [P, NT * N_GRP])
        g1 = st.sb("g1", [P, NT])
        taken = st.sb("taken", [P, NT])
        first = st.sb("first", [P, NT, N_GRP])
        rank_e = st.sb("rank_e", [P, NT, E])
        oh = [st.sb(f"oh{n}", [P, NT, E]) for n in range(2)]
        both = st.sb("both", [P, NT, E])
        wsum = st.sb("wsum", [P, NT])
        nb = st.sb("nb", [P, E])
        nb2 = st.sb("nb2", [P, E])
        nbt = st.sb("nbt", [P, E])
        pos = st.sb("pos", [P, NT, E])
        bl = st.sb("bl", [P, MOE_BLOCKS])
        with nc.Block() as block:

            @block.sync
            def _(sp):
                sp.dma_start(rw[:], router_w.rearrange("(k p) e -> p k e", p=P)).then_inc(loaded, 16)
                sp.dma_start(rb[:], bcast_rows(router_b)).then_inc(loaded, 16)

            @block.tensor
            def _(pe):
                pe.wait_ge(loaded, 32)
                for t in range(NT):
                    for k in range(KD):
                        mm = nc.tensor.matmul(lg[:, t * E:(t + 1) * E], xT[:, k, t * P:(t + 1) * P], rw[:, k, :],
                                              start=(k == 0), stop=(k == KD - 1))
                mm.then_inc(logit_ready, 1)
                pe.wait_ge(m_ready, 1)
                for t in range(NT):
                    for a in range(t):
                        nc.tensor.matmul(cm[:, t * E:(t + 1) * E], ones[:], both[:, a, :], start=(a == 0), stop=False)
                    nc.tensor.matmul(cm[:, t * E:(t + 1) * E], strict[:], both[:, t, :], start=(t == 0), stop=True)
                for t in range(NT):
                    mm = nc.tensor.matmul(cm[:, NT * E:(NT + 1) * E], ones[:], both[:, t, :],
                                          start=(t == 0), stop=(t == NT - 1))
                mm.then_inc(cum_ready, 1)

            @block.scalar
            def _(act):
                act.wait_ge(logit_ready, 1)
                nc.scalar.activation(sc[:].rearrange("p t e -> p (t e)"), lg[:, 0:NT * E], ACT.Exp,
                                     scale=-1.0).then_inc(e_ready, 1)

            @block.vector
            def _(dve):
                V = nc.vector
                V.drain()
                for e in range(E):
                    V.memset(rank_e[:, :, e:e + 1], float(E - e))
                dve.wait_ge(e_ready, 1)
                dve.wait_ge(loaded, 32)
                V.tensor_scalar(tmp[:], sc[:], 1.0, None, ALU.add)
                V.drain()
                V.reciprocal(sc[:], tmp[:])
                V.drain()
                for t in range(NT):
                    V.tensor_add(bi[:, t, :], sc[:, t, :], rb[:])
                V.drain()
                b4 = bi[:].rearrange("p t (g j) -> p (t g) j", j=EPG)
                pr = [(a, b) for a in range(EPG) for b in range(a + 1, EPG)]
                for n, (a, b) in enumerate(pr):
                    V.tensor_add(gs[:] if n == 0 else pairs[:], b4[:, :, a], b4[:, :, b])
                    V.drain()
                    if n:
                        V.tensor_max(gs[:], gs[:], pairs[:])
                        V.drain()
                gs3 = gs[:].rearrange("p (t g) -> p t g", g=N_GRP)
                V.tensor_reduce(g1[:], gs3, AX.X, ALU.max)
                V.memset(taken[:], 0.0)
                V.drain()
                for g in range(N_GRP):
                    V.tensor_tensor(first[:, :, g], gs3[:, :, g], g1[:], ALU.is_equal)
                    V.drain()
                    V.scalar_tensor_tensor(first[:, :, g], taken[:], 1.0, first[:, :, g], ALU.is_lt, ALU.mult)
                    V.drain()
                    V.tensor_add(taken[:], taken[:], first[:, :, g])
                    V.drain()
                for g in range(N_GRP):
                    for j in range(EPG):
                        e = g * EPG + j
                        V.tensor_mul(bi[:, :, e], bi[:, :, e], first[:, :, g])
                        V.tensor_scalar(tmp[:, :, e], first[:, :, g], 1.0, -NEG, ALU.subtract, ALU.mult)
                V.drain()
                V.tensor_add(bi[:], bi[:], tmp[:])
                V.drain()
                for n in range(2):
                    V.tensor_reduce(g1[:], bi[:], AX.X, ALU.max)
                    V.drain()
                    for t in range(NT):
                        V.scalar_tensor_tensor(tmp[:, t, :], bi[:, t, :], g1[:, t:t + 1], rank_e[:, t, :],
                                               ALU.is_equal, ALU.mult)
                    V.drain()
                    V.tensor_reduce(g1[:], tmp[:], AX.X, ALU.max)
                    V.drain()
                    for t in range(NT):
                        V.tensor_scalar(oh[n][:, t, :], tmp[:, t, :], g1[:, t:t + 1], None, ALU.is_equal)
                    V.drain()
                    if n == 0:
                        V.scalar_tensor_tensor(bi[:], oh[0][:], -1e38, bi[:], ALU.mult, ALU.add)
                        V.drain()
                V.tensor_add(both[:], oh[0][:], oh[1][:]).then_inc(m_ready, 1)
                for n, wt in ((0, wA), (1, wB)):
                    V.tensor_mul(tmp[:], oh[n][:], sc[:])
                    V.drain()
                    V.tensor_reduce(wt[:], tmp[:], AX.X, ALU.add)
                    V.drain()
                V.tensor_add(wsum[:], wA[:], wB[:])
                V.drain()
                V.reciprocal(wsum[:], wsum[:])
                V.drain()
                V.tensor_mul(wA[:], wA[:], wsum[:])
                V.tensor_mul(wB[:], wB[:], wsum[:])
                dve.wait_ge(cum_ready, 1)
                cnt = cm[:, NT * E:(NT + 1) * E]
                V.tensor_scalar(nb[:], cnt, 0.0, None, ALU.is_gt)
                for q in range(1, S // P):
                    V.drain()
                    V.tensor_scalar(nbt[:], cnt, float(q * P), None, ALU.is_gt)
                    V.drain()
                    V.tensor_add(nb[:], nb[:], nbt[:])
                V.drain()
                V.tensor_copy(nbt[:], nb[:])
                V.drain()
                a, b = nb, nb2
                for sh in (1, 2, 4, 8):
                    V.tensor_copy(b[:, 0:sh], a[:, 0:sh])
                    V.tensor_add(b[:, sh:E], a[:, sh:E], a[:, 0:E - sh])
                    V.drain()
                    a, b = b, a
                V.tensor_sub(nbt[:], a[:], nbt[:])
                V.memset(bl[:], 0.0)
                V.drain()
                for t in range(NT):
                    V.scalar_tensor_tensor(pos[:, t, :], nbt[:], float(P), cm[:, t * E:(t + 1) * E],
                                           ALU.mult, ALU.add)
                for e in range(E):
                    V.scalar_tensor_tensor(bl[:], iota[:, 0:MOE_BLOCKS], a[:, e:e + 1], bl[:], ALU.is_ge, ALU.add)
                    V.drain()
                V.tensor_scalar(bl[:], bl[:], float(E - 1), None, ALU.min)
                V.drain()
                V.tensor_copy(blk_e[:, 0:MOE_BLOCKS], bl[:])
                V.drain()
                V.tensor_scalar(bl[:, 0:MOE_BLOCKS // 2], iota[:, 0:MOE_BLOCKS // 2], 2.0, a[:, E - 1:E],
                                ALU.mult, ALU.is_lt)
                V.drain()
                V.tensor_reduce(nb2[:, 0:1] if a is nb else nb[:, 0:1], bl[:, 0:MOE_BLOCKS // 2], AX.X, ALU.add)
                V.drain()
                V.tensor_copy(blk_e[:, MOE_BLOCKS:MOE_BLOCKS + 1], nb2[:, 0:1] if a is nb else nb[:, 0:1])
                for n, pt in ((0, posA), (1, posB)):
                    V.tensor_mul(tmp[:], oh[n][:], pos[:])
                    V.drain()
                    V.tensor_reduce(pt[:], tmp[:], AX.X, ALU.add)
                    V.drain()


def scatter_rows(nc, name, x, sbr, slots_dram):
    posA, posB, wA, wB, blk_e = sbr
    with stage(nc, name) as st:
        idx = [st.sb(f"idx{n}", [P, NT], U32) for n in range(2)]
        idx_ready, put = st.sem("idx_ready"), st.sem("put")
        with nc.Block() as block:

            @block.vector
            def _(dve):
                nc.vector.tensor_copy(idx[0][:], posA[:])
                nc.vector.tensor_copy(idx[1][:], posB[:])
                nc.vector.drain().then_inc(idx_ready, 1)

            @block.gpsimd
            def _(pool):
                pool.wait_ge(idx_ready, 1)
                for t in range(NT):
                    for n in range(2):
                        pool.indirect_dma_start(out=slots_dram, in_=x[:, t, :], in_offset=None,
                                                out_offset=bass.IndirectOffsetOnAxis(ap=idx[n][:, t:t + 1], axis=0)) \
                            .then_inc(put, 16)
                pool.wait_ge(put, 16 * 2 * NT)


def moe_experts(nc, name, ident, sbr, slots_dram, w_gate, w_up, w_down, y_dram):
    blk_e = sbr[4]
    KF = D_EXP // P
    with stage(nc, name) as st:
        w = [[st.sb(f"w{n}{r}", [P, KD * D_EXP]) for r in range(2)] for n in range(3)]
        w_ready = [[st.sem(f"w_ready{n}{r}") for r in range(2)] for n in range(3)]
        xs = [st.sb(f"xs{r}", [P, D]) for r in range(2)]
        xs_ready = [st.sem(f"xs_ready{r}") for r in range(2)]
        xg = [st.sb(f"xg{r}", [P, KD * P]) for r in range(2)]
        sig = st.sb("sig", [P, D_EXP])
        hid = [st.sb(f"hid{r}", [P, D_EXP]) for r in range(2)]
        hT = st.sb("hT", [P, KF * P])
        yb = [st.sb(f"y{r}", [P, D]) for r in range(2)]
        x_ps, h_ps = st.ps("x_ps"), st.ps("h_ps")
        g_ps = [st.ps(f"g_ps{r}") for r in range(2)]
        u_ps = [st.ps(f"u_ps{r}") for r in range(2)]
        y_ps = [st.ps(f"y_ps{r}") for r in range(2)]
        turned = st.sem("turned")
        xg_copied = st.sem("xg_copied")
        gate_ready, up_ready, sig_ready = st.sem("gate_ready"), st.sem("up_ready"), st.sem("sig_ready")
        hid_ready = st.sem("hid_ready")
        hT_ps_ready = st.sem("hT_ps_ready")
        hT_ready = st.sem("hT_ready")
        down_ready = st.sem("down_ready")
        y_copied = st.sem("y_copied")
        stored, yb_free = st.sem("stored"), st.sem("yb_free")

        def pairs(eng):
            return eng.value_load(blk_e[0:1, MOE_BLOCKS:MOE_BLOCKS + 1], min_val=1, max_val=MOE_BLOCKS // 2)

        with nc.Block() as block:

            @block.sync
            def _(sp):
                with sp.Fori(0, pairs(sp)) as i:
                    for r in range(2):
                        b = 2 * i + r
                        e = sp.value_load(blk_e[0:1, ds(b, 1)], min_val=0, max_val=N_EXP - 1)
                        sp.wait_ge(hid_ready, b + 1)
                        sp.dma_start(xs[r][:], slots_dram[ds(b * P, P), :]).then_inc(xs_ready[r], 16)
                        for n, src in enumerate((w_gate, w_up)):
                            sp.dma_start(w[n][r][:], src[ds(e, 1)].rearrange("a (k p) n -> p (a k) n", p=P)) \
                                .then_inc(w_ready[n][r], 16)
                        sp.wait_ge(down_ready, 2 * b + 2)
                        sp.dma_start(w[2][r][:], w_down[ds(e, 1)].rearrange("a (k p) n -> p (a k) n", p=P)) \
                            .then_inc(w_ready[2][r], 16)

            @block.tensor
            def _(pe):
                with pe.Fori(0, pairs(pe)) as i:
                    def gate_up(r):
                        b = 2 * i + r
                        pe.wait_ge(xs_ready[r], 16 * i + 16)
                        for h in range(2):
                            pe.wait_ge(xg_copied, 2 * b + h + 1)
                            for c in range(4):
                                cc = h * 4 + c
                                mm = nc.tensor.transpose(x_ps[:, c * P:(c + 1) * P], xs[r][:, cc * P:(cc + 1) * P],
                                                         ident[:])
                            mm.then_inc(turned, 1)
                        pe.wait_ge(xg_copied, 2 * b + 3)
                        pe.wait_ge(hid_ready, b + 1)
                        for n, (ps, done) in enumerate(((g_ps, gate_ready), (u_ps, up_ready))):
                            pe.wait_ge(w_ready[n][r], 16 * i + 16)
                            for k in range(KD):
                                mm = nc.tensor.matmul(ps[r][:], xg[r][:, k * P:(k + 1) * P],
                                                      w[n][r][:, k * D_EXP:(k + 1) * D_EXP],
                                                      start=(k == 0), stop=(k == KD - 1))
                            mm.then_inc(done, 1)

                    def down(r):
                        b = 2 * i + r
                        pe.wait_ge(hid_ready, b + 3)
                        pe.wait_ge(hT_ready, b + 1)
                        for f in range(KF):
                            mm = nc.tensor.transpose(h_ps[:, f * P:(f + 1) * P], hid[r][:, f * P:(f + 1) * P], ident[:])
                        mm.then_inc(hT_ps_ready, 1)
                        pe.wait_ge(hT_ready, b + 2)
                        pe.wait_ge(w_ready[2][r], 16 * i + 16)
                        for h in range(2):
                            pe.wait_ge(y_copied, 2 * b + h + 1)
                            for f in range(KF):
                                mm = nc.tensor.matmul(y_ps[h][:], hT[:, f * P:(f + 1) * P],
                                                      w[2][r][:, f * D + h * 512:f * D + (h + 1) * 512],
                                                      start=(f == 0), stop=(f == KF - 1))
                            mm.then_inc(down_ready, 1)
                    gate_up(0)
                    gate_up(1)
                    down(0)
                    down(1)

            @block.vector
            def _(dve):
                V = nc.vector
                dve.sem_inc(hid_ready, 2)
                with dve.Fori(0, pairs(dve)) as i:
                    def hidden(r):
                        b = 2 * i + r
                        dve.wait_ge(sig_ready, b + 1)
                        V.tensor_mul(hid[r][:], sig[:], g_ps[r][:])
                        V.drain()
                        dve.wait_ge(up_ready, b + 1)
                        V.tensor_mul(hid[r][:], hid[r][:], u_ps[r][:]).then_inc(hid_ready, 1)

                    def turn(r):
                        dve.wait_ge(hT_ps_ready, 2 * i + r + 1)
                        dve.wait_ge(down_ready, 2 * (2 * i + r) + 4)
                        V.tensor_copy(hT[:], h_ps[:]).then_inc(hT_ready, 1)
                    hidden(0)
                    hidden(1)
                    turn(0)
                    turn(1)

            @block.scalar
            def _(act):
                act.sem_inc(xg_copied, 1)
                act.sem_inc(hT_ready, 1)
                act.sem_inc(down_ready, 4)
                act.sem_inc(y_copied, 2)
                act.sem_inc(yb_free, 2)
                with act.Fori(0, pairs(act)) as i:
                    for r in range(2):
                        b = 2 * i + r
                        for h in range(2):
                            act.wait_ge(turned, 2 * b + h + 1)
                            nc.scalar.activation(xg[r][:, h * 512:(h + 1) * 512], x_ps[:],
                                                 ACT.Copy).then_inc(xg_copied, 1)
                        act.wait_ge(gate_ready, b + 1)
                        act.wait_ge(hid_ready, b + 2)
                        nc.scalar.activation(sig[:], g_ps[r][:], ACT.Sigmoid).then_inc(sig_ready, 1)
                    for r in range(2):
                        b = 2 * i + r
                        act.wait_ge(yb_free, b + 1)
                        for h in range(2):
                            act.wait_ge(down_ready, 2 * b + h + 5)
                            nc.scalar.activation(yb[r][:, h * 512:(h + 1) * 512], y_ps[h][:],
                                                 ACT.Copy).then_inc(y_copied, 1)

            @block.gpsimd
            def _(pool):
                with pool.Fori(0, pairs(pool)) as i:
                    for r in range(2):
                        b = 2 * i + r
                        pool.wait_ge(y_copied, 2 * b + 4)
                        pool.dma_start(y_dram[ds(b * P, P), :], yb[r][:]).then_inc(stored, 16)
                        pool.wait_ge(stored, 16 * b + 16)
                        pool.sem_inc(yb_free, 1)


def moe_combine(nc, name, sbr, y_dram, out_dram):
    posA, posB, wA, wB, blk_e = sbr
    with stage(nc, name) as st:
        idx = [st.sb(f"idx{n}", [P, NT], U32) for n in range(2)]
        row = [[st.sb(f"row{n}{t}", [P, D]) for t in range(NT)] for n in range(2)]
        idx_ready, got, done, stored = st.sem("idx_ready"), st.sem("got"), st.sem("done"), st.sem("stored")
        with nc.Block() as block:

            @block.vector
            def _(dve):
                nc.vector.tensor_copy(idx[0][:], posA[:])
                nc.vector.tensor_copy(idx[1][:], posB[:])
                nc.vector.drain().then_inc(idx_ready, 1)
                dve.wait_ge(got, 16 * 2 * NT)
                for t in range(NT):
                    nc.vector.tensor_scalar(row[0][t][:], row[0][t][:], wA[:, t:t + 1], None, ALU.mult)
                nc.vector.drain()
                for t in range(NT):
                    nc.vector.scalar_tensor_tensor(row[0][t][:], row[1][t][:], wB[:, t:t + 1], row[0][t][:],
                                                   ALU.mult, ALU.add).then_inc(done, 1)

            @block.gpsimd
            def _(pool):
                pool.wait_ge(idx_ready, 1)
                for t in range(NT):
                    for n in range(2):
                        pool.indirect_dma_start(out=row[n][t][:], out_offset=None, in_=y_dram,
                                                in_offset=bass.IndirectOffsetOnAxis(ap=idx[n][:, t:t + 1], axis=0)) \
                            .then_inc(got, 16)

            @block.sync
            def _(sp):
                for t in range(NT):
                    sp.wait_ge(done, t + 1)
                    sp.dma_start(out_dram[t * P:(t + 1) * P, :], row[0][t][:]).then_inc(stored, 16)
                sp.wait_ge(stored, 16 * NT)


def first_inputs_stage(nc, x, x_dram):
    with stage(nc, "load_x") as st:
        x_in = st.sem("x_in")
        with nc.Block() as block:

            @block.sync
            def _(sp):
                sp.dma_start(x[:], x_dram.rearrange("(t p) d -> p t d", p=P)).then_inc(x_in, 16)
                sp.wait_ge(x_in, 16)


def moe_layer(nc, i, a, x, xT, cst, slots, y_dram, f_dram, sbr):
    ident, strict, ones, iota, pidx = cst
    route(nc, f"route{i}", xT, x, a["router_w"], a["router_b"], sbr, strict, ones, iota)
    scatter_rows(nc, f"scat{i}", x, sbr, slots)
    moe_experts(nc, f"moe{i}", ident, sbr, slots, a["exp_w_gate"][i], a["exp_w_up"][i], a["exp_w_down"][i], y_dram)
    moe_combine(nc, f"comb{i}", sbr, y_dram, f_dram)


def memory_attention(nc, name, ident, q_dram, mk_dram, mv_dram, mix):
    attention(nc, name, ident, MEM_HEADS, MEM_DH, MEM_DH, N_MEM,
              lambda h: [q_dram[ds(h * MEM_DH, MEM_DH), :]],
              lambda h: [mk_dram[ds(h * MEM_DH, MEM_DH), :]],
              lambda h: [((slice(None), slice(0, 2), slice(None)),
                          mv_dram.rearrange("(c p) f -> p c f", p=P)[:, :, ds(h * MEM_DH, MEM_DH)])],
              lambda q, u: q[:, u * P:(u + 1) * P], lambda k, u: k[:, :], lambda u: (0, 1),
              lambda h, u: mix[u * P:(u + 1) * P, ds(NA_W + h * MEM_DH, MEM_DH)],
              MEM_DH ** -0.5, n_keys=N_MEM, v_chunks=2)


def build(nc, a, out):
    def dram(name, shape, dt=F32):
        return nc.dram_tensor(name, list(shape), dt, kind="Internal").ap()

    with ExitStack() as ctx:
        def sb(name, shape, dt=F32):
            return ctx.enter_context(nc.sbuf_tensor(name, list(shape), dt))

        x, xT = sb("x", [P, NT, D]), sb("xT", [P, KD, S])
        ident, strict, ones, iota = (sb(n, [P, P]) for n in ("ident", "strict", "ones", "iota"))
        pidx = sb("pidx", [P, 1])
        sbr = [sb(n, [P, NT]) for n in ("posA", "posB", "wA", "wB")] + [sb("blk_e", [P, MOE_BLOCKS + 1], I32)]
        cst = (ident, strict, ones, iota, pidx)
        consts(nc, *cst)

        mk, mv = dram("mk", [MEM_W, N_MEM]), dram("mv", [N_MEM, MEM_W])
        norm(nc, "mem_ln", a["mem"][0], x, xT, ident, LN_EPS, False, a["mem_ln_g"], a["mem_ln_b"], n_tiles=N_MEM // P)
        gemm(nc, "mem_k", a["w_mem_kv"], 0, 1, MEM_W, xT, P, N_MEM, mk, "T")
        gemm(nc, "mem_v", a["w_mem_kv"], MEM_W, 1, MEM_W, xT, P, N_MEM, mv, "N")

        load_transposed(nc, "x_in", a["x"][0], xT, ident)
        first_inputs_stage(nc, x, a["x"][0])
        naq, nak, nav = dram("naq", [NA_W, S]), dram("nak", [NA_W, S]), dram("nav", [S, NA_W])
        memq = dram("memq", [MEM_W, S])
        mix = dram("mix", [S, D])
        win = a["na_w_in"][0]
        slots, y_dram = dram("x_slots", [MOE_BLOCKS * P, D]), dram("y_slots", [MOE_BLOCKS * P, D])
        by_cb = lambda ap: ap.rearrange("p (r b c) -> p b r c", r=ROWS, c=WIN_W)
        gemm(nc, "na_q", win, 0, 2, 384, xT, P, S, naq, "T", tok=by_cb, clear=slots)
        gemm(nc, "na_k", win, NA_W, 2, 384, xT, P, S, nak, "T", clear=y_dram)
        gemm(nc, "na_v", win, 2 * NA_W, 2, 384, xT, P, S, nav, "N")
        gemm(nc, "na_m", win, 3 * NA_W, 1, MEM_W, xT, P, S, memq, "T")
        start = [min(max(b * WIN_W - WIN_W // 2, 0), GRID_W - SPAN) for b in range(N_CB)]
        nav_rc = nav.rearrange("(r c) f -> r c f", c=GRID_W)
        mix_rc = mix.rearrange("(r c) f -> r c f", c=GRID_W)
        attention(nc, "na", ident, NA_HEADS, NA_DH, NA_DH, ROWS * SPAN,
                  lambda h: [naq[ds(h * NA_DH, NA_DH), :]],
                  lambda h: [nak[ds(h * NA_DH, NA_DH), :]],
                  lambda h: [((slice(None), 2 * b + half, slice(None)),
                              nav_rc[4 * half:4 * half + 4, start[b]:start[b] + SPAN, ds(h * NA_DH, NA_DH)])
                             for b in range(N_CB) for half in range(2)],
                  lambda q, u: q[:, u * P:(u + 1) * P],
                  lambda k, u: k[:, :].rearrange("p (r c) -> p r c", c=GRID_W)[:, :, start[u]:start[u] + SPAN],
                  lambda u: (2 * u, 2 * u + 1),
                  lambda h, u: mix_rc[:, u * WIN_W:(u + 1) * WIN_W, ds(h * NA_DH, NA_DH)],
                  NA_DH ** -0.5, bias_src=lambda h: a["na_bias"].rearrange("h p n -> p h n")[:, ds(h, 1), :],
                  v_chunks=8)
        memory_attention(nc, "mem0", ident, memq, mk, mv, mix)
        proj = dram("proj", [S, D])
        load_transposed(nc, "mixT0", mix, xT, ident)
        gemm(nc, "out0", a["w_out"][0], 0, 2, 512, xT, P, S, proj, "N")
        norm(nc, "ln00", x, x, xT, ident, LN_EPS, False, a["ln_g"][0, 0], a["ln_b"][0, 0], resid=proj, alpha=ALPHA)
        moe_layer(nc, 0, a, x, xT, cst, slots, y_dram, proj, sbr)
        norm(nc, "ln01", x, x, xT, ident, LN_EPS, False, a["ln_g"][0, 1], a["ln_b"][0, 1], resid=proj, alpha=ALPHA)
        first_block_rest(nc, a, x, xT, cst, mk, mv, mix, memq, proj, slots, y_dram, sbr, dram)
        second_block(nc, a, x, xT, cst, out, dram)


HC = ML_DH // 96
NC96 = ML_W // 96


def mlstm_conv(nc, a, xm_dram, z_dram, xm, xc, zs):
    with stage(nc, "conv") as st:
        cw = st.sb("cw", [96, NC96, CONV_K])
        cb = st.sb("cb", [96, NC96])
        sg = st.sb("sg", [96, NC96, S])
        ld, zld = st.sem("ld"), st.sem("zld")
        pre_ready, sig_ready, z_ready = st.sem("pre_ready"), st.sem("sig_ready"), st.sem("z_ready")
        pad = CONV_K // 2
        with nc.Block() as block:

            @block.sync
            def _(sp):
                sp.dma_start(xm[:, :, pad:pad + S], xm_dram.rearrange("(c p) t -> p c t", p=96)).then_inc(ld, 16)
                sp.dma_start(cw[:], a["ml_conv_wT"].rearrange("(c p) k -> p c k", p=96)).then_inc(ld, 16)
                sp.dma_start(cb[:], a["ml_conv_bP"]).then_inc(ld, 16)
                sp.dma_start(zs[:], z_dram.rearrange("(c p) t -> p c t", p=96)).then_inc(zld, 16)

            @block.vector
            def _(dve):
                V = nc.vector
                V.memset(xm[:, :, 0:pad], 0.0)
                V.memset(xm[:, :, pad + S:], 0.0)
                dve.wait_ge(ld, 48)
                V.drain()
                for k in range(CONV_K):
                    for c in range(NC96):
                        src = xm[:, c, k:k + S]
                        if k == 0:
                            V.tensor_scalar(xc[:, c, :], src, cw[:, c, k:k + 1], cb[:, c:c + 1], ALU.mult, ALU.add)
                        else:
                            last = V.scalar_tensor_tensor(xc[:, c, :], src, cw[:, c, k:k + 1], xc[:, c, :],
                                                          ALU.mult, ALU.add)
                    if k < CONV_K - 1:
                        V.drain()
                last.then_inc(pre_ready, 1)
                dve.wait_ge(sig_ready, 1)
                V.tensor_mul(xc[:], xc[:], sg[:])
                V.drain().then_inc(pre_ready, 1)
                dve.wait_ge(z_ready, 1)
                V.tensor_mul(zs[:], zs[:], sg[:])

            @block.scalar
            def _(act):
                act.wait_ge(pre_ready, 1)
                nc.scalar.activation(sg[:], xc[:], ACT.Sigmoid).then_inc(sig_ready, 1)
                act.wait_ge(zld, 16)
                act.wait_ge(pre_ready, 2)
                nc.scalar.activation(sg[:], zs[:], ACT.Sigmoid).then_inc(z_ready, 1)


def mlstm_gates(nc, a, xT, ident, ones, pidx, neg_m, diag_m, a_tok, e_tok):
    with stage(nc, "gates") as st:
        NH = ML_HEADS
        wg = st.sb("wg", [P, KD, 16])
        gb = st.sb("gb", [NH, 4])
        G = st.sb("G", [NH, 4, S])
        ab = st.sb("ab", [NH, S])
        buf = [st.sb(f"buf{n}", [NH, 2, S]) for n in range(2)]
        av = st.sb("av", [NH, 2, S])
        nm = st.sb("nm", [NH, 2, S])
        bv = st.sb("bv", [NH, 2, S])
        sel = st.sb("sel", [NH, NH, P])
        mask = st.sb("mask", [P, 2, P])
        zero = st.sb("zero", [P, P])
        ld, g_ready, f_ready, l_ready = st.sem("ld"), st.sem("g_ready"), st.sem("f_ready"), st.sem("l_ready")
        e_ready = st.sem("e_ready")
        rows_ready, tr_ready, bc_ready, bc_free = (st.sem("rows_ready"), st.sem("tr_ready"), st.sem("bc_ready"),
                                                   st.sem("bc_free"))
        z_ready, mask_ready = st.sem("z_ready"), st.sem("mask_ready")
        g_ps = [st.ps(f"g{n}") for n in range(4)]
        t_ps = st.ps("t")
        b_ps = [st.ps(f"b{n}") for n in range(2)]
        with nc.Block() as block:

            @block.sync
            def _(sp):
                sp.dma_start(wg[:], a["ml_w_in"][0].rearrange("(k p) n -> p k n", p=P)[:, :, 2 * ML_W:2 * ML_W + 16]) \
                    .then_inc(ld, 16)
                sp.dma_start(gb[:], a["ml_gate_bT"]).then_inc(ld, 16)

            @block.gpsimd
            def _(pool):
                nc.gpsimd.memset(zero[:], 0.0)
                nc.gpsimd.drain()
                nc.gpsimd.affine_select(out=mask[:, 0, :], in_=zero[:], pattern=[[1, P]], compare_op=ALU.is_ge,
                                        fill=NEG, base=0, channel_multiplier=-1)
                nc.gpsimd.affine_select(out=mask[:, 1, :], in_=zero[:], pattern=[[-1, P]], compare_op=ALU.is_ge,
                                        fill=NEG, base=0, channel_multiplier=1)
                nc.gpsimd.drain().then_inc(mask_ready, 1)

            @block.tensor
            def _(pe):
                pe.wait_ge(ld, 32)
                for g in range(4):
                    for k in range(KD):
                        mm = nc.tensor.matmul(g_ps[g][0:NH, :], wg[:, k, g * NH:(g + 1) * NH], xT[:, k, :],
                                              start=(k == 0), stop=(k == KD - 1))
                mm.then_inc(g_ready, 1)
                pe.wait_ge(rows_ready, 1)
                for n, src in enumerate((av, nm)):
                    for d in range(2):
                        for t in range(NT):
                            c = ((n * 2 + d) * NT + t) * NH
                            mm = nc.tensor.transpose(t_ps[:, c:c + NH], src[:, d, t * P:(t + 1) * P],
                                                     ident[0:NH, 0:NH])
                mm.then_inc(tr_ready, 1)
                pe.wait_ge(rows_ready, 2)
                for d in range(2):
                    for h in range(NH):
                        n = d * NH + h
                        pe.wait_ge(bc_free, n + 1)
                        nc.tensor.matmul(b_ps[n % 2][:], sel[:, h, :], buf[1][:, d, :], start=True, stop=True) \
                            .then_inc(bc_ready, 1)

            @block.scalar
            def _(act):
                act.wait_ge(f_ready, 1)
                for d in range(2):
                    act.wait_ge(f_ready, d + 1)
                    nc.scalar.activation(ab[:], ab[:], ACT.Exp, scale=-1.0)
                    nc.scalar.drain()
                    nc.scalar.activation(ab[:], ab[:], ACT.Ln, bias=1.0).then_inc(l_ready, 1)
                act.wait_ge(tr_ready, 1)
                n = 2 * NT * NH
                nc.scalar.activation(a_tok[:], t_ps[:, 0:n], ACT.Copy)
                nc.scalar.activation(e_tok[:], t_ps[:, n:2 * n], ACT.Exp)

            @block.vector
            def _(dve):
                V = nc.vector
                dve.sem_inc(bc_free, 2)
                for h in range(NH):
                    V.tensor_scalar(sel[:, h, :], ones[0:NH, :], pidx[0:NH, 0:1], float(h), ALU.mult, ALU.is_equal)
                dve.wait_ge(g_ready, 1)
                for g in range(4):
                    V.tensor_scalar(G[:, g, :], g_ps[g][0:NH, :], gb[:, g:g + 1], None, ALU.add)
                V.drain()
                for d in range(2):
                    f = G[:, 2 * d + 1, :]
                    V.scalar_tensor_tensor(ab[:], f, -1.0, f, ALU.mult, ALU.max)
                    V.drain().then_inc(f_ready, 1)
                    dve.wait_ge(l_ready, d + 1)
                    V.scalar_tensor_tensor(buf[0][:, d, :], f, 0.0, ab[:], ALU.min, ALU.subtract)
                    V.drain()

                def running(op, src, dst):
                    s, d_, sh = src, dst, 1
                    while sh < S:
                        o = V.tensor_add if op == "add" else V.tensor_max
                        V.tensor_copy(d_[:, 0, 0:sh], s[:, 0, 0:sh])
                        o(d_[:, 0, sh:S], s[:, 0, sh:S], s[:, 0, 0:S - sh])
                        V.tensor_copy(d_[:, 1, S - sh:S], s[:, 1, S - sh:S])
                        o(d_[:, 1, 0:S - sh], s[:, 1, 0:S - sh], s[:, 1, sh:S])
                        V.drain()
                        s, d_, sh = d_, s, sh * 2
                    return s

                res = running("add", buf[0], buf[1])
                V.tensor_copy(bv[:], res[:])
                for d in range(2):
                    V.tensor_sub(av[:, d, :], G[:, 2 * d, :], res[:, d, :])
                V.drain()
                V.tensor_scalar(buf[0][:], av[:], 0.0, None, ALU.max)
                V.drain()
                res = running("max", buf[0], buf[1])
                V.drain()
                V.scalar_tensor_tensor(nm[:], bv[:], -1.0, res[:], ALU.mult, ALU.subtract).then_inc(rows_ready, 1)
                V.drain()
                V.tensor_scalar(buf[1][:], res[:], -1.0, None, ALU.mult).then_inc(rows_ready, 1)
                dve.wait_ge(mask_ready, 1)
                for d in range(2):
                    for h in range(NH):
                        n = d * NH + h
                        dve.wait_ge(bc_ready, n + 1)
                        V.tensor_copy(neg_m[:, n, :], b_ps[n % 2][:])
                        for t in range(NT):
                            last = V.tensor_add(diag_m[:, n, t * P:(t + 1) * P], b_ps[n % 2][:, t * P:(t + 1) * P],
                                                mask[:, d, :])
                        last.then_inc(bc_free, 1)


def mlstm_qkv(nc, a, xm, xc, q, k, v):
    with stage(nc, "qkv") as st:
        NH = ML_HEADS
        w = st.sb("w", [96, 3 * NH * HC, ML_DH])
        ld, ready, free = st.sem("ld"), st.sem("ready"), st.sem("free")
        ps = [st.ps(f"ps{n}") for n in range(4)]
        pad = CONV_K // 2
        with nc.Block() as block:

            @block.sync
            def _(sp):
                sp.dma_start(w[:], a["ml_w_qkv"][0].rearrange("s h (c p) e -> p (s h c) e", p=96)).then_inc(ld, 16)

            @block.tensor
            def _(pe):
                pe.wait_ge(ld, 16)
                n = 0
                for s in range(2):
                    for h in range(NH):
                        for g in range(HC):
                            pe.wait_ge(free, n + 1)
                            for c in range(HC):
                                mm = nc.tensor.matmul(ps[n % 4][0:96, :],
                                                      w[:, (s * NH + h) * HC + c, g * 96:(g + 1) * 96],
                                                      xc[:, h * HC + c, :], start=(c == 0), stop=(c == HC - 1))
                            mm.then_inc(ready, 1)
                            n += 1
                for h in range(NH):
                    for t in range(NT):
                        pe.wait_ge(free, n + 1)
                        for c in range(HC):
                            mm = nc.tensor.matmul(ps[n % 4][:, 0:ML_DH],
                                                  xm[:, h * HC + c, pad + t * P:pad + (t + 1) * P],
                                                  w[:, (2 * NH + h) * HC + c, :], start=(c == 0), stop=(c == HC - 1))
                        mm.then_inc(ready, 1)
                        n += 1

            @block.scalar
            def _(act):
                act.sem_inc(free, 4)
                n = 0
                for dst, scale in ((q, 1.0), (k, ML_DH ** -0.5)):
                    for c in range(NH * HC):
                        act.wait_ge(ready, n + 1)
                        nc.scalar.activation(dst[:, c, :], ps[n % 4][0:96, :], ACT.Copy, scale=scale).then_inc(free, 1)
                        n += 1
                for h in range(NH):
                    for t in range(NT):
                        act.wait_ge(ready, n + 1)
                        nc.scalar.activation(v[:, t, h, 0:ML_DH], ps[n % 4][:, 0:ML_DH], ACT.Copy).then_inc(free, 1)
                        n += 1

            @block.vector
            def _(dve):
                for t in range(NT):
                    nc.vector.memset(v[:, t, :, ML_DH:ML_DH + 1], 1.0)


def mlstm_scan(nc, q, k, v, neg_m, diag_m, a_tok, e_tok, hs):
    NH = ML_HEADS
    combos = [(d, h) for d in range(2) for h in range(NH)]
    tiles = [[(s, s, NT) for s in range(NT)], [(s, 0, s + 1) for s in range(NT)]]
    units = [(n, d, h, s, lo, hi) for n, (d, h) in enumerate(combos) for (s, lo, hi) in tiles[d]]
    with stage(nc, "scan") as st:
        dec = [st.sb(f"dec{r}", [P, S]) for r in range(2)]
        wt = [st.sb(f"wt{r}", [P, S]) for r in range(2)]
        rd = st.sb("rd", [P, NT])
        rd2 = st.sb("rd2", [P, NT])
        s_ps = [st.ps(f"s{r}") for r in range(2)]
        n_ps = [st.ps(f"n{t}") for t in range(NT)]
        s_ready, dec_ready, wt_ready = st.sem("s_ready"), st.sem("dec_ready"), st.sem("wt_ready")
        wt_free, num_ready, num_free = st.sem("wt_free"), st.sem("num_ready"), st.sem("num_free")
        with nc.Block() as block:

            @block.tensor
            def _(pe):
                def scores(m):
                    n, d, h, s, lo, hi = units[m]
                    pe.wait_ge(wt_ready, m + 1)
                    for c in range(HC):
                        mm = nc.tensor.matmul(s_ps[m % 2][:, 0:(hi - lo) * P],
                                              k[:, h * HC + c, s * P:(s + 1) * P],
                                              q[:, h * HC + c, lo * P:hi * P], start=(c == 0), stop=(c == HC - 1))
                    mm.then_inc(s_ready, 1)
                scores(0)
                for m, (n, d, h, s, lo, hi) in enumerate(units):
                    if m + 1 < len(units):
                        scores(m + 1)
                    pe.wait_ge(wt_ready, m + 3)
                    if s == 0:
                        pe.wait_ge(num_free, n + 1)
                    for t in range(lo, hi):
                        first = s == 0 if d == 0 else s == t
                        last = s == t if d == 0 else s == NT - 1
                        mm = nc.tensor.matmul(n_ps[t][:, 0:ML_DH + 1], wt[m % 2][:, (t - lo) * P:(t - lo + 1) * P],
                                              v[:, s, h, :], start=first, stop=last)
                    mm.then_inc(wt_free, 1)

            @block.scalar
            def _(act):
                act.sem_inc(wt_ready, 2)
                for m, (n, d, h, s, lo, hi) in enumerate(units):
                    act.wait_ge(wt_ready, m + 1)
                    bias = a_tok[:, (d * NT + s) * NH + h:(d * NT + s) * NH + h + 1]
                    x0 = (s - lo) * P
                    last = nc.scalar.activation(dec[m % 2][:, x0:x0 + P], diag_m[:, n, s * P:(s + 1) * P], ACT.Exp,
                                                bias=bias)
                    if d == 0 and s < NT - 1:
                        last = nc.scalar.activation(dec[m % 2][:, P:(hi - lo) * P], neg_m[:, n, (s + 1) * P:S],
                                                    ACT.Exp, bias=bias)
                    if d == 1 and s > 0:
                        last = nc.scalar.activation(dec[m % 2][:, 0:s * P], neg_m[:, n, 0:s * P], ACT.Exp, bias=bias)
                    last.then_inc(dec_ready, 1)

            @block.vector
            def _(dve):
                V = nc.vector
                dve.sem_inc(wt_free, 2)
                dve.sem_inc(num_free, 1)

                def outputs(n, d, h):
                    dve.wait_ge(wt_free, NT * (n + 1) + 2)
                    for t in range(NT):
                        V.tensor_copy(rd[:, t:t + 1], n_ps[t][:, ML_DH:ML_DH + 1])
                    V.drain()
                    V.scalar_tensor_tensor(rd2[:], rd[:], -1.0, rd[:], ALU.mult, ALU.max)
                    V.drain()
                    for t in range(NT):
                        c = (d * NT + t) * NH + h
                        V.tensor_max(rd[:, t:t + 1], rd2[:, t:t + 1], e_tok[:, c:c + 1])
                    V.drain()
                    V.reciprocal(rd2[:], rd[:])
                    V.drain()
                    for t in range(NT):
                        o = hs[:, t, h * ML_DH:(h + 1) * ML_DH]
                        if d == 0:
                            last = V.tensor_scalar(o, n_ps[t][:, 0:ML_DH], rd2[:, t:t + 1], None, ALU.mult)
                        else:
                            last = V.scalar_tensor_tensor(o, n_ps[t][:, 0:ML_DH], rd2[:, t:t + 1], o,
                                                          ALU.mult, ALU.add)
                    last.then_inc(num_free, 1)
                    V.drain()

                for m, (n, d, h, s, lo, hi) in enumerate(units):
                    dve.wait_ge(s_ready, m + 1)
                    dve.wait_ge(dec_ready, m + 1)
                    dve.wait_ge(wt_free, m + 1)
                    V.tensor_mul(wt[m % 2][:, 0:(hi - lo) * P], s_ps[m % 2][:, 0:(hi - lo) * P],
                                 dec[m % 2][:, 0:(hi - lo) * P]).then_inc(wt_ready, 1)
                    if s == NT - 1:
                        outputs(n, d, h)


def mlstm_output(nc, a, ident, hs, xc, zs, mixT_dram):
    NH = ML_HEADS
    with stage(nc, "mlout") as st:
        stats = st.sb("stats", [P, NT * NH, 6])
        mv = st.sb("mv", [P, NT * NH, 2])
        rstd = st.sb("rstd", [P, NT * NH])
        sq = st.sb("sq", [P, NT * NH])
        ng, sk = st.sb("ng", [96, NC96]), st.sb("sk", [96, NC96])
        ld, var_ready, sqrt_ready, h_ready = st.sem("ld"), st.sem("var_ready"), st.sem("sqrt_ready"), st.sem("h_ready")
        t_ready, t_free, y_ready, stored = st.sem("t_ready"), st.sem("t_free"), st.sem("y_ready"), st.sem("stored")
        ps = [st.ps(f"ps{n}") for n in range(4)]
        with nc.Block() as block:

            @block.sync
            def _(sp):
                sp.dma_start(ng[:], a["ml_norm_gP"]).then_inc(ld, 16)
                sp.dma_start(sk[:], a["ml_skipP"]).then_inc(ld, 16)
                sp.wait_ge(y_ready, 1)
                sp.dma_start(mixT_dram.rearrange("(c p) t -> p c t", p=96), xc[:]).then_inc(stored, 16)
                sp.wait_ge(stored, 16)

            @block.scalar
            def _(act):
                act.wait_ge(var_ready, 1)
                nc.scalar.activation(sq[:], sq[:], ACT.Sqrt).then_inc(sqrt_ready, 1)

            @block.vector
            def _(dve):
                V = nc.vector
                dve.sem_inc(t_free, 4)
                for t in range(NT):
                    for h in range(NH):
                        V.bn_stats(stats[:, t * NH + h, :], hs[:, t, h * ML_DH:(h + 1) * ML_DH])
                V.drain()
                for g in range(NT * NH):
                    V.bn_aggr(mv[:, g, :], stats[:, g, :])
                V.drain()
                V.tensor_scalar(sq[:], mv[:, :, 1], LN_EPS, None, ALU.add).then_inc(var_ready, 1)
                dve.wait_ge(sqrt_ready, 1)
                V.reciprocal(rstd[:], sq[:])
                V.drain()
                for t in range(NT):
                    for h in range(NH):
                        g, o = t * NH + h, hs[:, t, h * ML_DH:(h + 1) * ML_DH]
                        last = V.tensor_scalar(o, o, mv[:, g, 0:1], rstd[:, g:g + 1], ALU.subtract, ALU.mult)
                last.then_inc(h_ready, 1)
                dve.wait_ge(ld, 32)
                for c in range(NC96):
                    V.tensor_scalar(xc[:, c, :], xc[:, c, :], sk[:, c:c + 1], None, ALU.mult)
                V.drain()
                for c in range(NC96):
                    dve.wait_ge(t_ready, c + 1)
                    V.scalar_tensor_tensor(xc[:, c, :], ps[c % 4][0:96, :], ng[:, c:c + 1], xc[:, c, :],
                                           ALU.mult, ALU.add).then_inc(t_free, 1)
                V.drain()
                V.tensor_mul(xc[:], xc[:], zs[:]).then_inc(y_ready, 1)

            @block.tensor
            def _(pe):
                pe.wait_ge(h_ready, 1)
                for c in range(NC96):
                    pe.wait_ge(t_free, c + 1)
                    for t in range(NT):
                        mm = nc.tensor.transpose(ps[c % 4][0:96, t * P:(t + 1) * P],
                                                 hs[:, t, c * 96:(c + 1) * 96], ident[:])
                    mm.then_inc(t_ready, 1)


def reload_chunks(nc, name, dstT, n, src):
    with stage(nc, name) as st:
        s = st.sem("loaded")
        with nc.Block() as block:

            @block.sync
            def _(sp):
                sp.dma_start(dstT[:, 0:n, :], src.rearrange("(c p) t -> p c t", p=P)).then_inc(s, 16)
                sp.wait_ge(s, 16)


def mlstm_mixer(nc, a, x, xT, cst, mk, mv, mix, memq, dram):
    ident, strict, ones, iota, pidx = cst
    win = a["ml_w_in"][0]
    xm_d, z_d, mixT_d = dram("ml_xm", [ML_W, S]), dram("ml_z", [ML_W, S]), dram("ml_mixT", [ML_W, S])
    gemm(nc, "ml_x", win, 0, 2, 384, xT, P, S, xm_d, "T", M=96)
    gemm(nc, "ml_z", win, ML_W, 2, 384, xT, P, S, z_d, "T", M=96)
    gemm(nc, "ml_m", win, 2 * ML_W + 16, 1, MEM_W, xT, P, S, memq, "T")
    memory_attention(nc, "mem1", ident, memq, mk, mv, mix)
    with ExitStack() as ctx:
        def sb(name, shape):
            return ctx.enter_context(nc.sbuf_tensor("ml_" + name, shape, F32))
        xc, zs = sb("xc", [96, NC96, S]), sb("zs", [96, NC96, S])
        hs = sb("hs", [P, NT, ML_W])
        with ExitStack() as inner:
            def si(name, shape):
                return inner.enter_context(nc.sbuf_tensor("mli_" + name, shape, F32))
            neg_m, diag_m = si("neg_m", [P, 8, S]), si("diag_m", [P, 8, S])
            a_tok, e_tok = si("a_tok", [P, 2 * NT * 4]), si("e_tok", [P, 2 * NT * 4])
            v = si("v", [P, NT, ML_HEADS, ML_DH + 1])
            mlstm_gates(nc, a, xT, ident, ones, pidx, neg_m, diag_m, a_tok, e_tok)
            q, k = si("q", [96, NC96, S]), si("k", [96, NC96, S])
            with nc.sbuf_tensor("ml_xm_s", [96, NC96, S + CONV_K - 1], F32) as xm:
                mlstm_conv(nc, a, xm_d, z_d, xm, xc, zs)
                mlstm_qkv(nc, a, xm, xc, q, k, v)
            mlstm_scan(nc, q, k, v, neg_m, diag_m, a_tok, e_tok, hs)
        mlstm_output(nc, a, ident, hs, xc, zs, mixT_d)
    load_transposed(nc, "mixT1", mix, xT, ident)
    reload_chunks(nc, "mixT1b", xT, ML_W // P, mixT_d)


def first_block_rest(nc, a, x, xT, cst, mk, mv, mix, memq, proj, slots, y_dram, sbr, dram):
    ident = cst[0]
    mlstm_mixer(nc, a, x, xT, cst, mk, mv, mix, memq, dram)
    gemm(nc, "out1", a["w_out"][1], 0, 2, 512, xT, P, S, proj, "N")
    norm(nc, "ln10", x, x, xT, ident, LN_EPS, False, a["ln_g"][1, 0], a["ln_b"][1, 0], resid=proj, alpha=ALPHA)
    moe_layer(nc, 1, a, x, xT, cst, slots, y_dram, proj, sbr)
    norm(nc, "ln11", x, x, xT, ident, LN_EPS, False, a["ln_g"][1, 1], a["ln_b"][1, 1], resid=proj, alpha=ALPHA)


def bias_parts():
    return [(0, 0), (0, 512), (1, 0), (2, 0)]


def condition(nc, a, condT):
    with stage(nc, "cond") as st:
        sg = st.sb("sg", [P, KD])
        ld, ready, sig = st.sem("ld"), st.sem("ready"), st.sem("sig")
        with nc.Block() as block:

            @block.sync
            def _(sp):
                sp.dma_start(condT[:], a["c_P"]).then_inc(ld, 16)

            @block.scalar
            def _(act):
                act.wait_ge(ld, 16)
                nc.scalar.activation(sg[:], condT[:], ACT.Sigmoid).then_inc(sig, 1)

            @block.vector
            def _(dve):
                dve.wait_ge(sig, 1)
                nc.vector.tensor_mul(condT[:], condT[:], sg[:])


def add_rows(nc, name, src, vec, dst, parts):
    n = vec.shape[0] // parts
    with stage(nc, name) as st:
        t, v = st.sb("t", [parts, n]), st.sb("v", [parts, n])
        ld, ready, stored = st.sem("ld"), st.sem("ready"), st.sem("stored")
        fold = lambda ap: ap.rearrange("(p n) -> p n", p=parts)
        with nc.Block() as block:

            @block.sync
            def _(sp):
                sp.dma_start(t[:], fold(src)).then_inc(ld, 16)
                sp.dma_start(v[:], fold(vec)).then_inc(ld, 16)
                sp.wait_ge(ready, 1)
                sp.dma_start(fold(dst), t[:]).then_inc(stored, 16)
                sp.wait_ge(stored, 16)

            @block.vector
            def _(dve):
                dve.wait_ge(ld, 32)
                nc.vector.tensor_add(t[:], t[:], v[:]).then_inc(ready, 1)


def latents(nc, a, ident, lat, cqT, ckvT, kp):
    QT, KT_ = Q_RANK // P, KV_RANK // P
    HR = ROPE // 2
    with stage(nc, "lat") as st:
        x = st.sb("x", [P, NT, Q_RANK + KV_RANK + ROPE])
        stats = st.sb("stats", [P, NT, 2, 6])
        mv = st.sb("mv", [P, NT * 2, 2])
        sq, rs = st.sb("sq", [P, NT * 2]), st.sb("rs", [P, NT * 2])
        gq, gk = st.sb("gq", [P, QT]), st.sb("gk", [P, KT_])
        ld, var_ready, sqrt_ready, x_ready = st.sem("ld"), st.sem("var_ready"), st.sem("sqrt_ready"), st.sem("x_ready")
        t_ready, t_free = st.sem("t_ready"), st.sem("t_free")
        ps = [st.ps(f"ps{n}") for n in range(4)]
        cuts = [(c * P, P, cqT[:, c, :], gq[:, c:c + 1]) for c in range(QT)]
        cuts += [(Q_RANK + c * P, P, ckvT[:, c, :], gk[:, c:c + 1]) for c in range(KT_)]
        cuts += [(Q_RANK + KV_RANK + c * HR, HR, kp[c][:], None) for c in range(2)]
        with nc.Block() as block:

            @block.sync
            def _(sp):
                sp.dma_start(x[:], lat.rearrange("(t p) f -> p t f", p=P)).then_inc(ld, 16)
                sp.dma_start(gq[:], a["g_q_lat_P"]).then_inc(ld, 16)
                sp.dma_start(gk[:], a["g_kv_lat_P"]).then_inc(ld, 16)

            @block.vector
            def _(dve):
                V = nc.vector
                dve.wait_ge(ld, 48)
                rng = [(0, Q_RANK), (Q_RANK, Q_RANK + KV_RANK)]
                for t in range(NT):
                    for n, (lo, hi) in enumerate(rng):
                        V.bn_stats(stats[:, t, n, :], x[:, t, lo:hi])
                V.drain()
                for t in range(NT):
                    for n in range(2):
                        V.bn_aggr(mv[:, t * 2 + n, :], stats[:, t, n, :])
                V.drain()
                V.tensor_mul(sq[:], mv[:, :, 0], mv[:, :, 0])
                V.drain()
                V.scalar_tensor_tensor(sq[:], mv[:, :, 1], EPS2, sq[:], ALU.add, ALU.add).then_inc(var_ready, 1)
                dve.wait_ge(sqrt_ready, 1)
                V.reciprocal(rs[:], sq[:])
                V.drain()
                for t in range(NT):
                    for n, (lo, hi) in enumerate(rng):
                        last = V.tensor_scalar(x[:, t, lo:hi], x[:, t, lo:hi], rs[:, t * 2 + n:t * 2 + n + 1], None,
                                               ALU.mult)
                last.then_inc(x_ready, 1)

            @block.tensor
            def _(pe):
                pe.wait_ge(x_ready, 1)
                for n, (lo, wd, dst, g) in enumerate(cuts):
                    pe.wait_ge(t_free, n + 1)
                    for t in range(NT):
                        mm = nc.tensor.transpose(ps[n % 4][0:wd, t * P:(t + 1) * P], x[:, t, lo:lo + wd], ident[:])
                    mm.then_inc(t_ready, 1)

            @block.scalar
            def _(act):
                act.sem_inc(t_free, 4)
                act.wait_ge(var_ready, 1)
                nc.scalar.activation(sq[:], sq[:], ACT.Sqrt).then_inc(sqrt_ready, 1)
                for n, (lo, wd, dst, g) in enumerate(cuts):
                    act.wait_ge(t_ready, n + 1)
                    nc.scalar.activation(dst, ps[n % 4][0:wd, :], ACT.Copy, scale=1.0 if g is None else g) \
                        .then_inc(t_free, 1)


TWO_PI_1 = 6.28125
TWO_PI_2 = 2029.0 / 2 ** 20
TWO_PI_3 = 2 * math.pi - TWO_PI_1 - TWO_PI_2
ROUND = 1.5 * 2 ** 23


def rotary(nc, a, q_all, kp, qpe, kpe):
    H4 = MLA_H // 4
    lim = 3.1415925
    with stage(nc, "rope") as st:
        pi = st.sb("pi", [P, S], I32)
        fr = st.sb("fr", [P, 1])
        ang, kk, cs, sn, gt = (st.sb(n, [P, S]) for n in ("ang", "kk", "cs", "sn", "gt"))
        t1, t2 = st.sb("t1", [P, H4, S]), st.sb("t2", [P, H4, S])
        o1, o2, tm = st.sb("o1", [P, H4, S]), st.sb("o2", [P, H4, S]), st.sb("tm", [P, S])
        k1, k2 = st.sb("k1", [32, S]), st.sb("k2", [32, S])
        ld, ang_ready, trig, done, stored = (st.sem("ld"), st.sem("ang_ready"), st.sem("trig"), st.sem("done"),
                                             st.sem("stored"))
        with nc.Block() as block:

            @block.sync
            def _(sp):
                sp.dma_start(pi[:], bcast_rows(a["positions_2"][0])).then_inc(ld, 16)
                sp.dma_start(fr[:], a["inv_freq"]).then_inc(ld, 16)
                nope = MLA_H * NOPE
                sp.dma_start(t1[:], q_all[nope:nope + 256, :].rearrange("(a p) t -> p a t", p=P)).then_inc(ld, 16)
                sp.dma_start(t2[:], q_all[nope + 256:nope + 512, :].rearrange("(a p) t -> p a t", p=P)).then_inc(ld, 16)
                sp.wait_ge(done, 1)
                qv = qpe.rearrange("(h c p) t -> h c p t", c=2, p=32)
                for hh in range(H4):
                    sp.dma_start(qv[4 * hh:4 * hh + 4, 0], o1[:, hh, :]).then_inc(stored, 16)
                    sp.dma_start(qv[4 * hh:4 * hh + 4, 1], o2[:, hh, :]).then_inc(stored, 16)
                sp.dma_start(kpe[0:32, :], k1[:]).then_inc(stored, 16)
                sp.dma_start(kpe[32:64, :], k2[:]).then_inc(stored, 16)
                sp.wait_ge(stored, 16 * (2 * H4 + 2))

            @block.vector
            def _(dve):
                V = nc.vector
                dve.wait_ge(ld, 64)
                V.tensor_copy(ang[:], pi[:])
                V.drain()
                V.tensor_scalar(ang[:], ang[:], fr[:, 0:1], None, ALU.mult)
                V.drain()
                V.tensor_scalar(kk[:], ang[:], 1.0 / (2 * math.pi), None, ALU.mult)
                V.drain()
                V.tensor_scalar(kk[:], kk[:], ROUND, None, ALU.add)
                V.drain()
                V.tensor_scalar(kk[:], kk[:], ROUND, None, ALU.subtract)
                for part in (TWO_PI_1, TWO_PI_2, TWO_PI_3):
                    V.drain()
                    V.scalar_tensor_tensor(ang[:], kk[:], -part, ang[:], ALU.mult, ALU.add)
                V.drain()
                V.tensor_scalar(cs[:], ang[:], math.pi / 2, None, ALU.add)
                V.drain()
                V.tensor_scalar(gt[:], cs[:], math.pi, -2 * math.pi, ALU.is_gt, ALU.mult)
                V.drain()
                V.tensor_add(cs[:], cs[:], gt[:])
                V.tensor_scalar(ang[:], ang[:], lim, -lim, ALU.min, ALU.max)
                V.drain()
                V.tensor_scalar(cs[:], cs[:], lim, -lim, ALU.min, ALU.max).then_inc(ang_ready, 1)
                dve.wait_ge(trig, 1)
                for hh in range(H4):
                    V.tensor_mul(o1[:, hh, :], t1[:, hh, :], cs[:])
                    V.tensor_mul(o2[:, hh, :], t1[:, hh, :], sn[:])
                    V.tensor_mul(tm[:], t2[:, hh, :], sn[:])
                    V.tensor_mul(gt[:], t2[:, hh, :], cs[:])
                    V.drain()
                    V.tensor_sub(o1[:, hh, :], o1[:, hh, :], tm[:])
                    V.tensor_add(o2[:, hh, :], o2[:, hh, :], gt[:])
                    V.drain()
                V.tensor_mul(k1[:], kp[0][:], cs[0:32, :])
                V.tensor_mul(k2[:], kp[0][:], sn[0:32, :])
                V.tensor_mul(tm[0:32, :], kp[1][:], sn[0:32, :])
                V.tensor_mul(gt[0:32, :], kp[1][:], cs[0:32, :])
                V.drain()
                V.tensor_sub(k1[:], k1[:], tm[0:32, :])
                V.tensor_add(k2[:], k2[:], gt[0:32, :])
                V.drain().then_inc(done, 1)

            @block.scalar
            def _(act):
                act.wait_ge(ang_ready, 1)
                nc.scalar.activation(cs[:], cs[:], ACT.Sin)
                nc.scalar.activation(sn[:], ang[:], ACT.Sin).then_inc(trig, 1)


G0_START = [min(max(u * P - 64, 0), S - 2 * P) for u in range(4)]
STEPS = list(range(1, 9)) + [math.ceil(8 * 128 ** (j / 8)) for j in range(1, 8)]


def relative_bias(nc, a, biases):
    parts = bias_parts()
    widths = (4 * 256, 4 * P, 4 * P)
    with stage(nc, "rel") as st:
        pki = st.sb("pki", [P, S], I32)
        pk = st.sb("pk", [P, S])
        pqi = st.sb("pqi", [P, 12], I32)
        pq = st.sb("pq", [P, 12])
        tab = st.sb("tab", [P, 3 * N_REL * DIL_H])
        bucket, rel = st.sb("bucket", [P, 512]), st.sb("rel", [P, 512])
        hit = [st.sb(f"hit{r}", [P, 512]) for r in range(2)]
        mask = st.sb("mask", [P, 2048])
        acc = st.sb("acc", [P, DIL_H, 512])
        rowt = [st.sb(f"rowt{r}", [P, DIL_H]) for r in range(2)]
        cnt = st.sb("cnt", [P, 1])
        ld, ready, stored = st.sem("ld"), st.sem("ready"), st.sem("stored")
        with nc.Block() as block:

            @block.sync
            def _(sp):
                sp.dma_start(pki[:], bcast_rows(a["positions_2"][0])).then_inc(ld, 16)
                sp.dma_start(pqi[:], a["pos_q"]).then_inc(ld, 16)
                sp.dma_start(tab[:], bcast_rows(a["rel_tab"])).then_inc(ld, 16)
                sp.dma_start(mask[:], a["band_mask"]).then_inc(ld, 16)
                for n, (g, c0) in enumerate(parts):
                    sp.wait_ge(ready, n + 1)
                    sp.dma_start(biases[g].rearrange("h p n -> p h n")[:, :, c0:c0 + 512], acc[:]).then_inc(stored, 16)
                sp.wait_ge(stored, 16 * len(parts))

            @block.vector
            def _(dve):
                V = nc.vector
                dve.wait_ge(ld, 64)
                V.tensor_copy(pk[:], pki[:])
                V.tensor_copy(pq[:], pqi[:])
                V.drain()
                for n, (g, c0) in enumerate(parts):
                    us = [(c0 // 256 + i, i * 256, 256) for i in range(2)] if g == 0 else \
                        [(u, u * P, P) for u in range(4)]
                    for u, col, wd in us:
                        if g == 0:
                            src, dst = pk[:, G0_START[u]:G0_START[u] + 256], rel[:, col:col + wd]
                        elif g == 1:
                            src, dst = pk[:].rearrange("p (i c) -> p c i", c=4)[:, u, :], rel[:, col:col + wd]
                        else:
                            src = pk[:].rearrange("p (i c) -> p c i", c=16)[:, 4 * u:4 * u + 4, :]
                            dst = rel[:, col:col + wd].rearrange("p (c i) -> p c i", c=4)
                        V.tensor_scalar(dst, src, pq[:, g * 4 + u:g * 4 + u + 1], None, ALU.subtract)
                    V.drain()
                    V.tensor_scalar(bucket[:], rel[:], 0.0, float(N_REL // 2), ALU.is_gt, ALU.mult)
                    V.scalar_tensor_tensor(rel[:], rel[:], -1.0, rel[:], ALU.mult, ALU.max)
                    V.drain()
                    for s in STEPS:
                        V.scalar_tensor_tensor(bucket[:], rel[:], float(s), bucket[:], ALU.is_ge, ALU.add)
                        V.drain()
                    if n:
                        dve.wait_ge(stored, 16 * n)
                    m0 = (0, 512, 1024, 1536)[n]
                    for h in range(DIL_H):
                        V.tensor_copy(acc[:, h, :], mask[:, m0:m0 + 512])
                    V.memset(cnt[:], 0.0)
                    V.drain()
                    with dve.Fori(0, N_REL // 2) as i:
                        for r in range(2):
                            b = 2 * i + r
                            row = tab[:, ds(b * DIL_H + g * N_REL * DIL_H, DIL_H)]
                            V.tensor_copy(rowt[r][:], row)
                            V.tensor_scalar(hit[r][:], bucket[:], cnt[:, 0:1], None, ALU.is_equal)
                            V.drain()
                            for h in range(DIL_H):
                                V.scalar_tensor_tensor(acc[:, h, :], hit[r][:], rowt[r][:, h:h + 1], acc[:, h, :],
                                                       ALU.mult, ALU.add)
                            V.tensor_scalar(cnt[:], cnt[:], 1.0, None, ALU.add)
                            V.drain()
                    V.drain().then_inc(ready, 1)


def dilated_views(g):
    if g == 0:
        return None, lambda m, u: m[u * P:(u + 1) * P, :]
    if g == 1:
        return (lambda ap: ap.rearrange("p (i c) -> p c i", c=4),
                lambda m, u: m.rearrange("(i c) f -> c i f", c=4)[u])
    return (lambda ap: ap.rearrange("p (i c) -> p c i", c=16),
            lambda m, u: m.rearrange("(i c) f -> c i f", c=16)[4 * u:4 * u + 4])


def dilated(nc, a, ident, xT, g, win, col0, bias, o_dram, stat_dram, dram):
    cols, rows = dilated_views(g)
    qk, v = dram(f"dqk{g}", [2 * D, S]), dram(f"dv{g}", [S, D])
    gemm(nc, f"dqk{g}", win, col0, 4, 512, xT, P, S, qk, "T", tok=cols)
    gemm(nc, f"dv{g}", win, col0 + 2 * D, 2, 512, xT, P, S, v, "N")
    full = slice(None)
    hs = lambda h: ds(h * P, P)
    if g == 0:
        nk, chunks = 256, 8
        v_src = lambda h: [((full, 2 * u + c, full), v[G0_START[u] + c * P:G0_START[u] + (c + 1) * P, hs(h)])
                           for u in range(4) for c in range(2)]
        k_at = lambda k, u: k[:, G0_START[u]:G0_START[u] + 256]
        v_at = lambda u: (2 * u, 2 * u + 1)
    else:
        nk, chunks = P, 4
        sub = (lambda ap, h: ap[:, hs(h)]) if g == 1 else (lambda ap, h: ap[:, :, hs(h)])
        v_src = lambda h: [((full, u, full), sub(rows(v, u), h)) for u in range(4)]
        k_at = lambda k, u: k[:, u * P:(u + 1) * P]
        v_at = lambda u: (u,)

    def out(h, u):
        r = rows(o_dram, u)
        return r[:, :, hs(h)] if g == 2 else r[:, hs(h)]
    attention(nc, f"dil{g}", ident, DIL_H, P, P, nk,
              lambda h: [qk[hs(h), :]], lambda h: [qk[ds(h * P + D, P), :]], v_src,
              lambda q, u: q[:, u * P:(u + 1) * P], k_at, v_at, out, P ** -0.5,
              bias_src=lambda h: bias.rearrange("h p n -> p h n")[:, ds(h, 1), :], v_chunks=chunks,
              stats_out=lambda u: rows(stat_dram, u))


def merge(nc, oa, ogs, stats_d, gates, xT, ident):
    H = DIL_H
    with stage(nc, "merge") as st:
        o = [[st.sb(f"o{n}{t}", [P, D]) for t in range(NT)] for n in range(4)]
        gt = [st.sb(f"g{t}", [P, 2 * D]) for t in range(NT)]
        sd = st.sb("sd", [P, NT, 3, H, 2])
        lse = st.sb("lse", [P, NT, 3, H])
        mx, sm = st.sb("mx", [P, NT, H]), st.sb("sm", [P, NT, H])
        ld, sld = [st.sem(f"ld{t}") for t in range(NT)], st.sem("sld")
        ln_ready, l_ready, e_ready, g_ready = st.sem("ln_ready"), st.sem("l_ready"), st.sem("e_ready"), st.sem("g_ready")
        y_ready, t_ready, t_free = st.sem("y_ready"), st.sem("t_ready"), st.sem("t_free")
        ps = [st.ps(f"ps{n}") for n in range(4)]
        with nc.Block() as block:

            @block.sync
            def _(sp):
                for g in range(3):
                    for t in range(NT):
                        sp.dma_start(sd[:, t, g].rearrange("p h s -> p (h s)"), stats_d[g][t * P:(t + 1) * P, :]) \
                            .then_inc(sld, 16)
                for t in range(NT):
                    for n, src in enumerate([oa] + ogs):
                        sp.dma_start(o[n][t][:], src[t * P:(t + 1) * P, :]).then_inc(ld[t], 16)
                    sp.dma_start(gt[t][:], gates[t * P:(t + 1) * P, :]).then_inc(ld[t], 16)

            @block.scalar
            def _(act):
                act.sem_inc(t_free, 4)
                act.wait_ge(sld, 16 * 3 * NT)
                nc.scalar.activation(lse[:].rearrange("p t g h -> p (t g h)"),
                                     sd[:].rearrange("p t g h s -> p (t g h) s")[:, :, 1], ACT.Ln).then_inc(ln_ready, 1)
                act.wait_ge(l_ready, 1)
                nc.scalar.activation(lse[:], lse[:], ACT.Exp).then_inc(e_ready, 1)
                for t in range(NT):
                    act.wait_ge(ld[t], 16 * 5)
                    nc.scalar.activation(gt[t][:], gt[t][:], ACT.Sigmoid).then_inc(g_ready, 1)
                for c in range(KD):
                    act.wait_ge(t_ready, c + 1)
                    nc.scalar.activation(xT[:, c, :], ps[c % 4][:], ACT.Copy).then_inc(t_free, 1)

            @block.vector
            def _(dve):
                V = nc.vector
                dve.wait_ge(ln_ready, 1)
                f = lse[:].rearrange("p t g h -> p (t g h)")
                V.tensor_sub(f, f, sd[:].rearrange("p t g h s -> p (t g h) s")[:, :, 0])
                V.drain()
                V.tensor_max(mx[:], lse[:, :, 0], lse[:, :, 1])
                V.drain()
                V.tensor_max(mx[:], mx[:], lse[:, :, 2])
                V.drain()
                for g in range(3):
                    last = V.tensor_sub(lse[:, :, g], lse[:, :, g], mx[:])
                last.then_inc(l_ready, 1)
                dve.wait_ge(e_ready, 1)
                V.tensor_add(sm[:], lse[:, :, 0], lse[:, :, 1])
                V.drain()
                V.tensor_add(sm[:], sm[:], lse[:, :, 2])
                V.drain()
                V.reciprocal(sm[:], sm[:])
                V.drain()
                for g in range(3):
                    V.tensor_mul(lse[:, :, g], lse[:, :, g], sm[:])
                V.drain()
                for t in range(NT):
                    dve.wait_ge(ld[t], 16 * 5)
                    for g in range(3):
                        for h in range(H):
                            cut = slice(h * P, (h + 1) * P)
                            w = lse[:, t, g, h:h + 1]
                            if g == 0:
                                V.tensor_scalar(o[1][t][:, cut], o[1][t][:, cut], w, None, ALU.mult)
                            else:
                                V.scalar_tensor_tensor(o[1][t][:, cut], o[1 + g][t][:, cut], w, o[1][t][:, cut],
                                                       ALU.mult, ALU.add)
                        V.drain()
                    dve.wait_ge(g_ready, t + 1)
                    V.tensor_mul(o[0][t][:], o[0][t][:], gt[t][:, 0:D])
                    V.tensor_mul(o[1][t][:], o[1][t][:], gt[t][:, D:])
                    V.drain()
                    V.tensor_add(o[0][t][:], o[0][t][:], o[1][t][:]).then_inc(y_ready, 1)

            @block.tensor
            def _(pe):
                pe.wait_ge(y_ready, NT)
                for c in range(KD):
                    pe.wait_ge(t_free, c + 1)
                    for t in range(NT):
                        mm = nc.tensor.transpose(ps[c % 4][:, t * P:(t + 1) * P], o[0][t][:, c * P:(c + 1) * P], ident[:])
                    mm.then_inc(t_ready, 1)


def ec_route(nc, a, xT, ident, ones, pidx, affT_d, aff, rank, comb):
    E = N_EXP
    with stage(nc, "ecr") as st:
        rw = st.sb("rw", [P, KD, E])
        bc = st.sb("bc", [P, E, S])
        earlier = st.sb("earlier", [P, NT, S])
        junk = [st.sb(f"junk{r}", [P, S]) for r in range(8)]
        mx, sm = st.sb("mx", [P, NT]), st.sb("sm", [P, NT])
        gtc, tie = st.sb("gtc", [P, NT, E]), st.sb("tie", [P, NT, E])
        aT, rT = st.sb("aT", [E, S]), st.sb("rT", [E, S])
        pairsel = st.sb("pairsel", [E, E // 2, P])
        p64 = st.sb("p64", [P, 2])
        ab = [st.sb(f"ab{r}", [P, S]) for r in range(2)]
        ld, lg_ready, x_ready, e_ready, a_ready = (st.sem("ld"), st.sem("lg_ready"), st.sem("x_ready"),
                                                   st.sem("e_ready"), st.sem("a_ready"))
        at_ready, at_copied, at_stored, bc_in, r_ready = (st.sem("at_ready"), st.sem("at_copied"),
                                                          st.sem("at_stored"), st.sem("bc_in"), st.sem("r_ready"))
        rt_ready, rt_copied = st.sem("rt_ready"), st.sem("rt_copied")
        sel_ready, m_ready = st.sem("sel_ready"), st.sem("m_ready")
        pr_ready, ab_ready, comb_done = st.sem("pr_ready"), st.sem("ab_ready"), st.sem("comb_done")
        lg, tp = st.ps("lg"), st.ps("tp")
        rb = [st.ps(f"rb{r}") for r in range(2)]
        abp = [st.ps(f"abp{r}") for r in range(2)]
        with nc.Block() as block:

            @block.sync
            def _(sp):
                sp.dma_start(rw[:], a["w_router_2"][0].rearrange("(k p) e -> p k e", p=P)).then_inc(ld, 16)
                sp.wait_ge(at_copied, 1)
                sp.dma_start(affT_d.rearrange("(e t) -> e t", e=E), aT[:]).then_inc(at_stored, 16)
                sp.wait_ge(at_stored, 16)
                sp.dma_start(bc[:].rearrange("p e t -> p (e t)"), bcast_rows(affT_d)).then_inc(bc_in, 16)

            @block.gpsimd
            def _(pool):
                nc.gpsimd.memset(earlier[:], 1.0)
                nc.gpsimd.memset(pairsel[:], 1.0)
                nc.gpsimd.drain()
                for t in range(NT):
                    nc.gpsimd.affine_select(out=earlier[:, t, :], in_=earlier[:, t, :], pattern=[[-1, S]],
                                            compare_op=ALU.is_gt, fill=0.0, base=t * P, channel_multiplier=1)
                nc.gpsimd.drain().then_inc(m_ready, 1)
                for h in range(2):
                    v = pairsel[:, :, h * 64:(h + 1) * 64]
                    nc.gpsimd.affine_select(out=v, in_=v, pattern=[[-2, E // 2], [0, 64]], compare_op=ALU.is_equal,
                                            fill=0.0, base=-h, channel_multiplier=1)
                nc.gpsimd.drain().then_inc(sel_ready, 1)

            @block.tensor
            def _(pe):
                pe.wait_ge(ld, 16)
                for t in range(NT):
                    for k in range(KD):
                        mm = nc.tensor.matmul(lg[:, t * E:(t + 1) * E], xT[:, k, t * P:(t + 1) * P], rw[:, k, :],
                                              start=(k == 0), stop=(k == KD - 1))
                mm.then_inc(lg_ready, 1)
                pe.wait_ge(a_ready, 1)
                for t in range(NT):
                    mm = nc.tensor.transpose(tp[0:E, t * P:(t + 1) * P], aff[:, t, :], ident[:])
                mm.then_inc(at_ready, 1)
                pe.wait_ge(r_ready, 1)
                pe.wait_ge(at_copied, 1)
                for t in range(NT):
                    mm = nc.tensor.transpose(tp[0:E, t * P:(t + 1) * P], rank[:, t, :], ident[:])
                mm.then_inc(rt_ready, 1)
                pe.wait_ge(rt_copied, 1)
                pe.wait_ge(sel_ready, 1)
                for n in range(E // 2):
                    if n >= 2:
                        pe.wait_ge(comb_done, n - 1)
                    nc.tensor.matmul(abp[n % 2][:], pairsel[:, n, :], aT[:], start=True, stop=True)
                    nc.tensor.matmul(rb[n % 2][:], pairsel[:, n, :], rT[:], start=True, stop=True).then_inc(pr_ready, 1)

            @block.scalar
            def _(act):
                act.wait_ge(x_ready, 1)
                nc.scalar.activation(aff[:], aff[:], ACT.Exp).then_inc(e_ready, 1)
                act.wait_ge(at_ready, 1)
                nc.scalar.activation(aT[:], tp[0:E, :], ACT.Copy).then_inc(at_copied, 1)
                act.wait_ge(rt_ready, 1)
                nc.scalar.activation(rT[:], tp[0:E, :], ACT.Copy).then_inc(rt_copied, 1)
                for n in range(E // 2):
                    if n >= 2:
                        act.wait_ge(comb_done, n - 1)
                    act.wait_ge(pr_ready, n + 1)
                    nc.scalar.activation(ab[n % 2][:], abp[n % 2][:], ACT.Copy).then_inc(ab_ready, 1)

            @block.vector
            def _(dve):
                V = nc.vector
                V.tensor_scalar(p64[:, 1:2], pidx[:, 0:1], 64.0, -64.0, ALU.is_ge, ALU.mult)
                V.drain()
                V.tensor_add(p64[:, 0:1], p64[:, 1:2], pidx[:, 0:1])
                dve.wait_ge(lg_ready, 1)
                lg3 = lg[:, 0:NT * E].rearrange("p (t e) -> p t e", e=E)
                V.tensor_reduce(mx[:], lg3, AX.X, ALU.max)
                V.drain()
                for t in range(NT):
                    last = V.tensor_scalar(aff[:, t, :], lg3[:, t, :], mx[:, t:t + 1], None, ALU.subtract)
                last.then_inc(x_ready, 1)
                dve.wait_ge(e_ready, 1)
                V.tensor_reduce(sm[:], aff[:], AX.X, ALU.add)
                V.drain()
                V.reciprocal(sm[:], sm[:])
                V.drain()
                for t in range(NT):
                    last = V.tensor_scalar(aff[:, t, :], aff[:, t, :], sm[:, t:t + 1], None, ALU.mult)
                last.then_inc(a_ready, 1)
                dve.wait_ge(bc_in, 16)
                dve.wait_ge(m_ready, 1)
                for t in range(NT):
                    for e in range(E):
                        if e % 4 == 0:
                            V.drain()
                        V.tensor_scalar(junk[2 * (e % 4)][:], bc[:, e, :], aff[:, t, e:e + 1], 0.0, ALU.is_gt, ALU.add,
                                        accum_out=gtc[:, t, e:e + 1])
                        V.scalar_tensor_tensor(junk[2 * (e % 4) + 1][:], bc[:, e, :], aff[:, t, e:e + 1], earlier[:, t, :],
                                               ALU.is_equal, ALU.mult, accum_out=tie[:, t, e:e + 1])
                V.drain()
                V.tensor_add(rank[:], gtc[:], tie[:])
                V.drain().then_inc(r_ready, 1)
                for n in range(E // 2):
                    dve.wait_ge(pr_ready, n + 1)
                    dve.wait_ge(ab_ready, n + 1)
                    V.scalar_tensor_tensor(comb[:, n, :], rb[n % 2][:], p64[:, 0:1], ab[n % 2][:], ALU.is_equal,
                                           ALU.mult).then_inc(comb_done, 1)


def ec_experts(nc, a, h, ident, iota, rank, y_dram):
    E, HW = N_EXP, 512
    NS = D_FF // HW
    KF = HW // P
    SB = 2 * NS
    wg, wu, wd = a["w_gate_2"][0], a["w_up_2"][0], a["w_down_2"][0]
    lo, hi = slice(0, CAP), slice(CAP, P)
    with stage(nc, "ec") as st:
        w = [[st.sb(f"w{n}{r}", [P, KD * HW]) for r in range(2)] for n in range(3)]
        w_ready = [[st.sem(f"w_ready{n}{r}") for r in range(2)] for n in range(3)]
        sel = st.sb("sel", [P, NT, P])
        pr = st.sb("pr", [P, NT, 2])
        xg = st.sb("xg", [P, KD, P])
        sig = [st.sb(f"sig{r}", [CAP, HW]) for r in range(2)]
        up = [st.sb(f"up{r}", [CAP, HW]) for r in range(2)]
        hid = [st.sb(f"hid{r}", [CAP, HW]) for r in range(2)]
        hT = [st.sb(f"hT{r}", [P, KF * CAP]) for r in range(2)]
        yb = [st.sb(f"y{r}", [P, 512]) for r in range(2)]
        gu_ps = [st.ps(f"gu{r}") for r in range(2)]
        h_ps = [st.ps(f"h{r}") for r in range(2)]
        y_ps = [st.ps(f"yp{r}") for r in range(2)]
        x_ps = st.ps("x")
        sel_ready, gath_ready = st.sem("sel_ready"), st.sem("gath_ready")
        xg_copied = st.sem("xg_copied")
        gu_ready, act_ready = st.sem("gu_ready"), st.sem("act_ready")
        hid_ready = st.sem("hid_ready")
        hTp_ready = st.sem("hTp_ready")
        hT_ready = st.sem("hT_ready")
        down_ready = st.sem("down_ready")
        y_copied = st.sem("y_copied")
        stored, yb_free = st.sem("stored"), st.sem("yb_free")
        with nc.Block() as block:

            @block.sync
            def _(sp):
                with sp.Fori(0, E // 2) as i:
                    for s in range(SB):
                        e, j, r = 2 * i + s // NS, s % NS, s % 2
                        n = SB * i + s
                        sp.wait_ge(hid_ready, n + 1)
                        for m, src in enumerate((wg, wu)):
                            sp.dma_start(w[m][r][:], src[ds(e, 1)].rearrange("a (k p) n -> p (a k) n", p=P)
                                         [:, :, j * HW:(j + 1) * HW]).then_inc(w_ready[m][r], 16)
                        sp.wait_ge(down_ready, n + 1)
                        sp.dma_start(w[2][r][:], wd[ds(e, 1)].rearrange("a (k p) n -> p (a k) n", p=P)
                                     [:, j * KF:(j + 1) * KF, :]).then_inc(w_ready[2][r], 16)

            @block.tensor
            def _(pe):
                with pe.Fori(0, E // 2) as i:
                    pe.wait_ge(sel_ready, i + 1)
                    for hh in range(2):
                        pe.wait_ge(xg_copied, 2 * i + hh + 1)
                        for c in range(4):
                            for t in range(NT):
                                cc = hh * 4 + c
                                mm = nc.tensor.matmul(x_ps[:, c * P:(c + 1) * P], h[:, t, cc * P:(cc + 1) * P],
                                                      sel[:, t, :], start=(t == 0), stop=(t == NT - 1))
                        mm.then_inc(gath_ready, 1)
                    pe.wait_ge(xg_copied, 2 * i + 3)

                    def gate_up(s):
                        n, c0, r = SB * i + s, (s // NS) * CAP, s % 2
                        for m in range(2):
                            pe.wait_ge(w_ready[m][r], 16 * (NS * i + s // 2 + 1))
                        pe.wait_ge(hid_ready, n + 1)
                        for k in range(KD):
                            for m, part in enumerate((lo, hi)):
                                mm = nc.tensor.matmul(gu_ps[r][part, :], xg[:, k, c0:c0 + CAP],
                                                      w[m][r][:, k * HW:(k + 1) * HW],
                                                      start=(k == 0), stop=(k == KD - 1))
                        mm.then_inc(gu_ready, 1)

                    def turn(s):
                        n, r = SB * i + s, s % 2
                        pe.wait_ge(hid_ready, n + 3)
                        pe.wait_ge(hT_ready, n + 1)
                        for f in range(KF):
                            mm = nc.tensor.matmul(h_ps[r][:, f * CAP:(f + 1) * CAP], hid[r][:, f * P:(f + 1) * P],
                                                  ident[0:CAP, 0:CAP], start=True, stop=True)
                        mm.then_inc(hTp_ready, 1)

                    def down(s):
                        n, j, r, ex = SB * i + s, s % NS, s % 2, s // NS
                        pe.wait_ge(w_ready[2][r], 16 * (NS * i + s // 2 + 1))
                        pe.wait_ge(hT_ready, n + 3)
                        if j == 0:
                            pe.wait_ge(y_copied, 2 * i + ex + 1)
                        for f in range(KF):
                            for hh, part in enumerate((lo, hi)):
                                mm = nc.tensor.matmul(y_ps[ex][part, :], hT[r][:, f * CAP:(f + 1) * CAP],
                                                      w[2][r][:, f * D + hh * 512:f * D + (hh + 1) * 512],
                                                      start=(j == 0 and f == 0), stop=(j == NS - 1 and f == KF - 1))
                        mm.then_inc(down_ready, 1)

                    gate_up(0)
                    for s in range(1, SB):
                        gate_up(s)
                        turn(s - 1)
                        down(s - 1)
                    turn(SB - 1)
                    down(SB - 1)

            @block.vector
            def _(dve):
                V = nc.vector
                dve.sem_inc(hid_ready, 2)

                def select(v):
                    for t in range(NT):
                        for r in range(2):
                            V.tensor_scalar(sel[:, t, r * CAP:(r + 1) * CAP], iota[:, 0:CAP], pr[:, t, r:r + 1], None,
                                            ALU.is_equal)
                with dve.Fori(0, E // 2) as i:
                    V.tensor_copy(pr[:], rank[:, :, ds(2 * i, 2)])
                    V.drain()
                    select(i)
                    V.drain().then_inc(sel_ready, 1)
                    for s in range(SB):
                        n, r = SB * i + s, s % 2
                        dve.wait_ge(act_ready, n + 1)
                        V.tensor_mul(sig[r][:], sig[r][:], gu_ps[r][lo, :])
                        V.drain()
                        V.tensor_mul(hid[r][:], sig[r][:], up[r][:]).then_inc(hid_ready, 1)
                        if s >= 1:
                            dve.wait_ge(hTp_ready, n)
                            V.tensor_copy(hT[(s - 1) % 2][:], h_ps[(s - 1) % 2][:, 0:KF * CAP]).then_inc(hT_ready, 1)
                    dve.wait_ge(hTp_ready, SB * i + SB)
                    V.tensor_copy(hT[(SB - 1) % 2][:], h_ps[(SB - 1) % 2][:, 0:KF * CAP]).then_inc(hT_ready, 1)

            @block.scalar
            def _(act):
                act.sem_inc(xg_copied, 1)
                act.sem_inc(hT_ready, 2)
                act.sem_inc(down_ready, 2)
                act.sem_inc(y_copied, 2)
                act.sem_inc(yb_free, 2)
                with act.Fori(0, E // 2) as i:
                    for hh in range(2):
                        act.wait_ge(gath_ready, 2 * i + hh + 1)
                        nc.scalar.activation(xg[:, hh * 4:hh * 4 + 4, :].rearrange("p c s -> p (c s)"), x_ps[:],
                                             ACT.Copy).then_inc(xg_copied, 1)

                    def y_out(r):
                        act.wait_ge(yb_free, 2 * i + r + 1)
                        act.wait_ge(down_ready, SB * i + (r + 1) * NS + 2)
                        nc.scalar.activation(yb[r][:], y_ps[r][:], ACT.Copy).then_inc(y_copied, 1)

                    for s in range(SB):
                        n, r = SB * i + s, s % 2
                        act.wait_ge(gu_ready, n + 1)
                        act.wait_ge(hid_ready, n + 1)
                        nc.scalar.activation(sig[r][:], gu_ps[r][lo, :], ACT.Sigmoid)
                        nc.scalar.activation(up[r][:], gu_ps[r][hi, :], ACT.Copy).then_inc(act_ready, 1)
                        if s == NS + 1:
                            y_out(0)
                    y_out(1)

            @block.gpsimd
            def _(pool):
                with pool.Fori(0, E // 2) as i:
                    for r in range(2):
                        e = 2 * i + r
                        pool.wait_ge(y_copied, e + 3)
                        pool.dma_start(y_dram[ds(e * CAP, CAP), 0:512], yb[r][lo, :]).then_inc(stored, 16)
                        pool.dma_start(y_dram[ds(e * CAP, CAP), 512:D], yb[r][hi, :]).then_inc(stored, 16)
                        pool.wait_ge(stored, 32 * e + 32)
                        pool.sem_inc(yb_free, 1)


def ec_combine(nc, comb, y_dram, out_dram):
    NP_ = N_EXP // 2
    with stage(nc, "ecc") as st:
        y = st.sb("y", [P, NP_, D])
        ob = [st.sb(f"o{r}", [P, 512]) for r in range(2)]
        ld, ready, copied, stored = st.sem("ld"), st.sem("ready"), st.sem("copied"), st.sem("stored")
        ps = [st.ps(f"ps{r}") for r in range(2)]
        units = [(t, hh) for t in range(NT) for hh in range(2)]
        with nc.Block() as block:

            @block.sync
            def _(sp):
                sp.dma_start(y[:], y_dram.rearrange("(n p) d -> p n d", p=P)).then_inc(ld, 16)
                for n, (t, hh) in enumerate(units):
                    sp.wait_ge(copied, n + 1)
                    sp.dma_start(out_dram[t * P:(t + 1) * P, hh * 512:(hh + 1) * 512], ob[n % 2][:]).then_inc(stored, 16)
                    sp.wait_ge(stored, 16 * (n + 1))

            @block.tensor
            def _(pe):
                pe.wait_ge(ld, 16)
                for n, (t, hh) in enumerate(units):
                    if n >= 2:
                        pe.wait_ge(copied, n - 1)
                    for c in range(NP_):
                        mm = nc.tensor.matmul(ps[n % 2][:], comb[:, c, t * P:(t + 1) * P],
                                              y[:, c, hh * 512:(hh + 1) * 512], start=(c == 0), stop=(c == NP_ - 1))
                    mm.then_inc(ready, 1)

            @block.scalar
            def _(act):
                for n, (t, hh) in enumerate(units):
                    if n >= 2:
                        act.wait_ge(stored, 16 * (n - 1))
                    act.wait_ge(ready, n + 1)
                    nc.scalar.activation(ob[n % 2][:], ps[n % 2][:], ACT.Copy).then_inc(copied, 1)


def second_block(nc, a, x, xT, cst, out, dram):
    ident, strict, ones, iota, pidx = cst
    mod0, mod = dram("mod0", [1, 6 * D]), dram("mod", [6 * D])
    with nc.sbuf_tensor("condT", [P, KD, 1], F32) as condT:
        condition(nc, a, condT[:, :, 0])
        gemm(nc, "ada", a["w_ada_2"][0], 0, 12, 512, condT, P, 1, mod0, "N")
    add_rows(nc, "ada_b", mod0[0], a["b_ada_2"][0], mod, 96)
    sh1, sc1, gt1, sh2, sc2, gt2 = (mod[n * D:(n + 1) * D] for n in range(6))
    win = a["w_in_2"][0]
    biases = [dram(f"bias{g}", [DIL_H, P, (1024, 512, 512)[g]]) for g in range(3)]
    relative_bias(nc, a, biases)
    with nc.sbuf_tensor("h", [P, NT, D], F32) as h:
        norm(nc, "rms1", x, h, xT, ident, EPS2, True, a["g_norm_mix_2"][0], sh1, one_plus=sc1)
        n_lat = Q_RANK + KV_RANK + ROPE
        lat = dram("lat", [S, n_lat])
        gemm(nc, "lat_w", win, 0, 2, n_lat // 2, xT, P, S, lat, "N")
        gates = dram("gates", [S, 2 * D])
        gemm(nc, "gates_w", win, n_lat + 9 * D, 4, 512, xT, P, S, gates, "N")
        ogs = [dram(f"og{g}", [S, D]) for g in range(3)]
        sts = [dram(f"stat{g}", [S, 2 * DIL_H]) for g in range(3)]
        for g in range(3):
            dilated(nc, a, ident, xT, g, win, n_lat + g * 3 * D, biases[g], ogs[g], sts[g], dram)
        q_all, k_all, v_all = dram("mla_q", [MLA_H * (NOPE + ROPE), S]), dram("mla_k", [D, S]), dram("mla_v", [S, D])
        qpe, kpe, oa = dram("mla_qpe", [MLA_H * ROPE, S]), dram("mla_kpe", [ROPE, S]), dram("oa", [S, D])
        with ExitStack() as c2:
            sb = lambda n, s: c2.enter_context(nc.sbuf_tensor("mla_" + n, s, F32))
            cqT, ckvT = sb("cqT", [P, Q_RANK // P, S]), sb("ckvT", [P, KV_RANK // P, S])
            kp = [sb(f"kp{n}", [ROPE // 2, S]) for n in range(2)]
            latents(nc, a, ident, lat, cqT, ckvT, kp)
            gemm(nc, "uq", a["w_uq_L"], 0, 3, 512, cqT, P, S, q_all, "T")
            gemm(nc, "uk", a["w_ukv_L"], 0, 2, 512, ckvT, P, S, k_all, "T")
            gemm(nc, "uv", a["w_ukv_L"], D, 2, 512, ckvT, P, S, v_all, "N")
            rotary(nc, a, q_all, kp, qpe, kpe)
        attention(nc, "mla", ident, MLA_H, NOPE, P, S,
                  lambda hd: [q_all[ds(hd * NOPE, NOPE), :], qpe[ds(hd * ROPE, ROPE), :]],
                  lambda hd: [k_all[ds(hd * NOPE, NOPE), :], kpe],
                  lambda hd: [((slice(None), slice(0, NT), slice(None)),
                               v_all.rearrange("(c p) f -> p c f", p=P)[:, :, ds(hd * P, P)])],
                  lambda q, u: q[:, u * P:(u + 1) * P], lambda k, u: k[:, :], lambda u: range(NT),
                  lambda hd, u: oa[u * P:(u + 1) * P, ds(hd * P, P)],
                  (NOPE + ROPE) ** -0.5, pe_dims=ROPE, v_chunks=NT)
        merge(nc, oa, ogs, sts, gates, xT, ident)
        proj = dram("proj2", [S, D])
        gemm(nc, "out2", a["w_out_2"][0], 0, 2, 512, xT, P, S, proj, "N")
        norm(nc, "rms2", x, h, xT, ident, EPS2, True, a["g_norm_ffn_2"][0], sh2, resid=proj, gate=gt1, one_plus=sc2)
        affT_d, y_d = dram("affT", [N_EXP * S]), dram("ec_y", [N_EXP * CAP, D])
        with nc.sbuf_tensor("ec_comb", [P, N_EXP // 2, S], F32) as comb:
            with nc.sbuf_tensor("ec_aff", [P, NT, N_EXP], F32) as aff, \
                    nc.sbuf_tensor("ec_rank", [P, NT, N_EXP], F32) as rank:
                ec_route(nc, a, xT, ident, ones, pidx, affT_d, aff, rank, comb)
                ec_experts(nc, a, h, ident, iota, rank, y_d)
            ec_combine(nc, comb, y_d, proj)
        norm(nc, "rms3", x, h, None, ident, EPS2, True, a["g_final_2"], resid=proj, gate=gt2, out_dram=out[0])


def na_bias_layout(rpb):
    q_cols = np.arange(GRID_W).reshape(N_CB, WIN_W)
    starts = np.clip(np.arange(N_CB) * WIN_W - WIN_W // 2, 0, GRID_W - SPAN)
    key_cols = starts[:, None] + np.arange(SPAN)
    lo = np.clip(q_cols - WIN_W // 2, 0, GRID_W - WIN_W)[:, :, None]
    kc = key_cols[:, None, :]
    inside = (kc >= lo) & (kc < lo + WIN_W)
    dc = np.where(inside, kc - q_cols[:, :, None] + WIN_W - 1, 2 * WIN_W - 1)
    dr = np.arange(ROWS)[None, :] - np.arange(ROWS)[:, None] + 7
    padded = np.pad(rpb, ((0, 0), (0, 0), (0, 1)), constant_values=NEG)
    got = padded[:, dr[:, None, None, :, None], dc.transpose(1, 0, 2)[None, :, :, None, :]]
    return np.ascontiguousarray(got.reshape(rpb.shape[0], P, N_CB * ROWS * SPAN))


ROPE_THETA = 10000.0


def unit_tokens():
    p, u = np.arange(P)[:, None], np.arange(4)[None, :]
    return np.concatenate([u * P + p, 4 * p + u, 16 * (p % 32) + 4 * u + p // 32], axis=1)


def band_mask():
    q = unit_tokens()
    keys = [np.array(G0_START)[:, None] + np.arange(256)[None, :], q[:, 4:8].T, q[:, 8:12].T]
    cols = []
    for g, (d, r) in enumerate(((1, 64), (4, 64), (16, 64))):
        for u in range(4):
            k, qq = keys[g][u][None, :], q[:, g * 4 + u][:, None]
            ok = (k % d == qq % d) & (np.abs(k // d - qq // d) <= r)
            cols.append(np.where(ok, 0.0, NEG))
    return np.concatenate(cols, axis=1).astype(np.float32)


def kernel(**inputs):
    import concourse.bacc as _bacc
    from concourse.bass_utils import run_bass_kernel_spmd as _run

    nc = _bacc.Bacc("TRN2", target_bir_lowering=False, num_devices=1)
    host = {k: np.ascontiguousarray(v) for k, v in inputs.items() if k != "na_rpb"}
    host["na_bias"] = na_bias_layout(np.asarray(inputs["na_rpb"])[0])
    host["ml_conv_wT"] = np.ascontiguousarray(np.asarray(inputs["ml_conv_w"])[0].T)
    host["ml_gate_bT"] = np.ascontiguousarray(np.asarray(inputs["ml_gate_b"])[0].T)
    for n in ("ml_conv_b", "ml_norm_g", "ml_skip"):
        host[n + "P"] = np.ascontiguousarray(np.asarray(inputs[n])[0].reshape(-1, 96).T)
    cols = lambda v: np.ascontiguousarray(np.asarray(v).reshape(-1, P).T)
    host["c_P"] = cols(inputs["c_2"])
    host["g_q_lat_P"], host["g_kv_lat_P"] = cols(inputs["g_q_lat_2"]), cols(inputs["g_kv_lat_2"])
    uq = np.asarray(inputs["w_uq_2"])[0].reshape(Q_RANK, MLA_H, NOPE + ROPE)
    cuts = (uq[:, :, :NOPE], uq[:, :, NOPE:NOPE + 32], uq[:, :, NOPE + 32:])
    host["w_uq_L"] = np.ascontiguousarray(np.concatenate([c.reshape(Q_RANK, -1) for c in cuts], axis=1))
    ukv = np.asarray(inputs["w_ukv_2"])[0].reshape(KV_RANK, MLA_H, 2 * P)
    host["w_ukv_L"] = np.ascontiguousarray(
        np.concatenate([ukv[:, :, :P].reshape(KV_RANK, -1), ukv[:, :, P:].reshape(KV_RANK, -1)], axis=1))
    host["rel_tab"] = np.ascontiguousarray(
        np.asarray(inputs["rel_bias_2"]).reshape(N_REL, 3, DIL_H).transpose(1, 0, 2).reshape(-1))
    host["pos_q"] = np.ascontiguousarray(np.asarray(inputs["positions_2"])[0][unit_tokens()])
    host["band_mask"] = band_mask()
    host["inv_freq"] = np.tile(ROPE_THETA ** (-np.arange(0, ROPE, 2) / ROPE), 4)[:, None].astype(np.float32)
    arrays, aps = {}, {}
    for k, v in host.items():
        if k not in USED:
            continue
        arrays[f"in_{k}"] = v
        aps[k] = nc.dram_tensor(f"in_{k}", v.shape, mybir.dt.from_np(v.dtype), kind="ExternalInput").ap()
    out = nc.dram_tensor("out_0", (1, S, D), F32, kind="ExternalOutput").ap()
    build(nc, aps, out)
    r = _run(nc, [arrays], core_ids=[0])
    return r.results[0]["out_0"]
```

```python
import math
from contextlib import ExitStack, contextmanager

import numpy as np
import concourse.bass as bass
from concourse import mybir

F32 = mybir.dt.float32
I32 = mybir.dt.int32
U32 = mybir.dt.uint32
ALU = mybir.AluOpType
ACT = mybir.ActivationFunctionType
AX = mybir.AxisListType
ds = bass.ds

P = 128
S = 512
NT = S // P
D = 1024
KD = D // P
NEG = -1e30

DEPTH = 2
ALPHA = (2 * DEPTH) ** 0.25
LN_EPS = 1e-5
GRID_W = 64
N_MEM = 256
MEM_HEADS, MEM_DH = 4, 64
MEM_W = MEM_HEADS * MEM_DH
NA_HEADS, NA_DH = 12, 64
NA_W = NA_HEADS * NA_DH
WIN_W = 16
SPAN = 2 * WIN_W
ROWS = S // GRID_W
N_CB = GRID_W // WIN_W
ML_HEADS, ML_DH = 4, 192
ML_W = ML_HEADS * ML_DH
CONV_K = 5
N_EXP, N_GRP, EPG = 16, 4, 4
D_EXP = 512
MOE_BLOCKS = 24

MLA_H, Q_RANK, KV_RANK, NOPE, ROPE = 8, 384, 256, 128, 64
DIL_H = 8
DIL = ((128, 1), (512, 4), (2048, 16))
N_REL = 32
EPS2 = 1e-6
CAP = 2 * S // N_EXP
D_FF = 2048


class Stage:

    def __init__(self, nc, name):
        self.nc, self.name, self.sems, self.ctx = nc, name, [], ExitStack()

    def sb(self, name, shape, dt=F32):
        return self.ctx.enter_context(self.nc.sbuf_tensor(f"{self.name}_{name}", list(shape), dt))

    def ps(self, name, shape=(P, 512)):
        return self.ctx.enter_context(self.nc.psum_tensor(f"{self.name}_{name}", list(shape), F32))

    def sem(self, name):
        s = self.nc.alloc_semaphore(f"{self.name}_{name}")
        self.sems.append(s)
        return s


@contextmanager
def stage(nc, name):
    st = Stage(nc, name)
    with st.ctx:
        yield st
    nc.clear_and_free_semaphores(st.sems)
    nc.all_engine_barrier()


def ring_loop(eng, n, body, unroll=2):
    whole = n // unroll
    if whole == 1:
        for r in range(unroll):
            body(r, r, 0)
    elif whole > 1:
        with eng.Fori(0, whole) as i:
            for r in range(unroll):
                body(i * unroll + r, r, i)
    for r in range(n - whole * unroll):
        body(whole * unroll + r, r, whole)


def bcast_rows(vec):
    return vec.partition_broadcast(P)


def job(W, col0, n_chunks, cw, xT, kp, n_tok, dest, mode, M=P, tok=None):
    tp = min(P, n_tok)
    G = cw // M if mode == "T" else n_tok // tp
    return dict(w=W.rearrange("(k p) n -> p k n", p=kp), col0=col0, n=n_chunks, cw=cw, xT=xT, kp=kp, n_tok=n_tok,
                mode=mode, M=M, tok=tok, nk=xT.shape[1], tp=tp, G=G, ow=n_tok if mode == "T" else cw,
                op=M if mode == "T" else tp,
                dest=dest.rearrange("(g p) t -> p g t", p=M) if mode == "T" else
                dest.rearrange("(g p) f -> p g f", p=tp))


def gemms(nc, name, jobs, side=None):
    base, groups = 0, 0
    for n, jb in enumerate(jobs):
        jb["base"], jb["groups"] = base, groups
        jb["slack"] = max(0, jb["G"] - jobs[n - 1]["G"]) if n else 0
        base += jb["n"]
        groups += jb["n"] * jb["G"]
    CREDIT = 8
    with stage(nc, name) as st:
        w = [st.sb(f"w{r}", [P, KD * 512]) for r in range(2)]
        ob = [st.sb(f"o{r}", [P, 2048]) for r in range(2)]
        ps = [st.ps(f"ps{b}") for b in range(8)]
        w_ready = [st.sem(f"w_ready{r}") for r in range(2)]
        bank_ready = st.sem("bank_ready")
        bank_free = st.sem("bank_free")
        stored, ob_free = st.sem("stored"), st.sem("ob_free")
        extra = side(st) if side else None
        w_of = lambda jb, r: w[r][0:jb["kp"], 0:jb["nk"] * jb["cw"]].rearrange("p (k n) -> p k n", n=jb["cw"])
        o_of = lambda jb, r: ob[r][0:jb["op"], 0:jb["G"] * jb["ow"]].rearrange("p (g n) -> p g n", n=jb["ow"])
        with nc.Block() as block:

            @block.sync
            def _(sp):
                if extra:
                    extra.sync(sp)
                for jb in jobs:
                    def load(j, r, i):
                        slot = (jb["base"] + r) % 2
                        sp.wait_ge(bank_free, j * jb["G"] + (CREDIT + jb["groups"] - jb["G"] + jb["slack"]))
                        sp.dma_start(w_of(jb, slot), jb["w"][:, :, ds(jb["col0"] + j * jb["cw"], jb["cw"])]) \
                            .then_inc(w_ready[slot], 16)
                    ring_loop(sp, jb["n"], load)
                if extra:
                    extra.finish(sp)

            @block.tensor
            def _(pe):
                for jb in jobs:
                    def chunk(j, r, i):
                        slot = (jb["base"] + r) % 2
                        wv, xT, G = w_of(jb, slot), jb["xT"], jb["G"]
                        pe.wait_ge(w_ready[slot], (i + (jb["base"] + r) // 2 + 1) * 16)
                        pe.wait_ge(bank_free, j * G + (CREDIT + jb["groups"] - G + jb["slack"]))
                        for g in range(G):
                            for k in range(jb["nk"]):
                                if jb["mode"] == "T":
                                    rhs = xT[:, k, 0:jb["n_tok"]]
                                    rhs = jb["tok"](rhs) if jb["tok"] else rhs
                                    lhs = wv[:, k, g * jb["M"]:(g + 1) * jb["M"]]
                                else:
                                    lhs, rhs = xT[:, k, g * jb["tp"]:(g + 1) * jb["tp"]], wv[:, k, :]
                                mm = nc.tensor.matmul(ps[slot * 4 + g][0:jb["op"], 0:jb["ow"]], lhs, rhs,
                                                      start=(k == 0), stop=(k == jb["nk"] - 1))
                            mm.then_inc(bank_ready, 1)
                    ring_loop(pe, jb["n"], chunk)

            @block.scalar
            def _(act):
                act.sem_inc(bank_free, CREDIT)
                act.sem_inc(ob_free, 2)
                for jb in jobs:
                    def evict(j, r, i):
                        slot = (jb["base"] + r) % 2
                        act.wait_ge(ob_free, j + (jb["base"] + 1))
                        for g in range(jb["G"]):
                            act.wait_ge(bank_ready, j * jb["G"] + (jb["groups"] + g + 1))
                            nc.scalar.activation(o_of(jb, slot)[:, g, :], ps[slot * 4 + g][0:jb["op"], 0:jb["ow"]],
                                                 ACT.Copy).then_inc(bank_free, 1)
                    ring_loop(act, jb["n"], evict)

            @block.gpsimd
            def _(pool):
                for jb in jobs:
                    def store(j, r, i):
                        slot, G = (jb["base"] + r) % 2, jb["G"]
                        pool.wait_ge(bank_free, j * G + (CREDIT + jb["groups"] + G))
                        if jb["mode"] == "T":
                            out = jb["dest"][:, ds(j * G, G), :]
                        else:
                            out = jb["dest"][:, :, ds(j * jb["cw"], jb["cw"])]
                        pool.dma_start(out, o_of(jb, slot)).then_inc(stored, 16)
                        pool.wait_ge(stored, j * 16 + (16 * jb["base"] + 16))
                        pool.sem_inc(ob_free, 1)
                    ring_loop(pool, jb["n"], store)
                    if extra and jb is jobs[0]:
                        extra.fill(pool)

            @block.vector
            def _(dve):
                if extra:
                    extra.vector(dve)


def gemm(nc, name, *args, **kw):
    gemms(nc, name, [job(*args, **kw)])


def norm(nc, name, x_src, dst, dstT, ident, eps, rms, gain, shift=None, resid=None, alpha=1.0,
         gate=None, one_plus=None, n_tiles=NT, out_dram=None):
    from_dram = x_src.shape[0] != P or len(x_src.shape) == 2
    with stage(nc, name) as st:
        g_bc = st.sb("g", [P, D])
        vecs = [(gain, g_bc)]
        if shift is not None:
            b_bc = st.sb("b", [P, D])
            vecs.append((shift, b_bc))
        if one_plus is not None:
            s_bc = st.sb("s", [P, D])
            vecs.append((one_plus, s_bc))
        if gate is not None:
            t_bc = st.sb("t", [P, D])
            vecs.append((gate, t_bc))
        xin = st.sb("xin", [P, n_tiles, D]) if from_dram else x_src
        res = st.sb("res", [P, n_tiles, D]) if resid is not None else None
        stats = st.sb("stats", [P, n_tiles, 2, 6])
        mv = st.sb("mv", [P, n_tiles, 2])
        sq = st.sb("sq", [P, n_tiles])
        rstd = st.sb("rstd", [P, n_tiles])
        vec_in, x_in = st.sem("vec_in"), [st.sem(f"x_in{t}") for t in range(n_tiles)]
        var_ready, sqrt_ready, y_ready = st.sem("var_ready"), st.sem("sqrt_ready"), st.sem("y_ready")
        t_ready, t_free, out_done = st.sem("t_ready"), st.sem("t_free"), st.sem("out_done")
        ps = [st.ps(f"ps{b}") for b in range(4)]
        per_tile = 16 * ((1 if from_dram else 0) + (1 if resid is not None else 0))
        with nc.Block() as block:

            @block.sync
            def _(sp):
                for t in range(n_tiles):
                    if from_dram:
                        sp.dma_start(xin[:, t, :], x_src[t * P:(t + 1) * P, :]).then_inc(x_in[t], 16)
                    if resid is not None:
                        sp.dma_start(res[:, t, :], resid[t * P:(t + 1) * P, :]).then_inc(x_in[t], 16)
                for v, t in vecs:
                    sp.dma_start(t[:], bcast_rows(v)).then_inc(vec_in, 16)
                if out_dram is not None:
                    for t in range(n_tiles):
                        sp.wait_ge(y_ready, t + 1)
                        sp.dma_start(out_dram[t * P:(t + 1) * P, :], dst[:, t, :]).then_inc(out_done, 16)
                    sp.wait_ge(out_done, 16 * n_tiles)

            @block.vector
            def _(dve):
                if gate is not None:
                    dve.wait_ge(vec_in, 16 * len(vecs))
                for t in range(n_tiles):
                    if per_tile:
                        dve.wait_ge(x_in[t], per_tile)
                    if resid is not None:
                        if gate is not None:
                            nc.vector.tensor_mul(res[:, t, :], res[:, t, :], t_bc[:])
                            nc.vector.drain()
                        nc.vector.scalar_tensor_tensor(xin[:, t, :], xin[:, t, :], alpha, res[:, t, :],
                                                       ALU.mult, ALU.add)
                        nc.vector.drain()
                    for h in range(2):
                        nc.vector.bn_stats(stats[:, t, h, :], xin[:, t, h * 512:(h + 1) * 512])
                    nc.vector.drain()
                    nc.vector.bn_aggr(mv[:, t, :], stats[:, t, :, :].rearrange("p a b -> p (a b)"))
                nc.vector.drain()
                if rms:
                    nc.vector.tensor_mul(sq[:], mv[:, :, 0], mv[:, :, 0])
                    nc.vector.drain()
                    nc.vector.scalar_tensor_tensor(sq[:], mv[:, :, 1], eps, sq[:],
                                                   ALU.add, ALU.add).then_inc(var_ready, 1)
                else:
                    nc.vector.tensor_scalar(sq[:], mv[:, :, 1], eps, None, ALU.add).then_inc(var_ready, 1)
                dve.wait_ge(sqrt_ready, 1)
                nc.vector.reciprocal(rstd[:], sq[:])
                dve.wait_ge(vec_in, 16 * len(vecs))
                if one_plus is not None:
                    nc.vector.scalar_tensor_tensor(g_bc[:], s_bc[:], 1.0, g_bc[:], ALU.add, ALU.mult)
                nc.vector.drain()
                for t in range(n_tiles):
                    if rms:
                        nc.vector.tensor_scalar(dst[:, t, :], xin[:, t, :], rstd[:, t:t + 1], None, ALU.mult)
                    else:
                        nc.vector.tensor_scalar(dst[:, t, :], xin[:, t, :], mv[:, t, 0:1], rstd[:, t:t + 1],
                                                ALU.subtract, ALU.mult)
                    nc.vector.drain()
                    last = nc.vector.tensor_mul(dst[:, t, :], dst[:, t, :], g_bc[:])
                    if shift is not None:
                        nc.vector.drain()
                        last = nc.vector.tensor_add(dst[:, t, :], dst[:, t, :], b_bc[:])
                    last.then_inc(y_ready, 1)

            @block.tensor
            def _(pe):
                if dstT is None:
                    return
                for n in range(2 * n_tiles):
                    t, c0 = n // 2, n % 2 * 4
                    pe.wait_ge(y_ready, t + 1)
                    pe.wait_ge(t_free, n + 1)
                    for c in range(4):
                        mm = nc.tensor.transpose(ps[n % 4][:, c * P:(c + 1) * P],
                                                 dst[:, t, (c0 + c) * P:(c0 + c + 1) * P], ident[:])
                    mm.then_inc(t_ready, 1)

            @block.scalar
            def _(act):
                act.sem_inc(t_free, 4)
                act.wait_ge(var_ready, 1)
                nc.scalar.activation(sq[:], sq[:], ACT.Sqrt).then_inc(sqrt_ready, 1)
                if dstT is None:
                    return
                for n in range(2 * n_tiles):
                    t, c0 = n // 2, n % 2 * 4
                    act.wait_ge(t_ready, n + 1)
                    nc.scalar.activation(dstT[:, c0:c0 + 4, t * P:(t + 1) * P],
                                         ps[n % 4][:].rearrange("p (c t) -> p c t", t=P), ACT.Copy).then_inc(t_free, 1)


def load_transposed(nc, name, src, dstT, ident, kp_list=None):
    with stage(nc, name) as st:
        x = st.sb("x", [P, NT, D])
        x_in = [st.sem(f"x_in{t}") for t in range(NT)]
        t_ready, t_free = st.sem("t_ready"), st.sem("t_free")
        ps = [st.ps(f"ps{b}") for b in range(4)]
        with nc.Block() as block:

            @block.sync
            def _(sp):
                for t in range(NT):
                    sp.dma_start(x[:, t, :], src[t * P:(t + 1) * P, :]).then_inc(x_in[t], 16)

            @block.tensor
            def _(pe):
                for n in range(2 * NT):
                    t, c0 = n // 2, n % 2 * 4
                    pe.wait_ge(x_in[t], 16)
                    pe.wait_ge(t_free, n + 1)
                    for c in range(4):
                        mm = nc.tensor.transpose(ps[n % 4][:, c * P:(c + 1) * P],
                                                 x[:, t, (c0 + c) * P:(c0 + c + 1) * P], ident[:])
                    mm.then_inc(t_ready, 1)

            @block.scalar
            def _(act):
                act.sem_inc(t_free, 4)
                for n in range(2 * NT):
                    t, c0 = n // 2, n % 2 * 4
                    act.wait_ge(t_ready, n + 1)
                    nc.scalar.activation(dstT[:, c0:c0 + 4, t * P:(t + 1) * P],
                                         ps[n % 4][:].rearrange("p (c t) -> p c t", t=P), ACT.Copy).then_inc(t_free, 1)


def attention(nc, name, ident, n_heads, dh, dv, nk, q_src, k_src, v_src, q_at, k_at, v_at, out, scale,
              bias_src=None, pe_dims=0, n_keys=S, stats_out=None, v_chunks=None, v_once=(), clear=()):
    U = 4
    nc_k = nk // P
    with stage(nc, name) as st:
        n_parts = 2 if pe_dims else 1
        dims = [dh] + ([pe_dims] if pe_dims else [])
        q = [[st.sb(f"q{r}{a}", [dims[a], S]) for a in range(n_parts)] for r in range(2)]
        k = [[st.sb(f"k{r}{a}", [dims[a], n_keys]) for a in range(n_parts)] for r in range(2)]
        v = [st.sb("v", [P, v_chunks, n_heads * dv])] * 2 if v_once else \
            [st.sb(f"v{r}", [P, v_chunks, dv]) for r in range(2)]
        v_in = st.sem("v_in")
        v_cols = lambda j: ds(j * dv, dv) if v_once else slice(0, dv)
        bias = [st.sb(f"bias{r}", [P, U * nk]) for r in range(2)] if bias_src else None
        ssb = [st.sb(f"s{r}", [P, nk]) for r in range(2)]
        pr = [st.sb(f"p{r}", [P, nk]) for r in range(2)]
        pT = [st.sb(f"pT{r}", [P, nk]) for r in range(2)]
        ob = [st.sb(f"o{r}", [P, U, dv]) for r in range(2)]
        nmx = st.sb("nmx", [P, 8])
        den = st.sb("den", [P, 8])
        rden = st.sb("rden", [P, 8])
        stat = st.sb("stat", [P, U, n_heads, 2]) if stats_out is not None else None
        s_ps = [st.ps(f"s_ps{b}") for b in range(2)]
        t_ps = [st.ps(f"t_ps{b}") for b in range(2)]
        o_ps = [st.ps(f"o_ps{b}") for b in range(2)]
        head_in = [st.sem(f"head_in{r}") for r in range(2)]
        s_ready, s_free = st.sem("s_ready"), st.sem("s_free")
        max_ready = st.sem("max_ready")
        exp_done = st.sem("exp_done")
        pT_ready = st.sem("pT_ready")
        pT_copied = st.sem("pT_copied")
        pv_done = st.sem("pv_done")
        out_done = st.sem("out_done")
        stored, ob_free = st.sem("stored"), st.sem("ob_free")
        stat_done = st.sem("stat_done")
        z = st.sb("z", [P, D]) if clear else None
        z_ready, cleared = st.sem("z_ready"), st.sem("cleared")
        probe = [len(q_src(0)), len(k_src(0)), len(v_src(0))]
        n_loads = sum(probe) + (1 if bias_src else 0)
        with nc.Block() as block:

            @block.sync
            def _(sp):
                def load(j, r, i):
                    sp.wait_ge(out_done, j * U + 4)
                    for a, ap in enumerate(q_src(j)):
                        sp.dma_start(q[r][a][:], ap).then_inc(head_in[r], 16)
                    for a, ap in enumerate(k_src(j)):
                        sp.dma_start(k[r][a][:], ap).then_inc(head_in[r], 16)
                    for sl, ap in v_src(j):
                        sp.dma_start(v[r][sl], ap).then_inc(head_in[r], 16)
                    if bias_src:
                        sp.dma_start(bias[r][:], bias_src(j)).then_inc(head_in[r], 16)
                for sl, ap in v_once:
                    sp.dma_start(v[0][sl], ap).then_inc(v_in, 16)
                ring_loop(sp, n_heads, load)

            @block.tensor
            def _(pe):
                if v_once:
                    pe.wait_ge(v_in, 16 * len(v_once))

                def scores(j, r, i, u):
                    n = j * U + u
                    if u == 0:
                        pe.wait_ge(head_in[r], (i + 1) * (16 * n_loads))
                    pe.wait_ge(s_free if bias_src else exp_done, n + 1)
                    for a in range(n_parts):
                        mm = nc.tensor.matmul(s_ps[u % 2][:, 0:nk], q_at(q[r][a], u), k_at(k[r][a], u),
                                              start=(a == 0), stop=(a == n_parts - 1))
                    mm.then_inc(s_ready, 1)

                def turn(j, r, i, u):
                    n = j * U + u
                    pe.wait_ge(exp_done, n + 3)
                    pe.wait_ge(pT_copied, n + 1)
                    for c in range(nc_k):
                        mm = nc.tensor.transpose(t_ps[u % 2][:, c * P:(c + 1) * P],
                                                 pr[u % 2][:, c * P:(c + 1) * P], ident[:])
                    mm.then_inc(pT_ready, 1)

                def values(j, r, i, u):
                    n = j * U + u
                    pe.wait_ge(pT_copied, n + 3)
                    pe.wait_ge(out_done, n + 7)
                    for c in range(nc_k):
                        mm = nc.tensor.matmul(o_ps[u % 2][:, 0:dv], pT[u % 2][:, c * P:(c + 1) * P],
                                              v[r][:, v_at(u)[c], v_cols(j)], start=(c == 0), stop=(c == nc_k - 1))
                    mm.then_inc(pv_done, 1)

                def pair(i, rs):
                    todo = [(i * 2 + r, r, i, u) for r in rs for u in range(U)]
                    scores(*todo[0])
                    for n, item in enumerate(todo):
                        if n + 1 < len(todo):
                            scores(*todo[n + 1])
                        turn(*item)
                        if n:
                            values(*todo[n - 1])
                    values(*todo[-1])
                if n_heads > 2:
                    with pe.Fori(0, n_heads // 2) as i:
                        pair(i, (0, 1))
                else:
                    pair(0, (0, 1))

            @block.vector
            def _(dve):
                dve.sem_inc(out_done, 8)

                def maxes(j, r, i, u):
                    n = j * U + u
                    c = r * U + u
                    dve.wait_ge(s_ready, n + 1)
                    if bias_src:
                        dve.wait_ge(exp_done, n + 1)
                        nc.vector.scalar_tensor_tensor(ssb[u % 2][:], s_ps[u % 2][:, 0:nk], scale,
                                                       bias[r][:, u * nk:(u + 1) * nk], ALU.mult,
                                                       ALU.add).then_inc(s_free, 1)
                        nc.vector.drain()
                        nc.vector.tensor_reduce(nmx[:, c:c + 1], ssb[u % 2][:], AX.X, ALU.max, negate=True) \
                            .then_inc(max_ready, 1)
                    else:
                        nc.vector.tensor_reduce(nmx[:, c:c + 1], s_ps[u % 2][:, 0:nk], AX.X, ALU.max)
                        nc.vector.drain()
                        nc.vector.tensor_scalar(nmx[:, c:c + 1], nmx[:, c:c + 1], -scale, None, ALU.mult) \
                            .then_inc(max_ready, 1)

                def outs(j, r, i, u):
                    n = j * U + u
                    c = r * U + u
                    dve.wait_ge(pv_done, n + 3)
                    dve.wait_ge(exp_done, n + 3)
                    if u == 0:
                        dve.wait_ge(ob_free, j + 1)
                    nc.vector.reciprocal(rden[:, c:c + 1], den[:, c:c + 1])
                    if stat is not None:
                        nc.vector.tensor_copy(stat[:, u, ds(j, 1), 0:1].rearrange("p a b -> p (a b)"), nmx[:, c:c + 1])
                        nc.vector.tensor_copy(stat[:, u, ds(j, 1), 1:2].rearrange("p a b -> p (a b)"), den[:, c:c + 1])
                    nc.vector.drain()
                    nc.vector.tensor_scalar(ob[r][:, u, :], o_ps[u % 2][:, 0:dv], rden[:, c:c + 1], None,
                                            ALU.mult).then_inc(out_done, 1)

                def pair(i, rs):
                    todo = [(i * 2 + r, r, i, u) for r in rs for u in range(U)]
                    maxes(*todo[0])
                    for n, item in enumerate(todo):
                        if n + 1 < len(todo):
                            maxes(*todo[n + 1])
                        if n:
                            outs(*todo[n - 1])
                    outs(*todo[-1])
                if n_heads > 2:
                    with dve.Fori(0, n_heads // 2) as i:
                        pair(i, (0, 1))
                else:
                    pair(0, (0, 1))

            @block.scalar
            def _(act):
                act.sem_inc(exp_done, 2)
                act.sem_inc(pT_copied, 2)

                def exps(j, r, i, u):
                    n = j * U + u
                    c = r * U + u
                    act.wait_ge(max_ready, n + 1)
                    act.wait_ge(pT_ready, n + 1)
                    src = ssb[u % 2][:] if bias_src else s_ps[u % 2][:, 0:nk]
                    e = nc.scalar.activation(pr[u % 2][:], src, ACT.Exp, bias=nmx[:, c:c + 1],
                                             scale=1.0 if bias_src else scale, accum_out=den[:, c:c + 1])
                    e.then_inc(exp_done, 1)

                def copies(j, r, i, u):
                    n = j * U + u
                    act.wait_ge(pT_ready, n + 3)
                    act.wait_ge(pv_done, n + 1)
                    nc.scalar.activation(pT[u % 2][:], t_ps[u % 2][:, 0:nk], ACT.Copy).then_inc(pT_copied, 1)

                def pair(i, rs):
                    todo = [(i * 2 + r, r, i, u) for r in rs for u in range(U)]
                    exps(*todo[0])
                    for n, item in enumerate(todo):
                        if n + 1 < len(todo):
                            exps(*todo[n + 1])
                        copies(*item)
                if n_heads > 2:
                    with act.Fori(0, n_heads // 2) as i:
                        pair(i, (0, 1))
                else:
                    pair(0, (0, 1))

            @block.gpsimd
            def _(pool):
                if bias_src:
                    pool.sem_inc(s_free, 2)
                pool.sem_inc(pT_ready, 2)
                pool.sem_inc(pv_done, 2)
                pool.sem_inc(ob_free, 2)
                if clear:
                    nc.gpsimd.memset(z[:], 0.0).then_inc(z_ready, 1)
                    pool.wait_ge(z_ready, 1)
                    for m in clear:
                        with pool.Fori(0, m.shape[0] // P) as b:
                            pool.dma_start(m[ds(b * P, P), :], z[:]).then_inc(cleared, 16)

                def store(j, r, i):
                    for u in range(U):
                        pool.wait_ge(out_done, j * U + u + 9)
                        pool.dma_start(out(j, u), ob[r][:, u, :]).then_inc(stored, 16)
                    pool.wait_ge(stored, (j + 1) * (16 * U))
                    pool.sem_inc(ob_free, 1)
                ring_loop(pool, n_heads, store)
                if clear:
                    pool.wait_ge(cleared, 16 * sum(m.shape[0] // P for m in clear))
                if stats_out is not None:
                    for u in range(U):
                        pool.dma_start(stats_out(u), stat[:, u, :, :].rearrange("p h s -> p (h s)")) \
                            .then_inc(stat_done, 16)
                    pool.wait_ge(stat_done, 16 * U)

USED = ("x", "mem", "mem_ln_g", "mem_ln_b", "w_mem_kv", "router_w", "router_b", "na_w_in", "na_bias", "w_out",
        "ln_g", "ln_b", "exp_w_gate", "exp_w_up", "exp_w_down", "ml_w_in", "ml_conv_wT", "ml_conv_bP", "ml_w_qkv",
        "ml_gate_bT", "ml_norm_gP", "ml_skipP", "c_P", "w_ada_2", "b_ada_2", "g_norm_mix_2", "w_in_2", "g_q_lat_P",
        "g_kv_lat_P", "w_uq_L", "w_ukv_L", "positions_2", "inv_freq", "rel_tab", "pos_q", "pos_k", "band_mask", "w_out_2",
        "g_norm_ffn_2", "w_router_2", "w_gate_2", "w_up_2", "w_down_2", "g_final_2")


def consts(nc, ident, strict, ones, iota, pidx):
    with stage(nc, "consts") as st:
        it = st.sb("it", [P, P], I32)
        pi = st.sb("pi", [P, 1], I32)
        c_ready = st.sem("c_ready")
        with nc.Block() as block:

            @block.gpsimd
            def _(pool):
                nc.gpsimd.iota(it[:], [[1, P]], base=0, channel_multiplier=0)
                nc.gpsimd.iota(pi[:], [[0, 1]], base=0, channel_multiplier=1)
                nc.gpsimd.memset(ones[:], 1.0)
                nc.gpsimd.drain().then_inc(c_ready, 1)

            @block.vector
            def _(dve):
                dve.wait_ge(c_ready, 1)
                nc.vector.tensor_copy(iota[:], it[:])
                nc.vector.tensor_copy(pidx[:], pi[:])
                nc.vector.drain()
                nc.vector.tensor_scalar(ident[:], iota[:], pidx[:, 0:1], None, ALU.is_equal)
                nc.vector.tensor_scalar(strict[:], iota[:], pidx[:, 0:1], None, ALU.is_gt)


def route(nc, name, xT, x, router_w, router_b, sbr, strict, ones, iota, spill=None):
    posA, posB, wA, wB, blk_e = sbr
    with stage(nc, name) as st:
        E = N_EXP
        rw = st.sb("rw", [P, KD, E])
        rb = st.sb("rb", [P, E])
        loaded = st.sem("loaded")
        logit_ready, e_ready = st.sem("logit_ready"), st.sem("e_ready")
        m_ready, cum_ready = st.sem("m_ready"), st.sem("cum_ready")
        lg = st.ps("lg")
        cm = st.ps("cm")
        sc = st.sb("sc", [P, NT, E])
        bi = st.sb("bi", [P, NT, E])
        tmp = st.sb("tmp", [P, NT, E])
        pairs = st.sb("pairs", [P, NT * N_GRP])
        gs = st.sb("gs", [P, NT * N_GRP])
        g1 = st.sb("g1", [P, NT])
        taken = st.sb("taken", [P, NT])
        first = st.sb("first", [P, NT, N_GRP])
        rank_e = st.sb("rank_e", [P, NT, E])
        oh = [st.sb(f"oh{n}", [P, NT, E]) for n in range(2)]
        both = st.sb("both", [P, NT, E])
        wsum = st.sb("wsum", [P, NT])
        nb = st.sb("nb", [P, E])
        nb2 = st.sb("nb2", [P, E])
        nbt = st.sb("nbt", [P, E])
        pos = st.sb("pos", [P, NT, E])
        bl = st.sb("bl", [P, MOE_BLOCKS])
        with nc.Block() as block:

            @block.sync
            def _(sp):
                sp.dma_start(rw[:], router_w.rearrange("(k p) e -> p k e", p=P)).then_inc(loaded, 16)
                sp.dma_start(rb[:], bcast_rows(router_b)).then_inc(loaded, 16)

            @block.tensor
            def _(pe):
                pe.wait_ge(loaded, 32)
                for t in range(NT):
                    for k in range(KD):
                        mm = nc.tensor.matmul(lg[:, t * E:(t + 1) * E], xT[:, k, t * P:(t + 1) * P], rw[:, k, :],
                                              start=(k == 0), stop=(k == KD - 1))
                mm.then_inc(logit_ready, 1)
                pe.wait_ge(m_ready, 1)
                for t in range(NT):
                    for a in range(t):
                        nc.tensor.matmul(cm[:, t * E:(t + 1) * E], ones[:], both[:, a, :], start=(a == 0), stop=False)
                    nc.tensor.matmul(cm[:, t * E:(t + 1) * E], strict[:], both[:, t, :], start=(t == 0), stop=True)
                for t in range(NT):
                    mm = nc.tensor.matmul(cm[:, NT * E:(NT + 1) * E], ones[:], both[:, t, :],
                                          start=(t == 0), stop=(t == NT - 1))
                mm.then_inc(cum_ready, 1)

            @block.scalar
            def _(act):
                act.wait_ge(logit_ready, 1)
                nc.scalar.activation(sc[:].rearrange("p t e -> p (t e)"), lg[:, 0:NT * E], ACT.Exp,
                                     scale=-1.0).then_inc(e_ready, 1)

            @block.vector
            def _(dve):
                V = nc.vector
                V.drain()
                for e in range(E):
                    V.memset(rank_e[:, :, e:e + 1], float(E - e))
                dve.wait_ge(e_ready, 1)
                dve.wait_ge(loaded, 32)
                V.tensor_scalar(tmp[:], sc[:], 1.0, None, ALU.add)
                V.drain()
                V.reciprocal(sc[:], tmp[:])
                V.drain()
                for t in range(NT):
                    V.tensor_add(bi[:, t, :], sc[:, t, :], rb[:])
                V.drain()
                b4 = bi[:].rearrange("p t (g j) -> p (t g) j", j=EPG)
                pr = [(a, b) for a in range(EPG) for b in range(a + 1, EPG)]
                for n, (a, b) in enumerate(pr):
                    V.tensor_add(gs[:] if n == 0 else pairs[:], b4[:, :, a], b4[:, :, b])
                    V.drain()
                    if n:
                        V.tensor_max(gs[:], gs[:], pairs[:])
                        V.drain()
                gs3 = gs[:].rearrange("p (t g) -> p t g", g=N_GRP)
                V.tensor_reduce(g1[:], gs3, AX.X, ALU.max)
                V.memset(taken[:], 0.0)
                V.drain()
                for g in range(N_GRP):
                    V.tensor_tensor(first[:, :, g], gs3[:, :, g], g1[:], ALU.is_equal)
                    V.drain()
                    V.scalar_tensor_tensor(first[:, :, g], taken[:], 1.0, first[:, :, g], ALU.is_lt, ALU.mult)
                    V.drain()
                    V.tensor_add(taken[:], taken[:], first[:, :, g])
                    V.drain()
                for g in range(N_GRP):
                    for j in range(EPG):
                        e = g * EPG + j
                        V.tensor_mul(bi[:, :, e], bi[:, :, e], first[:, :, g])
                        V.tensor_scalar(tmp[:, :, e], first[:, :, g], 1.0, -NEG, ALU.subtract, ALU.mult)
                V.drain()
                V.tensor_add(bi[:], bi[:], tmp[:])
                V.drain()
                for n in range(2):
                    V.tensor_reduce(g1[:], bi[:], AX.X, ALU.max)
                    V.drain()
                    for t in range(NT):
                        V.scalar_tensor_tensor(tmp[:, t, :], bi[:, t, :], g1[:, t:t + 1], rank_e[:, t, :],
                                               ALU.is_equal, ALU.mult)
                    V.drain()
                    V.tensor_reduce(g1[:], tmp[:], AX.X, ALU.max)
                    V.drain()
                    for t in range(NT):
                        V.tensor_scalar(oh[n][:, t, :], tmp[:, t, :], g1[:, t:t + 1], None, ALU.is_equal)
                    V.drain()
                    if n == 0:
                        V.scalar_tensor_tensor(bi[:], oh[0][:], -1e38, bi[:], ALU.mult, ALU.add)
                        V.drain()
                V.tensor_add(both[:], oh[0][:], oh[1][:]).then_inc(m_ready, 1)
                for n, wt in ((0, wA), (1, wB)):
                    V.tensor_mul(tmp[:], oh[n][:], sc[:])
                    V.drain()
                    V.tensor_reduce(wt[:], tmp[:], AX.X, ALU.add)
                    V.drain()
                V.tensor_add(wsum[:], wA[:], wB[:])
                V.drain()
                V.reciprocal(wsum[:], wsum[:])
                V.drain()
                V.tensor_mul(wA[:], wA[:], wsum[:])
                V.tensor_mul(wB[:], wB[:], wsum[:])
                dve.wait_ge(cum_ready, 1)
                cnt = cm[:, NT * E:(NT + 1) * E]
                V.tensor_scalar(nb[:], cnt, 0.0, None, ALU.is_gt)
                for q in range(1, S // P):
                    V.drain()
                    V.tensor_scalar(nbt[:], cnt, float(q * P), None, ALU.is_gt)
                    V.drain()
                    V.tensor_add(nb[:], nb[:], nbt[:])
                V.drain()
                V.tensor_copy(nbt[:], nb[:])
                V.drain()
                a, b = nb, nb2
                for sh in (1, 2, 4, 8):
                    V.tensor_copy(b[:, 0:sh], a[:, 0:sh])
                    V.tensor_add(b[:, sh:E], a[:, sh:E], a[:, 0:E - sh])
                    V.drain()
                    a, b = b, a
                V.tensor_sub(nbt[:], a[:], nbt[:])
                V.memset(bl[:], 0.0)
                V.drain()
                for t in range(NT):
                    V.scalar_tensor_tensor(pos[:, t, :], nbt[:], float(P), cm[:, t * E:(t + 1) * E],
                                           ALU.mult, ALU.add)
                for e in range(E):
                    V.scalar_tensor_tensor(bl[:], iota[:, 0:MOE_BLOCKS], a[:, e:e + 1], bl[:], ALU.is_ge, ALU.add)
                    V.drain()
                V.tensor_scalar(bl[:], bl[:], float(E - 1), None, ALU.min)
                V.drain()
                V.tensor_copy(blk_e[:, 0:MOE_BLOCKS], bl[:])
                V.drain()
                V.tensor_scalar(bl[:, 0:MOE_BLOCKS // 2], iota[:, 0:MOE_BLOCKS // 2], 2.0, a[:, E - 1:E],
                                ALU.mult, ALU.is_lt)
                V.drain()
                V.tensor_reduce(nb2[:, 0:1] if a is nb else nb[:, 0:1], bl[:, 0:MOE_BLOCKS // 2], AX.X, ALU.add)
                V.drain()
                V.tensor_copy(blk_e[:, MOE_BLOCKS:MOE_BLOCKS + 1], nb2[:, 0:1] if a is nb else nb[:, 0:1])
                for n, pt in ((0, posA), (1, posB)):
                    V.tensor_mul(tmp[:], oh[n][:], pos[:])
                    V.drain()
                    V.tensor_reduce(pt[:], tmp[:], AX.X, ALU.add)
                    V.drain()


def scatter_rows(nc, name, x, sbr, slots_dram):
    posA, posB, wA, wB, blk_e = sbr
    with stage(nc, name) as st:
        idx = [st.sb(f"idx{n}", [P, NT], U32) for n in range(2)]
        idx_ready, put = st.sem("idx_ready"), st.sem("put")
        with nc.Block() as block:

            @block.vector
            def _(dve):
                nc.vector.tensor_copy(idx[0][:], posA[:])
                nc.vector.tensor_copy(idx[1][:], posB[:])
                nc.vector.drain().then_inc(idx_ready, 1)

            @block.gpsimd
            def _(pool):
                pool.wait_ge(idx_ready, 1)
                for t in range(NT):
                    for n in range(2):
                        pool.indirect_dma_start(out=slots_dram, in_=x[:, t, :], in_offset=None,
                                                out_offset=bass.IndirectOffsetOnAxis(ap=idx[n][:, t:t + 1], axis=0)) \
                            .then_inc(put, 16)
                pool.wait_ge(put, 16 * 2 * NT)


def moe_experts(nc, name, ident, sbr, slots_dram, w_gate, w_up, w_down, y_dram):
    blk_e = sbr[4]
    KF = D_EXP // P
    with stage(nc, name) as st:
        w = [[st.sb(f"w{n}{r}", [P, KD * D_EXP]) for r in range(2)] for n in range(3)]
        w_ready = [[st.sem(f"w_ready{n}{r}") for r in range(2)] for n in range(3)]
        xs = [st.sb(f"xs{r}", [P, D]) for r in range(2)]
        xs_ready = [st.sem(f"xs_ready{r}") for r in range(2)]
        xg = [st.sb(f"xg{r}", [P, KD * P]) for r in range(2)]
        sig = st.sb("sig", [P, D_EXP])
        hid = [st.sb(f"hid{r}", [P, D_EXP]) for r in range(2)]
        hT = [st.sb(f"hT{r}", [P, KF * P]) for r in range(2)]
        yb = [st.sb(f"y{r}", [P, D]) for r in range(2)]
        x_ps = [st.ps(f"x_ps{r}") for r in range(2)]
        h_ps = [st.ps(f"h_ps{r}") for r in range(2)]
        g_ps, u_ps = st.ps("g_ps"), st.ps("u_ps")
        y_ps = [st.ps(f"y_ps{r}") for r in range(2)]
        turned = st.sem("turned")
        xg_copied = st.sem("xg_copied")
        g_free = st.sem("g_free")
        gate_ready, up_ready, sig_ready = st.sem("gate_ready"), st.sem("up_ready"), st.sem("sig_ready")
        hid_ready = st.sem("hid_ready")
        hT_ps_ready = st.sem("hT_ps_ready")
        hT_ready = st.sem("hT_ready")
        down_ready = st.sem("down_ready")
        y_copied = st.sem("y_copied")
        stored, yb_free = st.sem("stored"), st.sem("yb_free")

        def pairs(eng):
            return eng.value_load(blk_e[0:1, MOE_BLOCKS:MOE_BLOCKS + 1], min_val=1, max_val=MOE_BLOCKS // 2)

        with nc.Block() as block:

            @block.sync
            def _(sp):
                with sp.Fori(0, pairs(sp)) as i:
                    for r in range(2):
                        b = 2 * i + r
                        e = sp.value_load(blk_e[0:1, ds(b, 1)], min_val=0, max_val=N_EXP - 1)
                        sp.wait_ge(hid_ready, b + 1)
                        sp.dma_start(xs[r][:], slots_dram[ds(b * P, P), :]).then_inc(xs_ready[r], 16)
                        for n, src in enumerate((w_gate, w_up)):
                            sp.dma_start(w[n][r][:], src[ds(e, 1)].rearrange("a (k p) n -> p (a k) n", p=P)) \
                                .then_inc(w_ready[n][r], 16)
                        sp.wait_ge(down_ready, 2 * b + 2)
                        sp.dma_start(w[2][r][:], w_down[ds(e, 1)].rearrange("a (k p) n -> p (a k) n", p=P)) \
                            .then_inc(w_ready[2][r], 16)

            @block.tensor
            def _(pe):
                with pe.Fori(0, pairs(pe)) as i:
                    def turn_x(r):
                        pe.wait_ge(xs_ready[r], 16 * i + 16)
                        for h in range(2):
                            pe.wait_ge(xg_copied, 2 * (2 * i + r) + h + 1)
                            for c in range(4):
                                cc = h * 4 + c
                                mm = nc.tensor.transpose(x_ps[h][:, c * P:(c + 1) * P],
                                                         xs[r][:, cc * P:(cc + 1) * P], ident[:])
                            mm.then_inc(turned, 1)

                    def product(r, n, ps, done):
                        pe.wait_ge(w_ready[n][r], 16 * i + 16)
                        for k in range(KD):
                            mm = nc.tensor.matmul(ps[:], xg[r][:, k * P:(k + 1) * P],
                                                  w[n][r][:, k * D_EXP:(k + 1) * D_EXP],
                                                  start=(k == 0), stop=(k == KD - 1))
                        mm.then_inc(done, 1)

                    def gate(r):
                        b = 2 * i + r
                        pe.wait_ge(xg_copied, 2 * b + 4)
                        pe.wait_ge(g_free, b + 1)
                        product(r, 0, g_ps, gate_ready)

                    def up(r):
                        pe.wait_ge(hid_ready, 2 * i + r + 2)
                        product(r, 1, u_ps, up_ready)

                    def turn_h(r):
                        b = 2 * i + r
                        pe.wait_ge(hid_ready, b + 3)
                        pe.wait_ge(hT_ready, b + 1)
                        for f in range(KF):
                            mm = nc.tensor.transpose(h_ps[r][:, f * P:(f + 1) * P], hid[r][:, f * P:(f + 1) * P],
                                                     ident[:])
                        mm.then_inc(hT_ps_ready, 1)

                    def down(r):
                        b = 2 * i + r
                        pe.wait_ge(hT_ready, b + 3)
                        pe.wait_ge(w_ready[2][r], 16 * i + 16)
                        for h in range(2):
                            pe.wait_ge(y_copied, 2 * b + h + 1)
                            for f in range(KF):
                                mm = nc.tensor.matmul(y_ps[h][:], hT[r][:, f * P:(f + 1) * P],
                                                      w[2][r][:, f * D + h * 512:f * D + (h + 1) * 512],
                                                      start=(f == 0), stop=(f == KF - 1))
                            mm.then_inc(down_ready, 1)
                    turn_x(0)
                    gate(0)
                    turn_x(1)
                    up(0)
                    gate(1)
                    turn_h(0)
                    up(1)
                    down(0)
                    turn_h(1)
                    down(1)

            @block.vector
            def _(dve):
                V = nc.vector
                dve.sem_inc(hid_ready, 2)
                dve.sem_inc(g_free, 1)
                with dve.Fori(0, pairs(dve)) as i:
                    def hidden(r):
                        b = 2 * i + r
                        dve.wait_ge(sig_ready, b + 1)
                        V.tensor_mul(hid[r][:], sig[:], g_ps[:]).then_inc(g_free, 1)
                        V.drain()
                        dve.wait_ge(up_ready, b + 1)
                        V.tensor_mul(hid[r][:], hid[r][:], u_ps[:]).then_inc(hid_ready, 1)

                    def turn(r):
                        dve.wait_ge(hT_ps_ready, 2 * i + r + 1)
                        dve.wait_ge(down_ready, 2 * (2 * i + r) + 2)
                        V.tensor_copy(hT[r][:], h_ps[r][:]).then_inc(hT_ready, 1)
                    hidden(0)
                    turn(0)
                    hidden(1)
                    turn(1)

            @block.scalar
            def _(act):
                act.sem_inc(xg_copied, 2)
                act.sem_inc(hT_ready, 2)
                act.sem_inc(down_ready, 4)
                act.sem_inc(y_copied, 2)
                act.sem_inc(yb_free, 2)
                with act.Fori(0, pairs(act)) as i:
                    def copy_x(r):
                        for h in range(2):
                            act.wait_ge(turned, 2 * (2 * i + r) + h + 1)
                            nc.scalar.activation(xg[r][:, h * 512:(h + 1) * 512], x_ps[h][:],
                                                 ACT.Copy).then_inc(xg_copied, 1)

                    def sigmoid(r):
                        b = 2 * i + r
                        act.wait_ge(gate_ready, b + 1)
                        act.wait_ge(g_free, b + 1)
                        nc.scalar.activation(sig[:], g_ps[:], ACT.Sigmoid).then_inc(sig_ready, 1)
                    copy_x(0)
                    sigmoid(0)
                    copy_x(1)
                    sigmoid(1)
                    for r in range(2):
                        b = 2 * i + r
                        act.wait_ge(yb_free, b + 1)
                        for h in range(2):
                            act.wait_ge(down_ready, 2 * b + h + 5)
                            nc.scalar.activation(yb[r][:, h * 512:(h + 1) * 512], y_ps[h][:],
                                                 ACT.Copy).then_inc(y_copied, 1)

            @block.gpsimd
            def _(pool):
                with pool.Fori(0, pairs(pool)) as i:
                    for r in range(2):
                        b = 2 * i + r
                        pool.wait_ge(y_copied, 2 * b + 4)
                        pool.dma_start(y_dram[ds(b * P, P), :], yb[r][:]).then_inc(stored, 16)
                        pool.wait_ge(stored, 16 * b + 16)
                        pool.sem_inc(yb_free, 1)


def moe_combine(nc, name, sbr, y_dram, out_dram):
    posA, posB, wA, wB, blk_e = sbr
    with stage(nc, name) as st:
        idx = [st.sb(f"idx{n}", [P, NT], U32) for n in range(2)]
        row = [[st.sb(f"row{n}{t}", [P, D]) for t in range(NT)] for n in range(2)]
        idx_ready, got, done, stored = st.sem("idx_ready"), st.sem("got"), st.sem("done"), st.sem("stored")
        with nc.Block() as block:

            @block.vector
            def _(dve):
                nc.vector.tensor_copy(idx[0][:], posA[:])
                nc.vector.tensor_copy(idx[1][:], posB[:])
                nc.vector.drain().then_inc(idx_ready, 1)
                dve.wait_ge(got, 16 * 2 * NT)
                for t in range(NT):
                    nc.vector.tensor_scalar(row[0][t][:], row[0][t][:], wA[:, t:t + 1], None, ALU.mult)
                nc.vector.drain()
                for t in range(NT):
                    nc.vector.scalar_tensor_tensor(row[0][t][:], row[1][t][:], wB[:, t:t + 1], row[0][t][:],
                                                   ALU.mult, ALU.add).then_inc(done, 1)

            @block.gpsimd
            def _(pool):
                pool.wait_ge(idx_ready, 1)
                for t in range(NT):
                    for n in range(2):
                        pool.indirect_dma_start(out=row[n][t][:], out_offset=None, in_=y_dram,
                                                in_offset=bass.IndirectOffsetOnAxis(ap=idx[n][:, t:t + 1], axis=0)) \
                            .then_inc(got, 16)

            @block.sync
            def _(sp):
                for t in range(NT):
                    sp.wait_ge(done, t + 1)
                    sp.dma_start(out_dram[t * P:(t + 1) * P, :], row[0][t][:]).then_inc(stored, 16)
                sp.wait_ge(stored, 16 * NT)


def first_inputs_stage(nc, x, x_dram):
    with stage(nc, "load_x") as st:
        x_in = st.sem("x_in")
        with nc.Block() as block:

            @block.sync
            def _(sp):
                sp.dma_start(x[:], x_dram.rearrange("(t p) d -> p t d", p=P)).then_inc(x_in, 16)
                sp.wait_ge(x_in, 16)


def moe_layer(nc, i, a, x, xT, cst, slots, y_dram, f_dram, sbr):
    ident, strict, ones, iota, pidx = cst
    route(nc, f"route{i}", xT, x, a["router_w"], a["router_b"], sbr, strict, ones, iota)
    scatter_rows(nc, f"scat{i}", x, sbr, slots)
    moe_experts(nc, f"moe{i}", ident, sbr, slots, a["exp_w_gate"][i], a["exp_w_up"][i], a["exp_w_down"][i], y_dram)
    moe_combine(nc, f"comb{i}", sbr, y_dram, f_dram)


def memory_attention(nc, name, ident, q_dram, mk_dram, mv_dram, mix):
    attention(nc, name, ident, MEM_HEADS, MEM_DH, MEM_DH, N_MEM,
              lambda h: [q_dram[ds(h * MEM_DH, MEM_DH), :]],
              lambda h: [mk_dram[ds(h * MEM_DH, MEM_DH), :]],
              lambda h: [((slice(None), slice(0, 2), slice(None)),
                          mv_dram.rearrange("(c p) f -> p c f", p=P)[:, :, ds(h * MEM_DH, MEM_DH)])],
              lambda q, u: q[:, u * P:(u + 1) * P], lambda k, u: k[:, :], lambda u: (0, 1),
              lambda h, u: mix[u * P:(u + 1) * P, ds(NA_W + h * MEM_DH, MEM_DH)],
              MEM_DH ** -0.5, n_keys=N_MEM, v_chunks=2)


def build(nc, a, out):
    def dram(name, shape, dt=F32):
        return nc.dram_tensor(name, list(shape), dt, kind="Internal").ap()

    with ExitStack() as ctx:
        def sb(name, shape, dt=F32):
            return ctx.enter_context(nc.sbuf_tensor(name, list(shape), dt))

        x, xT = sb("x", [P, NT, D]), sb("xT", [P, KD, S])
        ident, strict, ones, iota = (sb(n, [P, P]) for n in ("ident", "strict", "ones", "iota"))
        pidx = sb("pidx", [P, 1])
        sbr = [sb(n, [P, NT]) for n in ("posA", "posB", "wA", "wB")] + [sb("blk_e", [P, MOE_BLOCKS + 1], I32)]
        cst = (ident, strict, ones, iota, pidx)
        consts(nc, *cst)

        mk, mv = dram("mk", [MEM_W, N_MEM]), dram("mv", [N_MEM, MEM_W])
        norm(nc, "mem_ln", a["mem"][0], x, xT, ident, LN_EPS, False, a["mem_ln_g"], a["mem_ln_b"], n_tiles=N_MEM // P)
        gemms(nc, "mem_kv", [job(a["w_mem_kv"], 0, 1, MEM_W, xT, P, N_MEM, mk, "T"),
                             job(a["w_mem_kv"], MEM_W, 1, MEM_W, xT, P, N_MEM, mv, "N")])
        mod0, mod = dram("mod0", [1, 6 * D]), dram("mod", [6 * D])
        biases = [dram("bias0", [DIL_H * 4 * UNIT0])] + [dram(f"bias{g}", [DIL_H, P, 4 * P]) for g in (1, 2)]
        condT = sb("condT", [P, KD, 1])
        condition(nc, a, condT[:, :, 0])

        load_transposed(nc, "x_in", a["x"][0], xT, ident)
        first_inputs_stage(nc, x, a["x"][0])
        naq, nak, nav = dram("naq", [NA_W, S]), dram("nak", [NA_W, S]), dram("nav", [S, NA_W])
        memq = dram("memq", [MEM_W, S])
        mix = dram("mix", [S, D])
        win = a["na_w_in"][0]
        slots, y_dram = dram("x_slots", [MOE_BLOCKS * P, D]), dram("y_slots", [MOE_BLOCKS * P, D])
        by_cb = lambda ap: ap.rearrange("p (r b c) -> p b r c", r=ROWS, c=WIN_W)
        gemms(nc, "proj0", [job(win, 0, 2, 384, xT, P, S, naq, "T", tok=by_cb),
                            job(win, NA_W, 2, 384, xT, P, S, nak, "T"),
                            job(win, 2 * NA_W, 2, 384, xT, P, S, nav, "N"),
                            job(win, 3 * NA_W, 1, MEM_W, xT, P, S, memq, "T"),
                            job(a["w_ada_2"][0], 0, 12, 512, condT, P, 1, mod0, "N")],
              side=lambda st: RelativeBias(nc, a, biases, (2,), st))
        add_rows(nc, "ada_b", mod0[0], a["b_ada_2"][0], mod, 96)
        start = [min(max(b * WIN_W - WIN_W // 2, 0), GRID_W - SPAN) for b in range(N_CB)]
        nav_rc = nav.rearrange("(r c) f -> r c f", c=GRID_W)
        mix_rc = mix.rearrange("(r c) f -> r c f", c=GRID_W)
        attention(nc, "na", ident, NA_HEADS, NA_DH, NA_DH, ROWS * SPAN,
                  lambda h: [naq[ds(h * NA_DH, NA_DH), :]],
                  lambda h: [nak[ds(h * NA_DH, NA_DH), :]],
                  lambda h: [],
                  lambda q, u: q[:, u * P:(u + 1) * P],
                  lambda k, u: k[:, :].rearrange("p (r c) -> p r c", c=GRID_W)[:, :, start[u]:start[u] + SPAN],
                  lambda u: (2 * u, 2 * u + 1),
                  lambda h, u: mix_rc[:, u * WIN_W:(u + 1) * WIN_W, ds(h * NA_DH, NA_DH)],
                  NA_DH ** -0.5, bias_src=lambda h: a["na_bias"].rearrange("h p n -> p h n")[:, ds(h, 1), :],
                  v_chunks=8, clear=(slots, y_dram),
                  v_once=[((slice(None), 2 * b + half, slice(None)),
                           nav_rc[4 * half:4 * half + 4, start[b]:start[b] + SPAN, :])
                          for b in range(N_CB) for half in range(2)])
        memory_attention(nc, "mem0", ident, memq, mk, mv, mix)
        proj = dram("proj", [S, D])
        load_transposed(nc, "mixT0", mix, xT, ident)
        gemm(nc, "out0", a["w_out"][0], 0, 2, 512, xT, P, S, proj, "N")
        norm(nc, "ln00", x, x, xT, ident, LN_EPS, False, a["ln_g"][0, 0], a["ln_b"][0, 0], resid=proj, alpha=ALPHA)
        moe_layer(nc, 0, a, x, xT, cst, slots, y_dram, proj, sbr)
        norm(nc, "ln01", x, x, xT, ident, LN_EPS, False, a["ln_g"][0, 1], a["ln_b"][0, 1], resid=proj, alpha=ALPHA)
        first_block_rest(nc, a, x, xT, cst, mk, mv, mix, memq, proj, slots, y_dram, sbr, dram)
        second_block(nc, a, x, xT, cst, mod, biases, out, dram)


HC = ML_DH // 96
NC96 = ML_W // 96


def mlstm_conv(nc, a, xm_dram, z_dram, xm, xc, zs):
    with stage(nc, "conv") as st:
        cw = st.sb("cw", [96, NC96, CONV_K])
        cb = st.sb("cb", [96, NC96])
        sg = st.sb("sg", [96, NC96, S])
        ld, zld = st.sem("ld"), st.sem("zld")
        pre_ready, sig_ready, z_ready = st.sem("pre_ready"), st.sem("sig_ready"), st.sem("z_ready")
        pad = CONV_K // 2
        with nc.Block() as block:

            @block.sync
            def _(sp):
                sp.dma_start(xm[:, :, pad:pad + S], xm_dram.rearrange("(c p) t -> p c t", p=96)).then_inc(ld, 16)
                sp.dma_start(cw[:], a["ml_conv_wT"].rearrange("(c p) k -> p c k", p=96)).then_inc(ld, 16)
                sp.dma_start(cb[:], a["ml_conv_bP"]).then_inc(ld, 16)
                sp.dma_start(zs[:], z_dram.rearrange("(c p) t -> p c t", p=96)).then_inc(zld, 16)

            @block.vector
            def _(dve):
                V = nc.vector
                V.memset(xm[:, :, 0:pad], 0.0)
                V.memset(xm[:, :, pad + S:], 0.0)
                dve.wait_ge(ld, 48)
                V.drain()
                for k in range(CONV_K):
                    for c in range(NC96):
                        src = xm[:, c, k:k + S]
                        if k == 0:
                            V.tensor_scalar(xc[:, c, :], src, cw[:, c, k:k + 1], cb[:, c:c + 1], ALU.mult, ALU.add)
                        else:
                            last = V.scalar_tensor_tensor(xc[:, c, :], src, cw[:, c, k:k + 1], xc[:, c, :],
                                                          ALU.mult, ALU.add)
                    if k < CONV_K - 1:
                        V.drain()
                last.then_inc(pre_ready, 1)
                dve.wait_ge(sig_ready, 1)
                V.tensor_mul(xc[:], xc[:], sg[:])
                V.drain().then_inc(pre_ready, 1)
                dve.wait_ge(z_ready, 1)
                V.tensor_mul(zs[:], zs[:], sg[:])

            @block.scalar
            def _(act):
                act.wait_ge(pre_ready, 1)
                nc.scalar.activation(sg[:], xc[:], ACT.Sigmoid).then_inc(sig_ready, 1)
                act.wait_ge(zld, 16)
                act.wait_ge(pre_ready, 2)
                nc.scalar.activation(sg[:], zs[:], ACT.Sigmoid).then_inc(z_ready, 1)


def mlstm_gates(nc, a, xT, ident, ones, pidx, neg_m, diag_m, a_tok, e_tok):
    with stage(nc, "gates") as st:
        NH = ML_HEADS
        wg = st.sb("wg", [P, KD, 16])
        gb = st.sb("gb", [NH, 4])
        G = st.sb("G", [NH, 4, S])
        ab = st.sb("ab", [NH, S])
        buf = [st.sb(f"buf{n}", [NH, 2, S]) for n in range(2)]
        av = st.sb("av", [NH, 2, S])
        nm = st.sb("nm", [NH, 2, S])
        bv = st.sb("bv", [NH, 2, S])
        sel = st.sb("sel", [NH, NH, P])
        mask = st.sb("mask", [P, 2, P])
        zero = st.sb("zero", [P, P])
        ld, g_ready, f_ready, l_ready = st.sem("ld"), st.sem("g_ready"), st.sem("f_ready"), st.sem("l_ready")
        e_ready = st.sem("e_ready")
        rows_ready, tr_ready, bc_ready, bc_free = (st.sem("rows_ready"), st.sem("tr_ready"), st.sem("bc_ready"),
                                                   st.sem("bc_free"))
        z_ready, mask_ready = st.sem("z_ready"), st.sem("mask_ready")
        g_ps = [st.ps(f"g{n}") for n in range(4)]
        t_ps = st.ps("t")
        b_ps = [st.ps(f"b{n}") for n in range(2)]
        with nc.Block() as block:

            @block.sync
            def _(sp):
                sp.dma_start(wg[:], a["ml_w_in"][0].rearrange("(k p) n -> p k n", p=P)[:, :, 2 * ML_W:2 * ML_W + 16]) \
                    .then_inc(ld, 16)
                sp.dma_start(gb[:], a["ml_gate_bT"]).then_inc(ld, 16)

            @block.gpsimd
            def _(pool):
                nc.gpsimd.memset(zero[:], 0.0)
                nc.gpsimd.drain()
                nc.gpsimd.affine_select(out=mask[:, 0, :], in_=zero[:], pattern=[[1, P]], compare_op=ALU.is_ge,
                                        fill=NEG, base=0, channel_multiplier=-1)
                nc.gpsimd.affine_select(out=mask[:, 1, :], in_=zero[:], pattern=[[-1, P]], compare_op=ALU.is_ge,
                                        fill=NEG, base=0, channel_multiplier=1)
                nc.gpsimd.drain().then_inc(mask_ready, 1)

            @block.tensor
            def _(pe):
                pe.wait_ge(ld, 32)
                for g in range(4):
                    for k in range(KD):
                        mm = nc.tensor.matmul(g_ps[g][0:NH, :], wg[:, k, g * NH:(g + 1) * NH], xT[:, k, :],
                                              start=(k == 0), stop=(k == KD - 1))
                mm.then_inc(g_ready, 1)
                pe.wait_ge(rows_ready, 1)
                for n, src in enumerate((av, nm)):
                    for d in range(2):
                        for t in range(NT):
                            c = ((n * 2 + d) * NT + t) * NH
                            mm = nc.tensor.transpose(t_ps[:, c:c + NH], src[:, d, t * P:(t + 1) * P],
                                                     ident[0:NH, 0:NH])
                mm.then_inc(tr_ready, 1)
                pe.wait_ge(rows_ready, 2)
                for d in range(2):
                    for h in range(NH):
                        n = d * NH + h
                        pe.wait_ge(bc_free, n + 1)
                        nc.tensor.matmul(b_ps[n % 2][:], sel[:, h, :], buf[1][:, d, :], start=True, stop=True) \
                            .then_inc(bc_ready, 1)

            @block.scalar
            def _(act):
                act.wait_ge(f_ready, 1)
                for d in range(2):
                    act.wait_ge(f_ready, d + 1)
                    nc.scalar.activation(ab[:], ab[:], ACT.Exp, scale=-1.0)
                    nc.scalar.drain()
                    nc.scalar.activation(ab[:], ab[:], ACT.Ln, bias=1.0).then_inc(l_ready, 1)
                act.wait_ge(tr_ready, 1)
                n = 2 * NT * NH
                nc.scalar.activation(a_tok[:], t_ps[:, 0:n], ACT.Copy)
                nc.scalar.activation(e_tok[:], t_ps[:, n:2 * n], ACT.Exp)

            @block.vector
            def _(dve):
                V = nc.vector
                dve.sem_inc(bc_free, 2)
                for h in range(NH):
                    V.tensor_scalar(sel[:, h, :], ones[0:NH, :], pidx[0:NH, 0:1], float(h), ALU.mult, ALU.is_equal)
                dve.wait_ge(g_ready, 1)
                for g in range(4):
                    V.tensor_scalar(G[:, g, :], g_ps[g][0:NH, :], gb[:, g:g + 1], None, ALU.add)
                V.drain()
                for d in range(2):
                    f = G[:, 2 * d + 1, :]
                    V.scalar_tensor_tensor(ab[:], f, -1.0, f, ALU.mult, ALU.max)
                    V.drain().then_inc(f_ready, 1)
                    dve.wait_ge(l_ready, d + 1)
                    V.scalar_tensor_tensor(buf[0][:, d, :], f, 0.0, ab[:], ALU.min, ALU.subtract)
                    V.drain()

                def running(op, src, dst):
                    s, d_, sh = src, dst, 1
                    while sh < S:
                        o = V.tensor_add if op == "add" else V.tensor_max
                        V.tensor_copy(d_[:, 0, 0:sh], s[:, 0, 0:sh])
                        o(d_[:, 0, sh:S], s[:, 0, sh:S], s[:, 0, 0:S - sh])
                        V.tensor_copy(d_[:, 1, S - sh:S], s[:, 1, S - sh:S])
                        o(d_[:, 1, 0:S - sh], s[:, 1, 0:S - sh], s[:, 1, sh:S])
                        V.drain()
                        s, d_, sh = d_, s, sh * 2
                    return s

                res = running("add", buf[0], buf[1])
                V.tensor_copy(bv[:], res[:])
                for d in range(2):
                    V.tensor_sub(av[:, d, :], G[:, 2 * d, :], res[:, d, :])
                V.drain()
                V.tensor_scalar(buf[0][:], av[:], 0.0, None, ALU.max)
                V.drain()
                res = running("max", buf[0], buf[1])
                V.drain()
                V.scalar_tensor_tensor(nm[:], bv[:], -1.0, res[:], ALU.mult, ALU.subtract).then_inc(rows_ready, 1)
                V.drain()
                V.tensor_scalar(buf[1][:], res[:], -1.0, None, ALU.mult).then_inc(rows_ready, 1)
                dve.wait_ge(mask_ready, 1)
                for d in range(2):
                    for h in range(NH):
                        n = d * NH + h
                        dve.wait_ge(bc_ready, n + 1)
                        V.tensor_copy(neg_m[:, n, :], b_ps[n % 2][:])
                        for t in range(NT):
                            last = V.tensor_add(diag_m[:, n, t * P:(t + 1) * P], b_ps[n % 2][:, t * P:(t + 1) * P],
                                                mask[:, d, :])
                        last.then_inc(bc_free, 1)


def mlstm_qkv(nc, a, xm, xc, q, k, v):
    with stage(nc, "qkv") as st:
        NH = ML_HEADS
        w = st.sb("w", [96, 3 * NH * HC, ML_DH])
        ld, ready, free = st.sem("ld"), st.sem("ready"), st.sem("free")
        ps = [st.ps(f"ps{n}") for n in range(4)]
        pad = CONV_K // 2
        with nc.Block() as block:

            @block.sync
            def _(sp):
                sp.dma_start(w[:], a["ml_w_qkv"][0].rearrange("s h (c p) e -> p (s h c) e", p=96)).then_inc(ld, 16)

            @block.tensor
            def _(pe):
                pe.wait_ge(ld, 16)
                n = 0
                for s in range(2):
                    for h in range(NH):
                        for g in range(HC):
                            pe.wait_ge(free, n + 1)
                            for c in range(HC):
                                mm = nc.tensor.matmul(ps[n % 4][0:96, :],
                                                      w[:, (s * NH + h) * HC + c, g * 96:(g + 1) * 96],
                                                      xc[:, h * HC + c, :], start=(c == 0), stop=(c == HC - 1))
                            mm.then_inc(ready, 1)
                            n += 1
                for h in range(NH):
                    for t in range(NT):
                        pe.wait_ge(free, n + 1)
                        for c in range(HC):
                            mm = nc.tensor.matmul(ps[n % 4][:, 0:ML_DH],
                                                  xm[:, h * HC + c, pad + t * P:pad + (t + 1) * P],
                                                  w[:, (2 * NH + h) * HC + c, :], start=(c == 0), stop=(c == HC - 1))
                        mm.then_inc(ready, 1)
                        n += 1

            @block.scalar
            def _(act):
                act.sem_inc(free, 4)
                n = 0
                for dst, scale in ((q, 1.0), (k, ML_DH ** -0.5)):
                    for c in range(NH * HC):
                        act.wait_ge(ready, n + 1)
                        nc.scalar.activation(dst[:, c, :], ps[n % 4][0:96, :], ACT.Copy, scale=scale).then_inc(free, 1)
                        n += 1
                for h in range(NH):
                    for t in range(NT):
                        act.wait_ge(ready, n + 1)
                        nc.scalar.activation(v[:, t, h, 0:ML_DH], ps[n % 4][:, 0:ML_DH], ACT.Copy).then_inc(free, 1)
                        n += 1

            @block.vector
            def _(dve):
                for t in range(NT):
                    nc.vector.memset(v[:, t, :, ML_DH:ML_DH + 1], 1.0)


def mlstm_scan(nc, q, k, v, neg_m, diag_m, a_tok, e_tok, hs):
    NH = ML_HEADS
    combos = [(d, h) for d in range(2) for h in range(NH)]
    tiles = [[(s, s, NT) for s in range(NT)], [(s, 0, s + 1) for s in range(NT)]]
    units = [(n, d, h, s, lo, hi) for n, (d, h) in enumerate(combos) for (s, lo, hi) in tiles[d]]
    with stage(nc, "scan") as st:
        dec = [st.sb(f"dec{r}", [P, S]) for r in range(2)]
        wt = [st.sb(f"wt{r}", [P, S]) for r in range(2)]
        rd = st.sb("rd", [P, NT])
        rd2 = st.sb("rd2", [P, NT])
        s_ps = [st.ps(f"s{r}") for r in range(2)]
        n_ps = [st.ps(f"n{t}") for t in range(NT)]
        s_ready, dec_ready, wt_ready = st.sem("s_ready"), st.sem("dec_ready"), st.sem("wt_ready")
        wt_free, num_ready, num_free = st.sem("wt_free"), st.sem("num_ready"), st.sem("num_free")
        with nc.Block() as block:

            @block.tensor
            def _(pe):
                def scores(m):
                    n, d, h, s, lo, hi = units[m]
                    pe.wait_ge(wt_ready, m + 1)
                    for c in range(HC):
                        mm = nc.tensor.matmul(s_ps[m % 2][:, 0:(hi - lo) * P],
                                              k[:, h * HC + c, s * P:(s + 1) * P],
                                              q[:, h * HC + c, lo * P:hi * P], start=(c == 0), stop=(c == HC - 1))
                    mm.then_inc(s_ready, 1)
                scores(0)
                for m, (n, d, h, s, lo, hi) in enumerate(units):
                    if m + 1 < len(units):
                        scores(m + 1)
                    pe.wait_ge(wt_ready, m + 3)
                    if s == 0:
                        pe.wait_ge(num_free, n + 1)
                    for t in range(lo, hi):
                        first = s == 0 if d == 0 else s == t
                        last = s == t if d == 0 else s == NT - 1
                        mm = nc.tensor.matmul(n_ps[t][:, 0:ML_DH + 1], wt[m % 2][:, (t - lo) * P:(t - lo + 1) * P],
                                              v[:, s, h, :], start=first, stop=last)
                    mm.then_inc(wt_free, 1)

            @block.scalar
            def _(act):
                act.sem_inc(wt_ready, 2)
                for m, (n, d, h, s, lo, hi) in enumerate(units):
                    act.wait_ge(wt_ready, m + 1)
                    bias = a_tok[:, (d * NT + s) * NH + h:(d * NT + s) * NH + h + 1]
                    x0 = (s - lo) * P
                    last = nc.scalar.activation(dec[m % 2][:, x0:x0 + P], diag_m[:, n, s * P:(s + 1) * P], ACT.Exp,
                                                bias=bias)
                    if d == 0 and s < NT - 1:
                        last = nc.scalar.activation(dec[m % 2][:, P:(hi - lo) * P], neg_m[:, n, (s + 1) * P:S],
                                                    ACT.Exp, bias=bias)
                    if d == 1 and s > 0:
                        last = nc.scalar.activation(dec[m % 2][:, 0:s * P], neg_m[:, n, 0:s * P], ACT.Exp, bias=bias)
                    last.then_inc(dec_ready, 1)

            @block.vector
            def _(dve):
                V = nc.vector
                dve.sem_inc(wt_free, 2)
                dve.sem_inc(num_free, 1)

                def outputs(n, d, h):
                    dve.wait_ge(wt_free, NT * (n + 1) + 2)
                    for t in range(NT):
                        V.tensor_copy(rd[:, t:t + 1], n_ps[t][:, ML_DH:ML_DH + 1])
                    V.drain()
                    V.scalar_tensor_tensor(rd2[:], rd[:], -1.0, rd[:], ALU.mult, ALU.max)
                    V.drain()
                    for t in range(NT):
                        c = (d * NT + t) * NH + h
                        V.tensor_max(rd[:, t:t + 1], rd2[:, t:t + 1], e_tok[:, c:c + 1])
                    V.drain()
                    V.reciprocal(rd2[:], rd[:])
                    V.drain()
                    for t in range(NT):
                        o = hs[:, t, h * ML_DH:(h + 1) * ML_DH]
                        if d == 0:
                            last = V.tensor_scalar(o, n_ps[t][:, 0:ML_DH], rd2[:, t:t + 1], None, ALU.mult)
                        else:
                            last = V.scalar_tensor_tensor(o, n_ps[t][:, 0:ML_DH], rd2[:, t:t + 1], o,
                                                          ALU.mult, ALU.add)
                    last.then_inc(num_free, 1)
                    V.drain()

                for m, (n, d, h, s, lo, hi) in enumerate(units):
                    dve.wait_ge(s_ready, m + 1)
                    dve.wait_ge(dec_ready, m + 1)
                    dve.wait_ge(wt_free, m + 1)
                    V.tensor_mul(wt[m % 2][:, 0:(hi - lo) * P], s_ps[m % 2][:, 0:(hi - lo) * P],
                                 dec[m % 2][:, 0:(hi - lo) * P]).then_inc(wt_ready, 1)
                    if s == NT - 1:
                        outputs(n, d, h)


def mlstm_output(nc, a, ident, hs, xc, zs, mixT_dram):
    NH = ML_HEADS
    with stage(nc, "mlout") as st:
        stats = st.sb("stats", [P, NT * NH, 6])
        mv = st.sb("mv", [P, NT * NH, 2])
        rstd = st.sb("rstd", [P, NT * NH])
        sq = st.sb("sq", [P, NT * NH])
        ng, sk = st.sb("ng", [96, NC96]), st.sb("sk", [96, NC96])
        ld, var_ready, sqrt_ready, h_ready = st.sem("ld"), st.sem("var_ready"), st.sem("sqrt_ready"), st.sem("h_ready")
        t_ready, t_free, y_ready, stored = st.sem("t_ready"), st.sem("t_free"), st.sem("y_ready"), st.sem("stored")
        ps = [st.ps(f"ps{n}") for n in range(4)]
        with nc.Block() as block:

            @block.sync
            def _(sp):
                sp.dma_start(ng[:], a["ml_norm_gP"]).then_inc(ld, 16)
                sp.dma_start(sk[:], a["ml_skipP"]).then_inc(ld, 16)
                sp.wait_ge(y_ready, 1)
                sp.dma_start(mixT_dram.rearrange("(c p) t -> p c t", p=96), xc[:]).then_inc(stored, 16)
                sp.wait_ge(stored, 16)

            @block.scalar
            def _(act):
                act.wait_ge(var_ready, 1)
                nc.scalar.activation(sq[:], sq[:], ACT.Sqrt).then_inc(sqrt_ready, 1)

            @block.vector
            def _(dve):
                V = nc.vector
                dve.sem_inc(t_free, 4)
                for t in range(NT):
                    for h in range(NH):
                        V.bn_stats(stats[:, t * NH + h, :], hs[:, t, h * ML_DH:(h + 1) * ML_DH])
                V.drain()
                for g in range(NT * NH):
                    V.bn_aggr(mv[:, g, :], stats[:, g, :])
                V.drain()
                V.tensor_scalar(sq[:], mv[:, :, 1], LN_EPS, None, ALU.add).then_inc(var_ready, 1)
                dve.wait_ge(sqrt_ready, 1)
                V.reciprocal(rstd[:], sq[:])
                V.drain()
                for t in range(NT):
                    for h in range(NH):
                        g, o = t * NH + h, hs[:, t, h * ML_DH:(h + 1) * ML_DH]
                        last = V.tensor_scalar(o, o, mv[:, g, 0:1], rstd[:, g:g + 1], ALU.subtract, ALU.mult)
                last.then_inc(h_ready, 1)
                dve.wait_ge(ld, 32)
                for c in range(NC96):
                    V.tensor_scalar(xc[:, c, :], xc[:, c, :], sk[:, c:c + 1], None, ALU.mult)
                V.drain()
                for c in range(NC96):
                    dve.wait_ge(t_ready, c + 1)
                    V.scalar_tensor_tensor(xc[:, c, :], ps[c % 4][0:96, :], ng[:, c:c + 1], xc[:, c, :],
                                           ALU.mult, ALU.add).then_inc(t_free, 1)
                V.drain()
                V.tensor_mul(xc[:], xc[:], zs[:]).then_inc(y_ready, 1)

            @block.tensor
            def _(pe):
                pe.wait_ge(h_ready, 1)
                for c in range(NC96):
                    pe.wait_ge(t_free, c + 1)
                    for t in range(NT):
                        mm = nc.tensor.transpose(ps[c % 4][0:96, t * P:(t + 1) * P],
                                                 hs[:, t, c * 96:(c + 1) * 96], ident[:])
                    mm.then_inc(t_ready, 1)


def reload_chunks(nc, name, dstT, n, src):
    with stage(nc, name) as st:
        s = st.sem("loaded")
        with nc.Block() as block:

            @block.sync
            def _(sp):
                sp.dma_start(dstT[:, 0:n, :], src.rearrange("(c p) t -> p c t", p=P)).then_inc(s, 16)
                sp.wait_ge(s, 16)


def mlstm_mixer(nc, a, x, xT, cst, mk, mv, mix, memq, dram):
    ident, strict, ones, iota, pidx = cst
    win = a["ml_w_in"][0]
    xm_d, z_d, mixT_d = dram("ml_xm", [ML_W, S]), dram("ml_z", [ML_W, S]), dram("ml_mixT", [ML_W, S])
    gemms(nc, "proj1", [job(win, 0, 2, 384, xT, P, S, xm_d, "T", M=96),
                        job(win, ML_W, 2, 384, xT, P, S, z_d, "T", M=96),
                        job(win, 2 * ML_W + 16, 1, MEM_W, xT, P, S, memq, "T")])
    memory_attention(nc, "mem1", ident, memq, mk, mv, mix)
    with ExitStack() as ctx:
        def sb(name, shape):
            return ctx.enter_context(nc.sbuf_tensor("ml_" + name, shape, F32))
        xc, zs = sb("xc", [96, NC96, S]), sb("zs", [96, NC96, S])
        hs = sb("hs", [P, NT, ML_W])
        with ExitStack() as inner:
            def si(name, shape):
                return inner.enter_context(nc.sbuf_tensor("mli_" + name, shape, F32))
            neg_m, diag_m = si("neg_m", [P, 8, S]), si("diag_m", [P, 8, S])
            a_tok, e_tok = si("a_tok", [P, 2 * NT * 4]), si("e_tok", [P, 2 * NT * 4])
            v = si("v", [P, NT, ML_HEADS, ML_DH + 1])
            mlstm_gates(nc, a, xT, ident, ones, pidx, neg_m, diag_m, a_tok, e_tok)
            q, k = si("q", [96, NC96, S]), si("k", [96, NC96, S])
            with nc.sbuf_tensor("ml_xm_s", [96, NC96, S + CONV_K - 1], F32) as xm:
                mlstm_conv(nc, a, xm_d, z_d, xm, xc, zs)
                mlstm_qkv(nc, a, xm, xc, q, k, v)
            mlstm_scan(nc, q, k, v, neg_m, diag_m, a_tok, e_tok, hs)
        mlstm_output(nc, a, ident, hs, xc, zs, mixT_d)
    load_transposed(nc, "mixT1", mix, xT, ident)
    reload_chunks(nc, "mixT1b", xT, ML_W // P, mixT_d)


def first_block_rest(nc, a, x, xT, cst, mk, mv, mix, memq, proj, slots, y_dram, sbr, dram):
    ident = cst[0]
    mlstm_mixer(nc, a, x, xT, cst, mk, mv, mix, memq, dram)
    gemm(nc, "out1", a["w_out"][1], 0, 2, 512, xT, P, S, proj, "N")
    norm(nc, "ln10", x, x, xT, ident, LN_EPS, False, a["ln_g"][1, 0], a["ln_b"][1, 0], resid=proj, alpha=ALPHA)
    moe_layer(nc, 1, a, x, xT, cst, slots, y_dram, proj, sbr)
    norm(nc, "ln11", x, x, xT, ident, LN_EPS, False, a["ln_g"][1, 1], a["ln_b"][1, 1], resid=proj, alpha=ALPHA)


def condition(nc, a, condT):
    with stage(nc, "cond") as st:
        sg = st.sb("sg", [P, KD])
        ld, ready, sig = st.sem("ld"), st.sem("ready"), st.sem("sig")
        with nc.Block() as block:

            @block.sync
            def _(sp):
                sp.dma_start(condT[:], a["c_P"]).then_inc(ld, 16)

            @block.scalar
            def _(act):
                act.wait_ge(ld, 16)
                nc.scalar.activation(sg[:], condT[:], ACT.Sigmoid).then_inc(sig, 1)

            @block.vector
            def _(dve):
                dve.wait_ge(sig, 1)
                nc.vector.tensor_mul(condT[:], condT[:], sg[:])


def add_rows(nc, name, src, vec, dst, parts):
    n = vec.shape[0] // parts
    with stage(nc, name) as st:
        t, v = st.sb("t", [parts, n]), st.sb("v", [parts, n])
        ld, ready, stored = st.sem("ld"), st.sem("ready"), st.sem("stored")
        fold = lambda ap: ap.rearrange("(p n) -> p n", p=parts)
        with nc.Block() as block:

            @block.sync
            def _(sp):
                sp.dma_start(t[:], fold(src)).then_inc(ld, 16)
                sp.dma_start(v[:], fold(vec)).then_inc(ld, 16)
                sp.wait_ge(ready, 1)
                sp.dma_start(fold(dst), t[:]).then_inc(stored, 16)
                sp.wait_ge(stored, 16)

            @block.vector
            def _(dve):
                dve.wait_ge(ld, 32)
                nc.vector.tensor_add(t[:], t[:], v[:]).then_inc(ready, 1)


def latents(nc, a, ident, lat, cqT, ckvT, kp):
    QT, KT_ = Q_RANK // P, KV_RANK // P
    HR = ROPE // 2
    with stage(nc, "lat") as st:
        x = st.sb("x", [P, NT, Q_RANK + KV_RANK + ROPE])
        stats = st.sb("stats", [P, NT, 2, 6])
        mv = st.sb("mv", [P, NT * 2, 2])
        sq, rs = st.sb("sq", [P, NT * 2]), st.sb("rs", [P, NT * 2])
        gq, gk = st.sb("gq", [P, QT]), st.sb("gk", [P, KT_])
        ld, var_ready, sqrt_ready, x_ready = st.sem("ld"), st.sem("var_ready"), st.sem("sqrt_ready"), st.sem("x_ready")
        t_ready, t_free = st.sem("t_ready"), st.sem("t_free")
        ps = [st.ps(f"ps{n}") for n in range(4)]
        cuts = [(c * P, P, cqT[:, c, :], gq[:, c:c + 1]) for c in range(QT)]
        cuts += [(Q_RANK + c * P, P, ckvT[:, c, :], gk[:, c:c + 1]) for c in range(KT_)]
        cuts += [(Q_RANK + KV_RANK + c * HR, HR, kp[c][:], None) for c in range(2)]
        with nc.Block() as block:

            @block.sync
            def _(sp):
                sp.dma_start(x[:], lat.rearrange("(t p) f -> p t f", p=P)).then_inc(ld, 16)
                sp.dma_start(gq[:], a["g_q_lat_P"]).then_inc(ld, 16)
                sp.dma_start(gk[:], a["g_kv_lat_P"]).then_inc(ld, 16)

            @block.vector
            def _(dve):
                V = nc.vector
                dve.wait_ge(ld, 48)
                rng = [(0, Q_RANK), (Q_RANK, Q_RANK + KV_RANK)]
                for t in range(NT):
                    for n, (lo, hi) in enumerate(rng):
                        V.bn_stats(stats[:, t, n, :], x[:, t, lo:hi])
                V.drain()
                for t in range(NT):
                    for n in range(2):
                        V.bn_aggr(mv[:, t * 2 + n, :], stats[:, t, n, :])
                V.drain()
                V.tensor_mul(sq[:], mv[:, :, 0], mv[:, :, 0])
                V.drain()
                V.scalar_tensor_tensor(sq[:], mv[:, :, 1], EPS2, sq[:], ALU.add, ALU.add).then_inc(var_ready, 1)
                dve.wait_ge(sqrt_ready, 1)
                V.reciprocal(rs[:], sq[:])
                V.drain()
                for t in range(NT):
                    for n, (lo, hi) in enumerate(rng):
                        last = V.tensor_scalar(x[:, t, lo:hi], x[:, t, lo:hi], rs[:, t * 2 + n:t * 2 + n + 1], None,
                                               ALU.mult)
                last.then_inc(x_ready, 1)

            @block.tensor
            def _(pe):
                pe.wait_ge(x_ready, 1)
                for n, (lo, wd, dst, g) in enumerate(cuts):
                    pe.wait_ge(t_free, n + 1)
                    for t in range(NT):
                        mm = nc.tensor.transpose(ps[n % 4][0:wd, t * P:(t + 1) * P], x[:, t, lo:lo + wd], ident[:])
                    mm.then_inc(t_ready, 1)

            @block.scalar
            def _(act):
                act.sem_inc(t_free, 4)
                act.wait_ge(var_ready, 1)
                nc.scalar.activation(sq[:], sq[:], ACT.Sqrt).then_inc(sqrt_ready, 1)
                for n, (lo, wd, dst, g) in enumerate(cuts):
                    act.wait_ge(t_ready, n + 1)
                    nc.scalar.activation(dst, ps[n % 4][0:wd, :], ACT.Copy, scale=1.0 if g is None else g) \
                        .then_inc(t_free, 1)


TWO_PI_1 = 6.28125
TWO_PI_2 = 2029.0 / 2 ** 20
TWO_PI_3 = 2 * math.pi - TWO_PI_1 - TWO_PI_2
ROUND = 1.5 * 2 ** 23


def rotary(nc, a, q_all, kp, qpe, kpe):
    H4 = MLA_H // 4
    lim = 3.1415925
    with stage(nc, "rope") as st:
        pi = st.sb("pi", [P, S], I32)
        fr = st.sb("fr", [P, 1])
        ang, kk, cs, sn, gt = (st.sb(n, [P, S]) for n in ("ang", "kk", "cs", "sn", "gt"))
        t1, t2 = st.sb("t1", [P, H4, S]), st.sb("t2", [P, H4, S])
        o1, o2, tm = st.sb("o1", [P, H4, S]), st.sb("o2", [P, H4, S]), st.sb("tm", [P, S])
        k1, k2 = st.sb("k1", [32, S]), st.sb("k2", [32, S])
        ld, ang_ready, trig, done, stored = (st.sem("ld"), st.sem("ang_ready"), st.sem("trig"), st.sem("done"),
                                             st.sem("stored"))
        with nc.Block() as block:

            @block.sync
            def _(sp):
                sp.dma_start(pi[:], bcast_rows(a["positions_2"][0])).then_inc(ld, 16)
                sp.dma_start(fr[:], a["inv_freq"]).then_inc(ld, 16)
                nope = MLA_H * NOPE
                sp.dma_start(t1[:], q_all[nope:nope + 256, :].rearrange("(a p) t -> p a t", p=P)).then_inc(ld, 16)
                sp.dma_start(t2[:], q_all[nope + 256:nope + 512, :].rearrange("(a p) t -> p a t", p=P)).then_inc(ld, 16)
                sp.wait_ge(done, 1)
                qv = qpe.rearrange("(h c p) t -> h c p t", c=2, p=32)
                for hh in range(H4):
                    sp.dma_start(qv[4 * hh:4 * hh + 4, 0], o1[:, hh, :]).then_inc(stored, 16)
                    sp.dma_start(qv[4 * hh:4 * hh + 4, 1], o2[:, hh, :]).then_inc(stored, 16)
                sp.dma_start(kpe[0:32, :], k1[:]).then_inc(stored, 16)
                sp.dma_start(kpe[32:64, :], k2[:]).then_inc(stored, 16)
                sp.wait_ge(stored, 16 * (2 * H4 + 2))

            @block.vector
            def _(dve):
                V = nc.vector
                dve.wait_ge(ld, 64)
                V.tensor_copy(ang[:], pi[:])
                V.drain()
                V.tensor_scalar(ang[:], ang[:], fr[:, 0:1], None, ALU.mult)
                V.drain()
                V.tensor_scalar(kk[:], ang[:], 1.0 / (2 * math.pi), None, ALU.mult)
                V.drain()
                V.tensor_scalar(kk[:], kk[:], ROUND, None, ALU.add)
                V.drain()
                V.tensor_scalar(kk[:], kk[:], ROUND, None, ALU.subtract)
                for part in (TWO_PI_1, TWO_PI_2, TWO_PI_3):
                    V.drain()
                    V.scalar_tensor_tensor(ang[:], kk[:], -part, ang[:], ALU.mult, ALU.add)
                V.drain()
                V.tensor_scalar(cs[:], ang[:], math.pi / 2, None, ALU.add)
                V.drain()
                V.tensor_scalar(gt[:], cs[:], math.pi, -2 * math.pi, ALU.is_gt, ALU.mult)
                V.drain()
                V.tensor_add(cs[:], cs[:], gt[:])
                V.tensor_scalar(ang[:], ang[:], lim, -lim, ALU.min, ALU.max)
                V.drain()
                V.tensor_scalar(cs[:], cs[:], lim, -lim, ALU.min, ALU.max).then_inc(ang_ready, 1)
                dve.wait_ge(trig, 1)
                for hh in range(H4):
                    V.tensor_mul(o1[:, hh, :], t1[:, hh, :], cs[:])
                    V.tensor_mul(o2[:, hh, :], t1[:, hh, :], sn[:])
                    V.tensor_mul(tm[:], t2[:, hh, :], sn[:])
                    V.tensor_mul(gt[:], t2[:, hh, :], cs[:])
                    V.drain()
                    V.tensor_sub(o1[:, hh, :], o1[:, hh, :], tm[:])
                    V.tensor_add(o2[:, hh, :], o2[:, hh, :], gt[:])
                    V.drain()
                V.tensor_mul(k1[:], kp[0][:], cs[0:32, :])
                V.tensor_mul(k2[:], kp[0][:], sn[0:32, :])
                V.tensor_mul(tm[0:32, :], kp[1][:], sn[0:32, :])
                V.tensor_mul(gt[0:32, :], kp[1][:], cs[0:32, :])
                V.drain()
                V.tensor_sub(k1[:], k1[:], tm[0:32, :])
                V.tensor_add(k2[:], k2[:], gt[0:32, :])
                V.drain().then_inc(done, 1)

            @block.scalar
            def _(act):
                act.wait_ge(ang_ready, 1)
                nc.scalar.activation(cs[:], cs[:], ACT.Sin)
                nc.scalar.activation(sn[:], ang[:], ACT.Sin).then_inc(trig, 1)


G0_START = [min(max(u * P - 64, 0), S - 2 * P) for u in range(4)]
STEPS = list(range(1, 9)) + [math.ceil(8 * 128 ** (j / 8)) for j in range(1, 8)]
BAND = 2 * 64 + 1
PITCH = 3 * P
UNIT0 = P * (PITCH + 1)
FILL = UNIT0 * 4 * DIL_H // P // 4
BIAS_WIDTH = (4 * BAND, 4 * P, 4 * 32)
BIAS_COL = (0, 4 * BAND, 4 * BAND + 4 * P)


class RelativeBias:

    def __init__(self, nc, a, biases, groups, st):
        self.nc, self.a, self.biases, self.groups = nc, a, biases, groups
        n, wd = sum(BIAS_WIDTH), max(BIAS_WIDTH)
        self.pki, self.pk = st.sb("pki", [P, n], I32), st.sb("pk", [P, n])
        self.pqi, self.pq = st.sb("pqi", [P, 12], I32), st.sb("pq", [P, 12])
        self.tab = st.sb("tab", [P, 3 * N_REL * DIL_H])
        self.bucket, self.rel = st.sb("bucket", [P, wd]), st.sb("rel", [P, wd])
        self.hit = [st.sb(f"hit{r}", [P, wd]) for r in range(2)]
        self.row = [st.sb(f"row{r}", [P, DIL_H]) for r in range(2)]
        self.cnt = st.sb("cnt", [P, 1])
        self.mask = st.sb("mask", [P, n])
        self.acc = {g: st.sb(f"acc{g}", [P, DIL_H, BIAS_WIDTH[g]]) for g in groups}
        self.neg = st.sb("neg", [P, FILL])
        self.ld, self.filled = st.sem("bias_ld"), st.sem("filled")
        self.neg_ready, self.ready, self.stored = st.sem("neg_ready"), st.sem("bias_ready"), st.sem("bias_stored")

    def sync(self, sp):
        a = self.a
        sp.dma_start(self.pki[:], a["pos_k"]).then_inc(self.ld, 16)
        sp.dma_start(self.pqi[:], a["pos_q"]).then_inc(self.ld, 16)
        sp.dma_start(self.tab[:], bcast_rows(a["rel_tab"])).then_inc(self.ld, 16)
        sp.dma_start(self.mask[:], a["band_mask"]).then_inc(self.ld, 16)

    def fill(self, pool):
        pool.wait_ge(self.neg_ready, 1)
        for g in self.groups:
            if g == 0:
                flat = self.biases[0].rearrange("(p n) -> p n", p=P)
                for c in range(4):
                    pool.dma_start(flat[:, c * FILL:(c + 1) * FILL], self.neg[:]).then_inc(self.filled, 16)
            if g == 2:
                flat = self.biases[2].rearrange("h p n -> p h n")
                for h in range(DIL_H):
                    pool.dma_start(flat[:, h, :], self.neg[:, 0:4 * P]).then_inc(self.filled, 16)

    def store(self, q, g):
        acc = self.acc[g]
        if g == 0:
            units = self.biases[0].rearrange("(h u p n) -> u p h n", h=DIL_H, u=4, p=P)
            for u in range(4):
                at = u * P - 64 - G0_START[u] + 64
                q.dma_start(units[u][:, :, at:at + BAND], acc[:, :, u * BAND:(u + 1) * BAND]).then_inc(self.stored, 16)
        elif g == 1:
            q.dma_start(self.biases[1].rearrange("h p n -> p h n"), acc[:, :, 0:4 * P]).then_inc(self.stored, 16)
        else:
            blocks = self.biases[2].rearrange("h (c p) (u d i) -> c d p h u i", c=4, u=4, d=4)
            for c in range(4):
                for u in range(4):
                    q.dma_start(blocks[c, c][:, :, u, :], acc[32 * c:32 * c + 32, :, u * 32:(u + 1) * 32]) \
                        .then_inc(self.stored, 16)
        return (4, 1, 16)[g]

    def finish(self, q):
        fills = 4 * (0 in self.groups) + DIL_H * (2 in self.groups)
        if fills:
            q.wait_ge(self.filled, 16 * fills)
        done = 0
        for n, g in enumerate(self.groups):
            q.wait_ge(self.ready, n + 1)
            done += self.store(q, g)
        q.wait_ge(self.stored, 16 * done)

    def vector(self, dve):
        V, pk, pq, bucket, rel = self.nc.vector, self.pk, self.pq, self.bucket, self.rel
        V.memset(self.neg[:], NEG).then_inc(self.neg_ready, 1)
        dve.wait_ge(self.ld, 64)
        V.tensor_copy(pk[:], self.pki[:])
        V.tensor_copy(pq[:], self.pqi[:])
        V.drain()
        for g in self.groups:
            acc = self.acc[g]
            wd, col, uw = BIAS_WIDTH[g], BIAS_COL[g], BIAS_WIDTH[g] // 4
            b, d = bucket[:, 0:wd], rel[:, 0:wd]
            for u in range(4):
                V.tensor_scalar(rel[:, u * uw:(u + 1) * uw], pk[:, col + u * uw:col + (u + 1) * uw],
                                pq[:, g * 4 + u:g * 4 + u + 1], None, ALU.subtract)
            V.drain()
            V.tensor_scalar(b, d, 0.0, float(N_REL // 2), ALU.is_gt, ALU.mult)
            V.drain()
            V.scalar_tensor_tensor(d, d, -1.0, d, ALU.mult, ALU.max)
            V.drain()
            for s in STEPS:
                V.scalar_tensor_tensor(b, d, float(s), b, ALU.is_ge, ALU.add)
                V.drain()
            for h in range(DIL_H):
                V.tensor_copy(acc[:, h, 0:wd], self.mask[:, col:col + wd])
            V.memset(self.cnt[:], 0.0)
            V.drain()
            with dve.Fori(0, N_REL // 2) as i:
                for r in range(2):
                    V.tensor_copy(self.row[r][:], self.tab[:, ds((2 * i + r) * DIL_H + g * N_REL * DIL_H, DIL_H)])
                    V.tensor_scalar(self.hit[r][:, 0:wd], b, self.cnt[:, 0:1], None, ALU.is_equal)
                    V.drain()
                    for h in range(DIL_H):
                        V.scalar_tensor_tensor(acc[:, h, 0:wd], self.hit[r][:, 0:wd], self.row[r][:, h:h + 1],
                                               acc[:, h, 0:wd], ALU.mult, ALU.add)
                    V.tensor_scalar(self.cnt[:], self.cnt[:], 1.0, None, ALU.add)
                    V.drain()
            V.drain().then_inc(self.ready, 1)


def dilated_views(g):
    if g == 0:
        return None, lambda m, u: m[u * P:(u + 1) * P, :]
    if g == 1:
        return (lambda ap: ap.rearrange("p (i c) -> p c i", c=4),
                lambda m, u: m.rearrange("(i c) f -> c i f", c=4)[u])
    return (lambda ap: ap.rearrange("p (i c) -> p c i", c=16),
            lambda m, u: m.rearrange("(i c) f -> c i f", c=16)[4 * u:4 * u + 4])


def dilated(nc, ident, g, qk, v, bias, o_dram, stat_dram):
    cols, rows = dilated_views(g)
    full = slice(None)
    hs = lambda h: ds(h * P, P)
    if g == 0:
        nk, chunks = 256, 8
        v_src = lambda h: [((full, 2 * u + c, full), v[G0_START[u] + c * P:G0_START[u] + (c + 1) * P, hs(h)])
                           for u in range(4) for c in range(2)]
        k_at = lambda k, u: k[:, G0_START[u]:G0_START[u] + 256]
        v_at = lambda u: (2 * u, 2 * u + 1)
    else:
        nk, chunks = P, 4
        sub = (lambda ap, h: ap[:, hs(h)]) if g == 1 else (lambda ap, h: ap[:, :, hs(h)])
        v_src = lambda h: [((full, u, full), sub(rows(v, u), h)) for u in range(4)]
        k_at = lambda k, u: k[:, u * P:(u + 1) * P]
        v_at = lambda u: (u,)

    if g == 0:
        b0 = bias.rearrange("(h u n) -> h u n", h=DIL_H, u=4)[:, :, 0:P * PITCH].rearrange("h u (p n) -> p h u n", p=P)
        b_src = lambda h: b0[:, ds(h, 1), :, 64:64 + 256]
    else:
        b_src = lambda h: bias.rearrange("h p n -> p h n")[:, ds(h, 1), :]

    def out(h, u):
        r = rows(o_dram, u)
        return r[:, :, hs(h)] if g == 2 else r[:, hs(h)]
    attention(nc, f"dil{g}", ident, DIL_H, P, P, nk,
              lambda h: [qk[hs(h), :]], lambda h: [qk[ds(h * P + D, P), :]], v_src,
              lambda q, u: q[:, u * P:(u + 1) * P], k_at, v_at, out, P ** -0.5,
              bias_src=b_src, v_chunks=chunks,
              stats_out=lambda u: rows(stat_dram, u))


def merge(nc, oa, ogs, stats_d, gates, xT, ident):
    H = DIL_H
    with stage(nc, "merge") as st:
        o = [[st.sb(f"o{n}{t}", [P, D]) for t in range(NT)] for n in range(4)]
        gt = [st.sb(f"g{t}", [P, 2 * D]) for t in range(NT)]
        sd = st.sb("sd", [P, NT, 3, H, 2])
        lse = st.sb("lse", [P, NT, 3, H])
        mx, sm = st.sb("mx", [P, NT, H]), st.sb("sm", [P, NT, H])
        ld, sld = [st.sem(f"ld{t}") for t in range(NT)], st.sem("sld")
        ln_ready, l_ready, e_ready, g_ready = st.sem("ln_ready"), st.sem("l_ready"), st.sem("e_ready"), st.sem("g_ready")
        y_ready, t_ready, t_free = st.sem("y_ready"), st.sem("t_ready"), st.sem("t_free")
        ps = [st.ps(f"ps{n}") for n in range(4)]
        with nc.Block() as block:

            @block.sync
            def _(sp):
                for g in range(3):
                    for t in range(NT):
                        sp.dma_start(sd[:, t, g].rearrange("p h s -> p (h s)"), stats_d[g][t * P:(t + 1) * P, :]) \
                            .then_inc(sld, 16)
                for t in range(NT):
                    for n, src in enumerate([oa] + ogs):
                        sp.dma_start(o[n][t][:], src[t * P:(t + 1) * P, :]).then_inc(ld[t], 16)
                    sp.dma_start(gt[t][:], gates[t * P:(t + 1) * P, :]).then_inc(ld[t], 16)

            @block.scalar
            def _(act):
                act.sem_inc(t_free, 4)
                act.wait_ge(sld, 16 * 3 * NT)
                nc.scalar.activation(lse[:].rearrange("p t g h -> p (t g h)"),
                                     sd[:].rearrange("p t g h s -> p (t g h) s")[:, :, 1], ACT.Ln).then_inc(ln_ready, 1)
                act.wait_ge(l_ready, 1)
                nc.scalar.activation(lse[:], lse[:], ACT.Exp).then_inc(e_ready, 1)
                for t in range(NT):
                    act.wait_ge(ld[t], 16 * 5)
                    nc.scalar.activation(gt[t][:], gt[t][:], ACT.Sigmoid).then_inc(g_ready, 1)
                for c in range(KD):
                    act.wait_ge(t_ready, c + 1)
                    nc.scalar.activation(xT[:, c, :], ps[c % 4][:], ACT.Copy).then_inc(t_free, 1)

            @block.vector
            def _(dve):
                V = nc.vector
                dve.wait_ge(ln_ready, 1)
                f = lse[:].rearrange("p t g h -> p (t g h)")
                V.tensor_sub(f, f, sd[:].rearrange("p t g h s -> p (t g h) s")[:, :, 0])
                V.drain()
                V.tensor_max(mx[:], lse[:, :, 0], lse[:, :, 1])
                V.drain()
                V.tensor_max(mx[:], mx[:], lse[:, :, 2])
                V.drain()
                for g in range(3):
                    last = V.tensor_sub(lse[:, :, g], lse[:, :, g], mx[:])
                last.then_inc(l_ready, 1)
                dve.wait_ge(e_ready, 1)
                V.tensor_add(sm[:], lse[:, :, 0], lse[:, :, 1])
                V.drain()
                V.tensor_add(sm[:], sm[:], lse[:, :, 2])
                V.drain()
                V.reciprocal(sm[:], sm[:])
                V.drain()
                for g in range(3):
                    V.tensor_mul(lse[:, :, g], lse[:, :, g], sm[:])
                V.drain()
                for t in range(NT):
                    dve.wait_ge(ld[t], 16 * 5)
                    for g in range(3):
                        for h in range(H):
                            cut = slice(h * P, (h + 1) * P)
                            w = lse[:, t, g, h:h + 1]
                            if g == 0:
                                V.tensor_scalar(o[1][t][:, cut], o[1][t][:, cut], w, None, ALU.mult)
                            else:
                                V.scalar_tensor_tensor(o[1][t][:, cut], o[1 + g][t][:, cut], w, o[1][t][:, cut],
                                                       ALU.mult, ALU.add)
                        V.drain()
                    dve.wait_ge(g_ready, t + 1)
                    V.tensor_mul(o[0][t][:], o[0][t][:], gt[t][:, 0:D])
                    V.tensor_mul(o[1][t][:], o[1][t][:], gt[t][:, D:])
                    V.drain()
                    V.tensor_add(o[0][t][:], o[0][t][:], o[1][t][:]).then_inc(y_ready, 1)

            @block.tensor
            def _(pe):
                pe.wait_ge(y_ready, NT)
                for c in range(KD):
                    pe.wait_ge(t_free, c + 1)
                    for t in range(NT):
                        mm = nc.tensor.transpose(ps[c % 4][:, t * P:(t + 1) * P], o[0][t][:, c * P:(c + 1) * P], ident[:])
                    mm.then_inc(t_ready, 1)


def ec_route(nc, a, xT, ident, ones, pidx, affT_d, aff, rank, comb):
    E = N_EXP
    with stage(nc, "ecr") as st:
        rw = st.sb("rw", [P, KD, E])
        bc = st.sb("bc", [P, E, S])
        earlier = st.sb("earlier", [P, NT, S])
        junk = [st.sb(f"junk{r}", [P, S]) for r in range(8)]
        mx, sm = st.sb("mx", [P, NT]), st.sb("sm", [P, NT])
        gtc, tie = st.sb("gtc", [P, NT, E]), st.sb("tie", [P, NT, E])
        aT, rT = st.sb("aT", [E, S]), st.sb("rT", [E, S])
        pairsel = st.sb("pairsel", [E, E // 2, P])
        p64 = st.sb("p64", [P, 2])
        ab = [st.sb(f"ab{r}", [P, S]) for r in range(2)]
        ld, lg_ready, x_ready, e_ready, a_ready = (st.sem("ld"), st.sem("lg_ready"), st.sem("x_ready"),
                                                   st.sem("e_ready"), st.sem("a_ready"))
        at_ready, at_copied, at_stored, bc_in, r_ready = (st.sem("at_ready"), st.sem("at_copied"),
                                                          st.sem("at_stored"), st.sem("bc_in"), st.sem("r_ready"))
        rt_ready, rt_copied = st.sem("rt_ready"), st.sem("rt_copied")
        sel_ready, m_ready = st.sem("sel_ready"), st.sem("m_ready")
        pr_ready, ab_ready, comb_done = st.sem("pr_ready"), st.sem("ab_ready"), st.sem("comb_done")
        lg, tp = st.ps("lg"), st.ps("tp")
        rb = [st.ps(f"rb{r}") for r in range(2)]
        abp = [st.ps(f"abp{r}") for r in range(2)]
        with nc.Block() as block:

            @block.sync
            def _(sp):
                sp.dma_start(rw[:], a["w_router_2"][0].rearrange("(k p) e -> p k e", p=P)).then_inc(ld, 16)
                sp.wait_ge(at_copied, 1)
                sp.dma_start(affT_d.rearrange("(e t) -> e t", e=E), aT[:]).then_inc(at_stored, 16)
                sp.wait_ge(at_stored, 16)
                sp.dma_start(bc[:].rearrange("p e t -> p (e t)"), bcast_rows(affT_d)).then_inc(bc_in, 16)

            @block.gpsimd
            def _(pool):
                nc.gpsimd.memset(earlier[:], 1.0)
                nc.gpsimd.memset(pairsel[:], 1.0)
                nc.gpsimd.drain()
                for t in range(NT):
                    nc.gpsimd.affine_select(out=earlier[:, t, :], in_=earlier[:, t, :], pattern=[[-1, S]],
                                            compare_op=ALU.is_gt, fill=0.0, base=t * P, channel_multiplier=1)
                nc.gpsimd.drain().then_inc(m_ready, 1)
                for h in range(2):
                    v = pairsel[:, :, h * 64:(h + 1) * 64]
                    nc.gpsimd.affine_select(out=v, in_=v, pattern=[[-2, E // 2], [0, 64]], compare_op=ALU.is_equal,
                                            fill=0.0, base=-h, channel_multiplier=1)
                nc.gpsimd.drain().then_inc(sel_ready, 1)

            @block.tensor
            def _(pe):
                pe.wait_ge(ld, 16)
                for t in range(NT):
                    for k in range(KD):
                        mm = nc.tensor.matmul(lg[:, t * E:(t + 1) * E], xT[:, k, t * P:(t + 1) * P], rw[:, k, :],
                                              start=(k == 0), stop=(k == KD - 1))
                mm.then_inc(lg_ready, 1)
                pe.wait_ge(a_ready, 1)
                for t in range(NT):
                    mm = nc.tensor.transpose(tp[0:E, t * P:(t + 1) * P], aff[:, t, :], ident[:])
                mm.then_inc(at_ready, 1)
                pe.wait_ge(r_ready, 1)
                pe.wait_ge(at_copied, 1)
                for t in range(NT):
                    mm = nc.tensor.transpose(tp[0:E, t * P:(t + 1) * P], rank[:, t, :], ident[:])
                mm.then_inc(rt_ready, 1)
                pe.wait_ge(rt_copied, 1)
                pe.wait_ge(sel_ready, 1)
                for n in range(E // 2):
                    if n >= 2:
                        pe.wait_ge(comb_done, n - 1)
                    nc.tensor.matmul(abp[n % 2][:], pairsel[:, n, :], aT[:], start=True, stop=True)
                    nc.tensor.matmul(rb[n % 2][:], pairsel[:, n, :], rT[:], start=True, stop=True).then_inc(pr_ready, 1)

            @block.scalar
            def _(act):
                act.wait_ge(x_ready, 1)
                nc.scalar.activation(aff[:], aff[:], ACT.Exp).then_inc(e_ready, 1)
                act.wait_ge(at_ready, 1)
                nc.scalar.activation(aT[:], tp[0:E, :], ACT.Copy).then_inc(at_copied, 1)
                act.wait_ge(rt_ready, 1)
                nc.scalar.activation(rT[:], tp[0:E, :], ACT.Copy).then_inc(rt_copied, 1)
                for n in range(E // 2):
                    if n >= 2:
                        act.wait_ge(comb_done, n - 1)
                    act.wait_ge(pr_ready, n + 1)
                    nc.scalar.activation(ab[n % 2][:], abp[n % 2][:], ACT.Copy).then_inc(ab_ready, 1)

            @block.vector
            def _(dve):
                V = nc.vector
                V.tensor_scalar(p64[:, 1:2], pidx[:, 0:1], 64.0, -64.0, ALU.is_ge, ALU.mult)
                V.drain()
                V.tensor_add(p64[:, 0:1], p64[:, 1:2], pidx[:, 0:1])
                dve.wait_ge(lg_ready, 1)
                lg3 = lg[:, 0:NT * E].rearrange("p (t e) -> p t e", e=E)
                V.tensor_reduce(mx[:], lg3, AX.X, ALU.max)
                V.drain()
                for t in range(NT):
                    last = V.tensor_scalar(aff[:, t, :], lg3[:, t, :], mx[:, t:t + 1], None, ALU.subtract)
                last.then_inc(x_ready, 1)
                dve.wait_ge(e_ready, 1)
                V.tensor_reduce(sm[:], aff[:], AX.X, ALU.add)
                V.drain()
                V.reciprocal(sm[:], sm[:])
                V.drain()
                for t in range(NT):
                    last = V.tensor_scalar(aff[:, t, :], aff[:, t, :], sm[:, t:t + 1], None, ALU.mult)
                last.then_inc(a_ready, 1)
                dve.wait_ge(bc_in, 16)
                dve.wait_ge(m_ready, 1)
                for t in range(NT):
                    for e in range(E):
                        if e % 4 == 0:
                            V.drain()
                        V.tensor_scalar(junk[2 * (e % 4)][:], bc[:, e, :], aff[:, t, e:e + 1], 0.0, ALU.is_gt, ALU.add,
                                        accum_out=gtc[:, t, e:e + 1])
                        V.scalar_tensor_tensor(junk[2 * (e % 4) + 1][:], bc[:, e, :], aff[:, t, e:e + 1], earlier[:, t, :],
                                               ALU.is_equal, ALU.mult, accum_out=tie[:, t, e:e + 1])
                V.drain()
                V.tensor_add(rank[:], gtc[:], tie[:])
                V.drain().then_inc(r_ready, 1)
                for n in range(E // 2):
                    dve.wait_ge(pr_ready, n + 1)
                    dve.wait_ge(ab_ready, n + 1)
                    V.scalar_tensor_tensor(comb[:, n, :], rb[n % 2][:], p64[:, 0:1], ab[n % 2][:], ALU.is_equal,
                                           ALU.mult).then_inc(comb_done, 1)


def ec_experts(nc, a, h, ident, iota, rank, y_dram):
    E, HW = N_EXP, 512
    NS = D_FF // HW
    KF = HW // P
    SB = 2 * NS
    wg, wu, wd = a["w_gate_2"][0], a["w_up_2"][0], a["w_down_2"][0]
    lo, hi = slice(0, CAP), slice(CAP, P)
    with stage(nc, "ec") as st:
        w = [[st.sb(f"w{n}{r}", [P, KD * HW]) for r in range(2)] for n in range(3)]
        w_ready = [[st.sem(f"w_ready{n}{r}") for r in range(2)] for n in range(3)]
        sel = st.sb("sel", [P, NT, P])
        pr = st.sb("pr", [P, NT, 2])
        xg = st.sb("xg", [P, KD, P])
        sig = [st.sb(f"sig{r}", [CAP, HW]) for r in range(2)]
        up = [st.sb(f"up{r}", [CAP, HW]) for r in range(2)]
        hid = [st.sb(f"hid{r}", [CAP, HW]) for r in range(2)]
        hT = [st.sb(f"hT{r}", [P, KF * CAP]) for r in range(2)]
        yb = [st.sb(f"y{r}", [P, 512]) for r in range(2)]
        gu_ps = [st.ps(f"gu{r}") for r in range(2)]
        h_ps = [st.ps(f"h{r}") for r in range(2)]
        y_ps = [st.ps(f"yp{r}") for r in range(2)]
        x_ps = st.ps("x")
        sel_ready, gath_ready = st.sem("sel_ready"), st.sem("gath_ready")
        xg_copied = st.sem("xg_copied")
        gu_ready, act_ready = st.sem("gu_ready"), st.sem("act_ready")
        hid_ready = st.sem("hid_ready")
        hTp_ready = st.sem("hTp_ready")
        hT_ready = st.sem("hT_ready")
        down_ready = st.sem("down_ready")
        y_copied = st.sem("y_copied")
        stored, yb_free = st.sem("stored"), st.sem("yb_free")
        with nc.Block() as block:

            @block.sync
            def _(sp):
                with sp.Fori(0, E // 2) as i:
                    for s in range(SB):
                        e, j, r = 2 * i + s // NS, s % NS, s % 2
                        n = SB * i + s
                        sp.wait_ge(hid_ready, n + 1)
                        for m, src in enumerate((wg, wu)):
                            sp.dma_start(w[m][r][:], src[ds(e, 1)].rearrange("a (k p) n -> p (a k) n", p=P)
                                         [:, :, j * HW:(j + 1) * HW]).then_inc(w_ready[m][r], 16)
                        sp.wait_ge(down_ready, n + 1)
                        sp.dma_start(w[2][r][:], wd[ds(e, 1)].rearrange("a (k p) n -> p (a k) n", p=P)
                                     [:, j * KF:(j + 1) * KF, :]).then_inc(w_ready[2][r], 16)

            @block.tensor
            def _(pe):
                with pe.Fori(0, E // 2) as i:
                    pe.wait_ge(sel_ready, i + 1)
                    for hh in range(2):
                        pe.wait_ge(xg_copied, 2 * i + hh + 1)
                        for c in range(4):
                            for t in range(NT):
                                cc = hh * 4 + c
                                mm = nc.tensor.matmul(x_ps[:, c * P:(c + 1) * P], h[:, t, cc * P:(cc + 1) * P],
                                                      sel[:, t, :], start=(t == 0), stop=(t == NT - 1))
                        mm.then_inc(gath_ready, 1)
                    pe.wait_ge(xg_copied, 2 * i + 3)

                    def gate_up(s):
                        n, c0, r = SB * i + s, (s // NS) * CAP, s % 2
                        for m in range(2):
                            pe.wait_ge(w_ready[m][r], 16 * (NS * i + s // 2 + 1))
                        pe.wait_ge(hid_ready, n + 1)
                        for k in range(KD):
                            for m, part in enumerate((lo, hi)):
                                mm = nc.tensor.matmul(gu_ps[r][part, :], xg[:, k, c0:c0 + CAP],
                                                      w[m][r][:, k * HW:(k + 1) * HW],
                                                      start=(k == 0), stop=(k == KD - 1))
                        mm.then_inc(gu_ready, 1)

                    def turn(s):
                        n, r = SB * i + s, s % 2
                        pe.wait_ge(hid_ready, n + 3)
                        pe.wait_ge(hT_ready, n + 1)
                        for f in range(KF):
                            mm = nc.tensor.matmul(h_ps[r][:, f * CAP:(f + 1) * CAP], hid[r][:, f * P:(f + 1) * P],
                                                  ident[0:CAP, 0:CAP], start=True, stop=True)
                        mm.then_inc(hTp_ready, 1)

                    def down(s):
                        n, j, r, ex = SB * i + s, s % NS, s % 2, s // NS
                        pe.wait_ge(w_ready[2][r], 16 * (NS * i + s // 2 + 1))
                        pe.wait_ge(hT_ready, n + 3)
                        if j == 0:
                            pe.wait_ge(y_copied, 2 * i + ex + 1)
                        for f in range(KF):
                            for hh, part in enumerate((lo, hi)):
                                mm = nc.tensor.matmul(y_ps[ex][part, :], hT[r][:, f * CAP:(f + 1) * CAP],
                                                      w[2][r][:, f * D + hh * 512:f * D + (hh + 1) * 512],
                                                      start=(j == 0 and f == 0), stop=(j == NS - 1 and f == KF - 1))
                        mm.then_inc(down_ready, 1)

                    gate_up(0)
                    for s in range(1, SB):
                        gate_up(s)
                        turn(s - 1)
                        down(s - 1)
                    turn(SB - 1)
                    down(SB - 1)

            @block.vector
            def _(dve):
                V = nc.vector
                dve.sem_inc(hid_ready, 2)

                def select(v):
                    for t in range(NT):
                        for r in range(2):
                            V.tensor_scalar(sel[:, t, r * CAP:(r + 1) * CAP], iota[:, 0:CAP], pr[:, t, r:r + 1], None,
                                            ALU.is_equal)
                with dve.Fori(0, E // 2) as i:
                    V.tensor_copy(pr[:], rank[:, :, ds(2 * i, 2)])
                    V.drain()
                    select(i)
                    V.drain().then_inc(sel_ready, 1)
                    for s in range(SB):
                        n, r = SB * i + s, s % 2
                        dve.wait_ge(act_ready, n + 1)
                        V.tensor_mul(sig[r][:], sig[r][:], gu_ps[r][lo, :])
                        V.drain()
                        V.tensor_mul(hid[r][:], sig[r][:], up[r][:]).then_inc(hid_ready, 1)
                        if s >= 1:
                            dve.wait_ge(hTp_ready, n)
                            V.tensor_copy(hT[(s - 1) % 2][:], h_ps[(s - 1) % 2][:, 0:KF * CAP]).then_inc(hT_ready, 1)
                    dve.wait_ge(hTp_ready, SB * i + SB)
                    V.tensor_copy(hT[(SB - 1) % 2][:], h_ps[(SB - 1) % 2][:, 0:KF * CAP]).then_inc(hT_ready, 1)

            @block.scalar
            def _(act):
                act.sem_inc(xg_copied, 1)
                act.sem_inc(hT_ready, 2)
                act.sem_inc(down_ready, 2)
                act.sem_inc(y_copied, 2)
                act.sem_inc(yb_free, 2)
                with act.Fori(0, E // 2) as i:
                    for hh in range(2):
                        act.wait_ge(gath_ready, 2 * i + hh + 1)
                        nc.scalar.activation(xg[:, hh * 4:hh * 4 + 4, :].rearrange("p c s -> p (c s)"), x_ps[:],
                                             ACT.Copy).then_inc(xg_copied, 1)

                    def y_out(r):
                        act.wait_ge(yb_free, 2 * i + r + 1)
                        act.wait_ge(down_ready, SB * i + (r + 1) * NS + 2)
                        nc.scalar.activation(yb[r][:], y_ps[r][:], ACT.Copy).then_inc(y_copied, 1)

                    for s in range(SB):
                        n, r = SB * i + s, s % 2
                        act.wait_ge(gu_ready, n + 1)
                        act.wait_ge(hid_ready, n + 1)
                        nc.scalar.activation(sig[r][:], gu_ps[r][lo, :], ACT.Sigmoid)
                        nc.scalar.activation(up[r][:], gu_ps[r][hi, :], ACT.Copy).then_inc(act_ready, 1)
                        if s == NS + 1:
                            y_out(0)
                    y_out(1)

            @block.gpsimd
            def _(pool):
                with pool.Fori(0, E // 2) as i:
                    for r in range(2):
                        e = 2 * i + r
                        pool.wait_ge(y_copied, e + 3)
                        pool.dma_start(y_dram[ds(e * CAP, CAP), 0:512], yb[r][lo, :]).then_inc(stored, 16)
                        pool.dma_start(y_dram[ds(e * CAP, CAP), 512:D], yb[r][hi, :]).then_inc(stored, 16)
                        pool.wait_ge(stored, 32 * e + 32)
                        pool.sem_inc(yb_free, 1)


def ec_combine(nc, comb, y_dram, out_dram):
    NP_ = N_EXP // 2
    with stage(nc, "ecc") as st:
        y = st.sb("y", [P, NP_, D])
        ob = [st.sb(f"o{r}", [P, 512]) for r in range(2)]
        ld, ready, copied, stored = st.sem("ld"), st.sem("ready"), st.sem("copied"), st.sem("stored")
        ps = [st.ps(f"ps{r}") for r in range(2)]
        units = [(t, hh) for t in range(NT) for hh in range(2)]
        with nc.Block() as block:

            @block.sync
            def _(sp):
                sp.dma_start(y[:], y_dram.rearrange("(n p) d -> p n d", p=P)).then_inc(ld, 16)
                for n, (t, hh) in enumerate(units):
                    sp.wait_ge(copied, n + 1)
                    sp.dma_start(out_dram[t * P:(t + 1) * P, hh * 512:(hh + 1) * 512], ob[n % 2][:]).then_inc(stored, 16)
                    sp.wait_ge(stored, 16 * (n + 1))

            @block.tensor
            def _(pe):
                pe.wait_ge(ld, 16)
                for n, (t, hh) in enumerate(units):
                    if n >= 2:
                        pe.wait_ge(copied, n - 1)
                    for c in range(NP_):
                        mm = nc.tensor.matmul(ps[n % 2][:], comb[:, c, t * P:(t + 1) * P],
                                              y[:, c, hh * 512:(hh + 1) * 512], start=(c == 0), stop=(c == NP_ - 1))
                    mm.then_inc(ready, 1)

            @block.scalar
            def _(act):
                for n, (t, hh) in enumerate(units):
                    if n >= 2:
                        act.wait_ge(stored, 16 * (n - 1))
                    act.wait_ge(ready, n + 1)
                    nc.scalar.activation(ob[n % 2][:], ps[n % 2][:], ACT.Copy).then_inc(copied, 1)


def second_block(nc, a, x, xT, cst, mod, biases, out, dram):
    ident, strict, ones, iota, pidx = cst
    sh1, sc1, gt1, sh2, sc2, gt2 = (mod[n * D:(n + 1) * D] for n in range(6))
    win = a["w_in_2"][0]
    with nc.sbuf_tensor("h", [P, NT, D], F32) as h:
        norm(nc, "rms1", x, h, xT, ident, EPS2, True, a["g_norm_mix_2"][0], sh1, one_plus=sc1)
        n_lat = Q_RANK + KV_RANK + ROPE
        lat, gates = dram("lat", [S, n_lat]), dram("gates", [S, 2 * D])
        qks = [dram(f"dqk{g}", [2 * D, S]) for g in range(3)]
        vs = [dram(f"dv{g}", [S, D]) for g in range(3)]
        at = [n_lat + g * 3 * D for g in range(3)]
        gemms(nc, "proj2", [job(win, 0, 2, n_lat // 2, xT, P, S, lat, "N"),
                            job(win, n_lat + 9 * D, 4, 512, xT, P, S, gates, "N")]
              + [job(win, at[g], 4, 512, xT, P, S, qks[g], "T", tok=dilated_views(g)[0]) for g in range(3)]
              + [job(win, at[g] + 2 * D, 2, 512, xT, P, S, vs[g], "N") for g in range(3)],
              side=lambda st: RelativeBias(nc, a, biases, (0, 1), st))
        ogs = [dram(f"og{g}", [S, D]) for g in range(3)]
        sts = [dram(f"stat{g}", [S, 2 * DIL_H]) for g in range(3)]
        for g in range(3):
            dilated(nc, ident, g, qks[g], vs[g], biases[g], ogs[g], sts[g])
        q_all, k_all, v_all = dram("mla_q", [MLA_H * (NOPE + ROPE), S]), dram("mla_k", [D, S]), dram("mla_v", [S, D])
        qpe, kpe, oa = dram("mla_qpe", [MLA_H * ROPE, S]), dram("mla_kpe", [ROPE, S]), dram("oa", [S, D])
        with ExitStack() as c2:
            sb = lambda n, s: c2.enter_context(nc.sbuf_tensor("mla_" + n, s, F32))
            cqT, ckvT = sb("cqT", [P, Q_RANK // P, S]), sb("ckvT", [P, KV_RANK // P, S])
            kp = [sb(f"kp{n}", [ROPE // 2, S]) for n in range(2)]
            latents(nc, a, ident, lat, cqT, ckvT, kp)
            gemms(nc, "ups", [job(a["w_uq_L"], 0, 3, 512, cqT, P, S, q_all, "T"),
                              job(a["w_ukv_L"], 0, 2, 512, ckvT, P, S, k_all, "T"),
                              job(a["w_ukv_L"], D, 2, 512, ckvT, P, S, v_all, "N")])
            rotary(nc, a, q_all, kp, qpe, kpe)
        attention(nc, "mla", ident, MLA_H, NOPE, P, S,
                  lambda hd: [q_all[ds(hd * NOPE, NOPE), :], qpe[ds(hd * ROPE, ROPE), :]],
                  lambda hd: [k_all[ds(hd * NOPE, NOPE), :], kpe],
                  lambda hd: [((slice(None), slice(0, NT), slice(None)),
                               v_all.rearrange("(c p) f -> p c f", p=P)[:, :, ds(hd * P, P)])],
                  lambda q, u: q[:, u * P:(u + 1) * P], lambda k, u: k[:, :], lambda u: range(NT),
                  lambda hd, u: oa[u * P:(u + 1) * P, ds(hd * P, P)],
                  (NOPE + ROPE) ** -0.5, pe_dims=ROPE, v_chunks=NT)
        merge(nc, oa, ogs, sts, gates, xT, ident)
        proj = dram("proj_2", [S, D])
        gemm(nc, "out2", a["w_out_2"][0], 0, 2, 512, xT, P, S, proj, "N")
        norm(nc, "rms2", x, h, xT, ident, EPS2, True, a["g_norm_ffn_2"][0], sh2, resid=proj, gate=gt1, one_plus=sc2)
        affT_d, y_d = dram("affT", [N_EXP * S]), dram("ec_y", [N_EXP * CAP, D])
        with nc.sbuf_tensor("ec_comb", [P, N_EXP // 2, S], F32) as comb:
            with nc.sbuf_tensor("ec_aff", [P, NT, N_EXP], F32) as aff, \
                    nc.sbuf_tensor("ec_rank", [P, NT, N_EXP], F32) as rank:
                ec_route(nc, a, xT, ident, ones, pidx, affT_d, aff, rank, comb)
                ec_experts(nc, a, h, ident, iota, rank, y_d)
            ec_combine(nc, comb, y_d, proj)
        norm(nc, "rms3", x, h, None, ident, EPS2, True, a["g_final_2"], resid=proj, gate=gt2, out_dram=out[0])


def na_bias_layout(rpb):
    q_cols = np.arange(GRID_W).reshape(N_CB, WIN_W)
    starts = np.clip(np.arange(N_CB) * WIN_W - WIN_W // 2, 0, GRID_W - SPAN)
    key_cols = starts[:, None] + np.arange(SPAN)
    lo = np.clip(q_cols - WIN_W // 2, 0, GRID_W - WIN_W)[:, :, None]
    kc = key_cols[:, None, :]
    inside = (kc >= lo) & (kc < lo + WIN_W)
    dc = np.where(inside, kc - q_cols[:, :, None] + WIN_W - 1, 2 * WIN_W - 1)
    dr = np.arange(ROWS)[None, :] - np.arange(ROWS)[:, None] + 7
    padded = np.pad(rpb, ((0, 0), (0, 0), (0, 1)), constant_values=NEG)
    got = padded[:, dr[:, None, None, :, None], dc.transpose(1, 0, 2)[None, :, :, None, :]]
    return np.ascontiguousarray(got.reshape(rpb.shape[0], P, N_CB * ROWS * SPAN))


ROPE_THETA = 10000.0


def unit_tokens():
    p, u = np.arange(P)[:, None], np.arange(4)[None, :]
    return np.concatenate([u * P + p, 4 * p + u, 16 * (p % 32) + 4 * u + p // 32], axis=1)


def band_tokens():
    p = np.arange(P)[:, None, None]
    u, j = np.arange(4)[None, :, None], lambda n: np.arange(n)[None, None, :]
    parts = (u * P + p - 64 + j(BAND), 4 * j(P) + u + 0 * p, 16 * j(32) + 4 * u + p // 32)
    return [x.reshape(P, -1) for x in parts]


def band_mask():
    k0, k1, k2 = band_tokens()
    i = np.arange(P)
    near = np.abs(np.tile(i, 4)[None, :] - i[:, None]) <= 64
    ok = np.concatenate([(k0 >= 0) & (k0 < S), near, np.ones(k2.shape, bool)], axis=1)
    return np.where(ok, 0.0, NEG).astype(np.float32)


def kernel(**inputs):
    import concourse.bacc as _bacc
    from concourse.bass_utils import run_bass_kernel_spmd as _run

    nc = _bacc.Bacc("TRN2", target_bir_lowering=False, num_devices=1)
    host = {k: np.ascontiguousarray(v) for k, v in inputs.items() if k != "na_rpb"}
    host["na_bias"] = na_bias_layout(np.asarray(inputs["na_rpb"])[0])
    host["ml_conv_wT"] = np.ascontiguousarray(np.asarray(inputs["ml_conv_w"])[0].T)
    host["ml_gate_bT"] = np.ascontiguousarray(np.asarray(inputs["ml_gate_b"])[0].T)
    for n in ("ml_conv_b", "ml_norm_g", "ml_skip"):
        host[n + "P"] = np.ascontiguousarray(np.asarray(inputs[n])[0].reshape(-1, 96).T)
    cols = lambda v: np.ascontiguousarray(np.asarray(v).reshape(-1, P).T)
    host["c_P"] = cols(inputs["c_2"])
    host["g_q_lat_P"], host["g_kv_lat_P"] = cols(inputs["g_q_lat_2"]), cols(inputs["g_kv_lat_2"])
    uq = np.asarray(inputs["w_uq_2"])[0].reshape(Q_RANK, MLA_H, NOPE + ROPE)
    cuts = (uq[:, :, :NOPE], uq[:, :, NOPE:NOPE + 32], uq[:, :, NOPE + 32:])
    host["w_uq_L"] = np.ascontiguousarray(np.concatenate([c.reshape(Q_RANK, -1) for c in cuts], axis=1))
    ukv = np.asarray(inputs["w_ukv_2"])[0].reshape(KV_RANK, MLA_H, 2 * P)
    host["w_ukv_L"] = np.ascontiguousarray(
        np.concatenate([ukv[:, :, :P].reshape(KV_RANK, -1), ukv[:, :, P:].reshape(KV_RANK, -1)], axis=1))
    host["rel_tab"] = np.ascontiguousarray(
        np.asarray(inputs["rel_bias_2"]).reshape(N_REL, 3, DIL_H).transpose(1, 0, 2).reshape(-1))
    host["pos_q"] = np.ascontiguousarray(np.asarray(inputs["positions_2"])[0][unit_tokens()])
    keys = np.clip(np.concatenate(band_tokens(), axis=1), 0, S - 1)
    host["pos_k"] = np.ascontiguousarray(np.asarray(inputs["positions_2"])[0][keys])
    host["band_mask"] = band_mask()
    host["inv_freq"] = np.tile(ROPE_THETA ** (-np.arange(0, ROPE, 2) / ROPE), 4)[:, None].astype(np.float32)
    arrays, aps = {}, {}
    for k, v in host.items():
        if k not in USED:
            continue
        arrays[f"in_{k}"] = v
        aps[k] = nc.dram_tensor(f"in_{k}", v.shape, mybir.dt.from_np(v.dtype), kind="ExternalInput").ap()
    out = nc.dram_tensor("out_0", (1, S, D), F32, kind="ExternalOutput").ap()
    build(nc, aps, out)
    r = _run(nc, [arrays], core_ids=[0])
    return r.results[0]["out_0"]
```
